# Optimizing a Trainium2 kernel written in Bass

```python
import math
import jax
import jax.numpy as jnp
from jax import lax
import numpy as np

D_MODEL = 1024
BATCH = 1
SEQ = 4096
DEPTH = 1
DEC_BATCH = 8
DEC_SEQ = 8
PAST_LEN = 4096
PAGE_SIZE = 128

A_HEADS = 8
A_HEAD_DIM = 64
A_WIDTH = A_HEADS * A_HEAD_DIM
A_SCALE = A_HEAD_DIM ** -0.5
DILATED_GROUPS = ((128, 1), (512, 4), (2048, 16))
WINDOW_MAX = 2048
SWA_BLOCK = 128
B_HEADS = 4
B_KEY_DIM = 64
B_VAL_DIM = 128
B_QK_WIDTH = B_HEADS * B_KEY_DIM
B_V_WIDTH = B_HEADS * B_VAL_DIM
GATE_RANK = 16
GATE_TEMP = 16.0
GLA_CHUNK = 64
MIX_WIDTH = A_WIDTH + B_V_WIDTH
IN_SIZES = (A_WIDTH, A_WIDTH, A_WIDTH, B_QK_WIDTH, B_QK_WIDTH, B_V_WIDTH, B_V_WIDTH, GATE_RANK)
IN_WIDTH = 3 * A_WIDTH + 2 * B_QK_WIDTH + 2 * B_V_WIDTH + GATE_RANK
N_MEM = 256
MEM_HEADS = 4
MEM_HEAD_DIM = 128
MEM_WIDTH = MEM_HEADS * MEM_HEAD_DIM
N_EXPERTS = 32
TOP_K = 4
D_FF = 1024
SWIGLU_ALPHA = 1.702
SWIGLU_LIMIT = 7.0
MOE_TOKEN_BLOCK = 8192
EPS = 1e-6

kernel_name = 'hybrid_dilated_swa_gla_mem_moe_step'

def rmsnorm(x, g):
    xf = x.astype(jnp.float32)
    y = xf * lax.rsqrt(jnp.mean(xf * xf, axis=-1, keepdims=True) + EPS)
    return (y * g.astype(jnp.float32)).astype(x.dtype)

def masked_softmax(s, valid):
    s = jnp.where(valid, s, -jnp.inf)
    m = jnp.max(s, axis=-1, keepdims=True)
    p = jnp.exp(s - m)
    l = jnp.sum(p, axis=-1, keepdims=True)
    return p / l, (m + jnp.log(l))[..., 0]

def combine_groups(outs, lses):
    w = jax.nn.softmax(jnp.stack(lses), axis=0)
    return jnp.sum(w[..., None] * jnp.stack(outs), axis=0)

def to_strided(t, dil, padded):
    bsz, seq, heads, hd = t.shape
    t = jnp.pad(t, ((0, 0), (0, padded - seq), (0, 0), (0, 0)))
    t = t.reshape(bsz, padded // dil, dil, heads, hd).transpose(0, 2, 1, 3, 4)
    return t.reshape(bsz, dil, padded // (dil * SWA_BLOCK), SWA_BLOCK, heads, hd)

def with_prev_block(t):
    prev = jnp.pad(t, ((0, 0), (0, 0), (1, 0), (0, 0), (0, 0), (0, 0)))[:, :, :-1]
    return jnp.concatenate([prev, t], axis=3)

def dilated_prompt(q, k, v):
    bsz, seq, heads, hd = q.shape
    outs, lses = [], []
    for window, dil in DILATED_GROUPS:
        span = window // dil
        unit = dil * SWA_BLOCK
        padded = -(-seq // unit) * unit
        nb = padded // unit
        qs = to_strided(q, dil, padded)
        ks = with_prev_block(to_strided(k, dil, padded))
        vs = with_prev_block(to_strided(v, dil, padded))
        s = jnp.einsum('brnqhd,brnkhd->brnhqk', qs, ks, preferred_element_type=jnp.float32) * A_SCALE
        qi = jnp.arange(SWA_BLOCK)[:, None]
        ki = jnp.arange(2 * SWA_BLOCK)[None, :]
        dist = qi + SWA_BLOCK - ki
        band = (dist >= 0) & (dist <= span)
        has_key = (jnp.arange(nb) > 0)[:, None, None] | (ki >= SWA_BLOCK)[None]
        valid = (band[None] & has_key)[None, None, :, None]
        pr, lse = masked_softmax(s, valid)
        o = jnp.einsum('brnhqk,brnkhd->brnqhd', pr, vs.astype(jnp.float32))
        o = o.reshape(bsz, dil, padded // dil, heads, hd).transpose(0, 2, 1, 3, 4)
        o = o.reshape(bsz, padded, heads, hd)[:, :seq]
        lse = lse.transpose(0, 1, 2, 4, 3).reshape(bsz, dil, padded // dil, heads).transpose(0, 2, 1, 3)
        lse = lse.reshape(bsz, padded, heads)[:, :seq]
        outs.append(o)
        lses.append(lse)
    return combine_groups(outs, lses).astype(q.dtype)

def dilated_sample(q, k_ext, v_ext, w_buf):
    n_new = q.shape[1]
    outs, lses = [], []
    for window, dil in DILATED_GROUPS:
        j = jnp.arange(window // dil + 1)
        idx = w_buf + jnp.arange(n_new)[:, None] - dil * j[None, :]
        valid = idx >= 0
        idx = jnp.maximum(idx, 0)
        kg = k_ext[:, idx]
        vg = v_ext[:, idx]
        s = jnp.einsum('bthd,btjhd->bthj', q, kg, preferred_element_type=jnp.float32) * A_SCALE
        pr, lse = masked_softmax(s, valid[None, :, None, :])
        outs.append(jnp.einsum('bthj,btjhd->bthd', pr, vg.astype(jnp.float32)))
        lses.append(lse)
    return combine_groups(outs, lses).astype(q.dtype)

def gla(q, k, v, log_a, s0):
    bsz, length, heads, dk = q.shape
    chunk = math.gcd(length, GLA_CHUNK)
    nc = length // chunk

    def chunks(t):
        t = t.astype(jnp.float32)
        return t.reshape(bsz, nc, chunk, heads, t.shape[-1]).transpose(1, 0, 3, 2, 4)

    causal = jnp.tril(jnp.ones((chunk, chunk), dtype=bool))

    def step(state, inp):
        qc, kc, vc, gc = inp
        b = jnp.cumsum(gc, axis=2)
        o_inter = jnp.einsum('bhck,bhkv->bhcv', qc * jnp.exp(b), state)
        rel = jnp.where(causal[:, :, None], b[:, :, :, None, :] - b[:, :, None, :, :], -jnp.inf)
        att = jnp.einsum('bhtk,bhsk,bhtsk->bhts', qc, kc, jnp.exp(rel))
        o = o_inter + jnp.einsum('bhts,bhsv->bhtv', att, vc)
        b_last = b[:, :, -1:, :]
        new_state = jnp.exp(b_last[:, :, 0, :])[..., None] * state + jnp.einsum(
            'bhsk,bhsv->bhkv', kc * jnp.exp(b_last - b), vc)
        return new_state, o

    s_fin, o = lax.scan(step, s0.astype(jnp.float32), (chunks(q), chunks(k), chunks(v), chunks(log_a)))
    o = o.transpose(1, 0, 3, 2, 4).reshape(bsz, length, heads, v.shape[-1])
    return o.astype(v.dtype), s_fin.astype(s0.dtype)

def project_in(x, p):
    lead = x.shape[:-1]
    z = rmsnorm(x, p['norm1']) @ p['w_in']
    offs = np.cumsum(IN_SIZES)[:-1].tolist()
    aq, ak, av, bq, bk, bv, br, blr = jnp.split(z, offs, axis=-1)
    aq = rmsnorm(aq.reshape(*lead, A_HEADS, A_HEAD_DIM), p['a_q_g'])
    ak = rmsnorm(ak.reshape(*lead, A_HEADS, A_HEAD_DIM), p['a_k_g'])
    av = av.reshape(*lead, A_HEADS, A_HEAD_DIM)
    bq = bq.reshape(*lead, B_HEADS, B_KEY_DIM) * (B_KEY_DIM ** -0.5)
    bk = bk.reshape(*lead, B_HEADS, B_KEY_DIM)
    bv = bv.reshape(*lead, B_HEADS, B_VAL_DIM)
    log_a = jax.nn.log_sigmoid((blr @ p['gla_w_a'] + p['gla_b_a']).astype(jnp.float32)) / GATE_TEMP
    log_a = log_a.reshape(*lead, B_HEADS, B_KEY_DIM)
    return aq, ak, av, bq, bk, bv, br, log_a

def mix_out(x, o_a, o_b, br, p):
    lead = x.shape[:-1]
    o_b = rmsnorm(o_b, p['gla_out_g']).reshape(*lead, B_V_WIDTH) * jax.nn.silu(br)
    o = jnp.concatenate([o_a.reshape(*lead, A_WIDTH), o_b], axis=-1)
    return x + o @ p['w_out']

def memory_kv(mem, p):
    bsz = mem.shape[0]
    mn = rmsnorm(mem, p['mem_norm'])
    mk = rmsnorm((mn @ p['mem_w_k']).reshape(bsz, N_MEM, MEM_HEADS, MEM_HEAD_DIM), p['mem_k_g'])
    mv = (mn @ p['mem_w_v']).reshape(bsz, N_MEM, MEM_HEADS, MEM_HEAD_DIM)
    return mk, mv

def moe_block(xb, p):
    logits = (xb @ p['router_w'] + p['router_b']).astype(jnp.float32)
    top_v, top_i = lax.top_k(logits, TOP_K)
    gates = jax.nn.softmax(top_v, axis=-1)
    eid = top_i.reshape(-1)
    order = jnp.argsort(eid)
    eid_s = eid[order]
    tok = order // TOP_K
    sizes = jnp.bincount(eid, length=N_EXPERTS).astype(jnp.int32)
    h = lax.ragged_dot(xb[tok], p['w1'], sizes) + p['b1'][eid_s]
    glu = jnp.minimum(h[:, 0::2], SWIGLU_LIMIT)
    lin = jnp.clip(h[:, 1::2], -SWIGLU_LIMIT, SWIGLU_LIMIT)
    act = glu * jax.nn.sigmoid(SWIGLU_ALPHA * glu) * (lin + 1.0)
    out = lax.ragged_dot(act, p['w2'], sizes) + p['b2'][eid_s]
    out = out * gates.reshape(-1)[order][:, None].astype(out.dtype)
    return jax.ops.segment_sum(out, tok, num_segments=xb.shape[0])

def moe(xn, p):
    lead = xn.shape[:-1]
    xf = xn.reshape(-1, D_MODEL)
    n_tok = xf.shape[0]
    blk = math.gcd(n_tok, MOE_TOKEN_BLOCK)
    y = lax.map(lambda xb: moe_block(xb, p), xf.reshape(n_tok // blk, blk, D_MODEL))
    return y.reshape(*lead, D_MODEL)

def memory_and_moe(h, mk, mv, p):
    lead = h.shape[:-1]
    hn = rmsnorm(h, p['norm2'])
    q = rmsnorm((hn @ p['mem_w_q']).reshape(*lead, MEM_HEADS, MEM_HEAD_DIM), p['mem_q_g'])
    s = jnp.einsum('blhd,bmhd->bhlm', q, mk, preferred_element_type=jnp.float32) * (MEM_HEAD_DIM ** -0.5)
    pr = jax.nn.softmax(s, axis=-1)
    o = jnp.einsum('bhlm,bmhd->blhd', pr, mv.astype(jnp.float32)).astype(h.dtype)
    h = h + o.reshape(*lead, MEM_WIDTH) @ p['mem_w_o']
    return h + moe(rmsnorm(h, p['norm3']), p)

def setup_inputs(seed: int = 0) -> dict:
    key = jax.random.key(seed)
    ks = iter(jax.random.split(key, 64))

    def nrm(shape, scale):
        return jax.random.normal(next(ks), shape, jnp.float32) * scale

    def gain(shape):
        return 1.0 + nrm(shape, 0.02)

    w_buf = min(WINDOW_MAX, PAST_LEN)
    return {
        'x_prompt': nrm((BATCH, SEQ, D_MODEL), 1.0),
        'x_sample': nrm((DEC_BATCH, DEC_SEQ, D_MODEL), 1.0),
        'mem_prompt': nrm((BATCH, N_MEM, D_MODEL), 1.0),
        'cache_swa_k': nrm((DEPTH, DEC_BATCH, w_buf, A_HEADS, A_HEAD_DIM), 1.0),
        'cache_swa_v': nrm((DEPTH, DEC_BATCH, w_buf, A_HEADS, A_HEAD_DIM), 1.0),
        'state_gla': nrm((DEPTH, DEC_BATCH, B_HEADS, B_KEY_DIM, B_VAL_DIM), 0.5),
        'cache_mem_k': nrm((DEPTH, DEC_BATCH, N_MEM, MEM_HEADS, MEM_HEAD_DIM), 1.0),
        'cache_mem_v': nrm((DEPTH, DEC_BATCH, N_MEM, MEM_HEADS, MEM_HEAD_DIM), 1.0),
        'norm1_g': gain((DEPTH, D_MODEL)),
        'w_in': nrm((DEPTH, D_MODEL, IN_WIDTH), D_MODEL ** -0.5),
        'a_q_norm_g': gain((DEPTH, A_HEAD_DIM)),
        'a_k_norm_g': gain((DEPTH, A_HEAD_DIM)),
        'gla_w_alpha': nrm((DEPTH, GATE_RANK, B_QK_WIDTH), GATE_RANK ** -0.5),
        'gla_b_alpha': nrm((DEPTH, B_QK_WIDTH), 0.1),
        'gla_out_norm_g': gain((DEPTH, B_VAL_DIM)),
        'w_out': nrm((DEPTH, MIX_WIDTH, D_MODEL), MIX_WIDTH ** -0.5),
        'norm2_g': gain((DEPTH, D_MODEL)),
        'mem_norm_g': gain((DEPTH, D_MODEL)),
        'mem_w_q': nrm((DEPTH, D_MODEL, MEM_WIDTH), D_MODEL ** -0.5),
        'mem_w_k': nrm((DEPTH, D_MODEL, MEM_WIDTH), D_MODEL ** -0.5),
        'mem_w_v': nrm((DEPTH, D_MODEL, MEM_WIDTH), D_MODEL ** -0.5),
        'mem_q_norm_g': gain((DEPTH, MEM_HEAD_DIM)),
        'mem_k_norm_g': gain((DEPTH, MEM_HEAD_DIM)),
        'mem_w_o': nrm((DEPTH, MEM_WIDTH, D_MODEL), MEM_WIDTH ** -0.5),
        'norm3_g': gain((DEPTH, D_MODEL)),
        'router_w': nrm((DEPTH, D_MODEL, N_EXPERTS), D_MODEL ** -0.5),
        'router_b': nrm((DEPTH, N_EXPERTS), 0.01),
        'exp_w1': nrm((DEPTH, N_EXPERTS, D_MODEL, 2 * D_FF), D_MODEL ** -0.5),
        'exp_b1': nrm((DEPTH, N_EXPERTS, 2 * D_FF), 0.01),
        'exp_w2': nrm((DEPTH, N_EXPERTS, D_FF, D_MODEL), D_FF ** -0.5),
        'exp_b2': nrm((DEPTH, N_EXPERTS, D_MODEL), 0.01),
    }

def reference(x_prompt, x_sample, mem_prompt, cache_swa_k, cache_swa_v, state_gla, cache_mem_k, cache_mem_v,
              norm1_g, w_in, a_q_norm_g, a_k_norm_g, gla_w_alpha, gla_b_alpha, gla_out_norm_g, w_out,
              norm2_g, mem_norm_g, mem_w_q, mem_w_k, mem_w_v, mem_q_norm_g, mem_k_norm_g, mem_w_o,
              norm3_g, router_w, router_b, exp_w1, exp_b1, exp_w2, exp_b2):
    xp, xs = x_prompt, x_sample
    w_buf = cache_swa_k.shape[2]
    swa_k_p, swa_v_p, gla_p, mem_k_p, mem_v_p = [], [], [], [], []
    swa_k_s, swa_v_s, gla_s = [], [], []
    for l in range(DEPTH):
        p = {'norm1': norm1_g[l], 'w_in': w_in[l], 'a_q_g': a_q_norm_g[l], 'a_k_g': a_k_norm_g[l],
             'gla_w_a': gla_w_alpha[l], 'gla_b_a': gla_b_alpha[l], 'gla_out_g': gla_out_norm_g[l],
             'w_out': w_out[l], 'norm2': norm2_g[l], 'mem_norm': mem_norm_g[l], 'mem_w_q': mem_w_q[l],
             'mem_w_k': mem_w_k[l], 'mem_w_v': mem_w_v[l], 'mem_q_g': mem_q_norm_g[l],
             'mem_k_g': mem_k_norm_g[l], 'mem_w_o': mem_w_o[l], 'norm3': norm3_g[l],
             'router_w': router_w[l], 'router_b': router_b[l], 'w1': exp_w1[l], 'b1': exp_b1[l],
             'w2': exp_w2[l], 'b2': exp_b2[l]}

        aq, ak, av, bq, bk, bv, br, la = project_in(xp, p)
        o_a = dilated_prompt(aq, ak, av)
        w_p = min(WINDOW_MAX, xp.shape[1])
        s0 = jnp.zeros((xp.shape[0], B_HEADS, B_KEY_DIM, B_VAL_DIM), xp.dtype)
        o_b, s_p = gla(bq, bk, bv, la, s0)
        h = mix_out(xp, o_a, o_b, br, p)
        mk, mv = memory_kv(mem_prompt, p)
        xp = memory_and_moe(h, mk, mv, p)
        swa_k_p.append(ak[:, -w_p:])
        swa_v_p.append(av[:, -w_p:])
        gla_p.append(s_p)
        mem_k_p.append(mk)
        mem_v_p.append(mv)

        aq, ak, av, bq, bk, bv, br, la = project_in(xs, p)
        k_ext = jnp.concatenate([cache_swa_k[l].astype(ak.dtype), ak], axis=1)
        v_ext = jnp.concatenate([cache_swa_v[l].astype(av.dtype), av], axis=1)
        o_a = dilated_sample(aq, k_ext, v_ext, w_buf)
        o_b, s_s = gla(bq, bk, bv, la, state_gla[l])
        h = mix_out(xs, o_a, o_b, br, p)
        xs = memory_and_moe(h, cache_mem_k[l], cache_mem_v[l], p)
        swa_k_s.append(k_ext[:, -w_buf:])
        swa_v_s.append(v_ext[:, -w_buf:])
        gla_s.append(s_s)

    return (xp, xs, jnp.stack(swa_k_p), jnp.stack(swa_v_p), jnp.stack(gla_p), jnp.stack(mem_k_p),
            jnp.stack(mem_v_p), jnp.stack(swa_k_s), jnp.stack(swa_v_s), jnp.stack(gla_s))


_drawn_inputs = setup_inputs


def setup_inputs(seed=0):
    import zlib

    import numpy as np

    out = dict(_drawn_inputs(seed))
    spreads = {}
    factors = {'a_q_norm_g': 5.015,
     'a_k_norm_g': 2.754,
     'norm2_g': 4.698,
     'mem_norm_g': 2.878,
     'mem_q_norm_g': 4.83,
     'mem_k_norm_g': 3.303,
     'exp_b1': 8.0,
     'exp_b2': 8.0,
     'router_b': 4.917}
    for name, (base, spread) in spreads.items():
        noise = np.random.default_rng([zlib.crc32(name.encode()), seed]).standard_normal(out[name].shape)
        drawn = base * np.exp(spread * noise) if base else spread * noise
        out[name] = jnp.asarray(drawn.astype(out[name].dtype))
    for name, factor in factors.items():
        out[name] = (out[name] * factor).astype(out[name].dtype)
    return out
```

```python
import math
from contextlib import ExitStack

import concourse.bass as bass
from concourse import mybir
from concourse.alu_op_type import AluOpType as ALU

F32 = mybir.dt.float32
I32 = mybir.dt.int32
U32 = mybir.dt.uint32
ACT = mybir.ActivationFunctionType
AX = mybir.AxisListType

P = 128
D = 1024
KD = D // P
SEQ, DEC_B, DEC_T, PAST = 4096, 8, 8, 4096
SAMPLE = DEC_B * DEC_T
NT = SEQ // P + 1
ROWS = NT * P
TOKENS = SEQ + SAMPLE
AH, AD = 8, 64
AW = AH * AD
GROUPS = ((128, 1), (512, 4), (2048, 16))
WBUF = 2048
BH, BK, BV = 4, 64, 128
BQK, BVW = BH * BK, BH * BV
RANK, TEMP = 16, 16.0
NMEM, MH, MD = 256, 4, 128
MW = MH * MD
NE, TOPK, FF = 32, 4, 1024
ALPHA, LIMIT, EPS = 1.702, 7.0, 1e-6
NEG = -1.0e30
ZQ, ZK, ZV, ZBQ, ZBK, ZBV, ZBR, ZLA = 0, 512, 1024, 1536, 1792, 2048, 2560, 3072
ZW = 3328
INW = 3088
NTL = (TOKENS * TOPK + NE * (P - 1)) // P
UW = AW + 2 * AH


class Pair:

    def __init__(self, eng, it):
        self.eng, self.it, self.kept = eng, it, {}

    def value(self, by, add):
        if isinstance(self.it, int):
            return by * self.it + add
        if (by, add) not in self.kept:
            self.kept[by, add] = self.eng.snap(self.it * by + add)
        return self.kept[by, add]


class Turn:

    def __init__(self, pair, n):
        self.pair, self.n, self.p = pair, n, n % 2

    @property
    def t(self):
        return self.pair.value(2, self.n)

    @property
    def now(self):
        return self.pair.value(2, self.n + 3)

    @property
    def back1(self):
        return self.pair.value(2, self.n + 2)

    @property
    def back2(self):
        return self.pair.value(2, self.n + 1)

    @property
    def twice(self):
        return self.pair.value(4, 2 * self.n + 4)

    @property
    def dma(self):
        return self.pair.value(16, 16 + 16 * (self.n // 2))

    @property
    def dma1(self):
        return self.pair.value(32, 16 + 16 * self.n)

    @property
    def dma2(self):
        return self.pair.value(32, 32 + 32 * (self.n // 2))

    @property
    def dma4(self):
        return self.pair.value(64, 64 + 64 * (self.n // 2))

    @property
    def dma5(self):
        return self.pair.value(80, 80 + 80 * (self.n // 2))

    def of(self, per, k):
        return self.pair.value(2 * per, per * self.n + k + 3)

    @property
    def prev(self):
        return Turn(self.pair, self.n - 1)

    @property
    def next(self):
        return Turn(self.pair, self.n + 1)


def at(eng, t):
    return Turn(Pair(eng, t // 2), t % 2)


def all_steps(eng, n, step, last=None):
    with eng.Fori(0, n // 2) as it:
        pair = Pair(eng, it)
        for k in range(2):
            step(Turn(pair, k))
    if n % 2:
        (last or step)(at(eng, n - 1))


class Phase:

    def __init__(self, nc, ctx, name):
        self.nc, self.ctx, self.name = nc, ctx, name
        self.granted, self.semaphores = [], []
        ctx.callback(self.clear)

    def clear(self):
        self.nc.clear_and_free_semaphores(self.semaphores)
        self.nc.all_engine_barrier()

    def semaphore(self, name):
        s = self.nc.alloc_semaphore(name=f"{self.name}_{name}")
        self.semaphores.append(s)
        return s

    def sb(self, name, shape, dt=F32):
        return self.ctx.enter_context(self.nc.sbuf_tensor(f"{self.name}_{name}", shape, dt))

    def ps(self, name, width=512):
        return self.ctx.enter_context(self.nc.psum_tensor(f"{self.name}_{name}", [P, width], F32))

    def event(self, name):
        s = self.semaphore(name)
        self.granted.append((s, 2))
        return s

    def loads(self, name, n=2):
        return [self.semaphore(f"{name}{i}") for i in range(n)]

    def load(self, name):
        return self.loads(name, 1)[0]

    def stores(self, name, n=2):
        s = self.loads(name, n)
        self.granted += [(x, 16) for x in s]
        return s

    def grant(self, eng):
        for s, v in self.granted:
            eng.sem_inc(s, v)


def make_identity(pool, ident):
    pool.memset(ident[:, :], 0.0)
    pool.drain()
    pool.affine_select(out=ident[:, :], in_=ident[:, :], compare_op=ALU.not_equal, fill=1.0, base=0,
                       pattern=[[-1, P]], channel_multiplier=1)


def across(ap, n):
    return ap.unsqueeze(2).to_broadcast([ap.shape[0], ap.shape[1], n])


def inverse_rms(dve, out, sums, width, tmp):
    half, t = tmp
    dve.tensor_scalar(half, sums, -0.5 / width, -0.5 * EPS, ALU.mult, ALU.add)
    dve.tensor_scalar(out, sums, 1.0 / width, EPS, ALU.mult, ALU.add)
    dve.drain()
    dve.tensor_scalar(out.bitcast(I32), out.bitcast(I32), -0.5, float(0x5F3759DF), ALU.mult, ALU.add)
    for _ in range(3):
        dve.drain()
        dve.tensor_tensor(t, out, out, ALU.mult)
        dve.drain()
        dve.tensor_tensor(t, t, half, ALU.mult)
        dve.drain()
        ins = dve.scalar_tensor_tensor(out, t, 1.5, out, ALU.add, ALU.mult)
    return ins


def project(nc, x_prompt, x_sample, norm1_g, w_in, a_q_g, a_k_g, w_alpha, b_alpha, Z, shifts):
    CH = 512
    NC = 6
    BANK = (0, 1, 2, 3, 4, 2)
    with ExitStack() as ctx:
        ph = Phase(nc, ctx, "pj")
        ident = ph.sb("ident", [P, P])
        w_sb = ph.sb("w", [P, KD, INW])
        g1c = ph.sb("g1c", [P, KD])
        qkg = ph.sb("qkg", [P, 2 * AW])
        wa = ph.sb("wa", [RANK + 1, BQK])
        x_sb = ph.sb("x", [P, 2, D])
        xs = ph.sb("xs", [P, D])
        xsq = ph.sb("xsq", [P, D])
        sq = ph.sb("sq", [P, D])
        ss = ph.sb("ss", [P, 2])
        xT = ph.sb("xT", [P, 2, KD, P])
        z_sb = ph.sb("z", [P, 2, ZW])
        hss = ph.sb("hss", [P, 2 * AH])
        hr = ph.sb("hr", [P, 2 * AH])
        lrT = ph.sb("lrT", [RANK + 1, P])
        gate_t = ph.sb("gate_t", [P, 2, BVW])
        la_t = ph.sb("la_t", [P, 3, BQK])
        tmp = ph.sb("tmp", [P, 2, 2 * AH])
        z_ps = [ph.ps(f"zps{i}") for i in range(5)]
        xT_ps = [ph.ps(f"xTps{i}") for i in range(2)]
        sm_ps = ph.ps("smps")

        const_in, w_loaded = ph.load("const_in"), ph.load("w_loaded")
        consts, shifted = ph.load("consts"), ph.load("shifted")
        x_loaded = ph.loads("x_loaded")
        z_stored = ph.stores("z_stored")
        x_summed, x_scaled = ph.event("x_summed"), ph.event("x_scaled")
        x_turned = [ph.event(f"x_turned{i}") for i in range(2)]
        xT_ready = ph.event("xT_ready")
        z_ready = [ph.event(f"z_ready{i}") for i in range(NC)]
        z_taken = [ph.event(f"z_taken{i}") for i in range(NC)]
        rank_ready, rank_taken = ph.event("rank_ready"), ph.event("rank_taken")
        decay_ready, decay_taken = ph.event("decay_ready"), ph.event("decay_taken")
        heads_squared, heads_summed = ph.event("heads_squared"), ph.event("heads_summed")
        heads_scaled, heads_done = ph.event("heads_scaled"), ph.event("heads_done")
        gate_exp = ph.event("gate_exp")
        la_abs, la_ln, la_done = ph.event("la_abs"), ph.event("la_ln"), ph.event("la_done")
        block = ctx.enter_context(nc.Block())

        @block.sync
        def _(sp):
            ph.grant(sp)
            sp.dma_start(g1c[:, :], norm1_g[0].rearrange("(k p) -> p k", p=P),
                         allow_slow_non_contiguous=True).then_inc(const_in, 16)
            sp.dma_start(qkg[:, 0:AW].rearrange("p (h d) -> p h d", h=AH),
                         a_q_g[0].unsqueeze(0).unsqueeze(0).to_broadcast([P, AH, AD])).then_inc(const_in, 16)
            sp.dma_start(qkg[:, AW:2 * AW].rearrange("p (h d) -> p h d", h=AH),
                         a_k_g[0].unsqueeze(0).unsqueeze(0).to_broadcast([P, AH, AD])).then_inc(const_in, 16)
            sp.dma_start(wa[0:RANK, :], w_alpha[0]).then_inc(const_in, 16)
            sp.dma_start(wa[RANK:RANK + 1, :], b_alpha).then_inc(const_in, 16)

            def load_x(p, rows):
                sp.dma_start(x_sb[:rows.shape[0], p, :], rows).then_inc(x_loaded[p], 16)

            xr = x_prompt[0].rearrange("(t r) d -> t r d", r=P)
            def pair_of_loads(it, shift):
                pair = Pair(sp, it)
                for k in range(2):
                    t = Turn(pair, k)
                    sp.wait_ge(x_scaled, t.back2)
                    load_x(k, xr[t.t])
                    if shift:
                        old, new = shifts[k]
                        sp.dma_start(new[0, bass.ds(it, 1), 0:WBUF - DEC_T].rearrange("o r h d -> (o r) (h d)"),
                                     old[0, bass.ds(it, 1), DEC_T:WBUF].rearrange("o r h d -> (o r) (h d)")
                                     ).then_inc(shifted, 16)

            with sp.Fori(0, DEC_B) as it:
                pair_of_loads(it, True)
            with sp.Fori(DEC_B, (NT - 1) // 2) as it:
                pair_of_loads(it, False)
            sp.wait_ge(x_scaled, at(sp, NT - 1).back2)
            load_x(0, x_sample.rearrange("b t d -> (b t) d"))
            sp.wait_ge(shifted, 2 * 16 * DEC_B)

        @block.gpsimd
        def _(pool):
            make_identity(pool, ident)
            pool.memset(lrT[:, :], 1.0)
            pool.drain()
            pool.sem_inc(consts, 1)
            pool.wait_ge(const_in, 5 * 16)

            def step(t):
                pool.wait_ge(heads_scaled, t.now)
                qk = z_sb[:, t.p, 0:2 * AW]
                pool.tensor_tensor(qk, qk, qkg[:, :], ALU.mult).then_inc(heads_done, 1)

            all_steps(pool, NT, step)

        @block.scalar
        def _(act):
            for c in range(3):
                lo, hi = (0, 1024, 2048)[c], (1024, 2048, INW)[c]
                act.dma_start(w_sb[:, :, lo:hi], w_in[0][:, lo:hi].rearrange("(k p) n -> p k n", p=P)
                              ).then_inc(w_loaded, 16)
            act.wait_ge(consts, 1)

            def norm_x(t):
                act.wait_ge(x_loaded[t.p], t.dma)
                act.wait_ge(x_scaled, t.back1)
                act.activation(xsq[:, :], x_sb[:, t.p, :], ACT.Square, accum_out=ss[:, 0:1]
                               ).then_inc(x_summed, 1)

            def step(t, more=True):
                p = t.p
                act.wait_ge(z_stored[p], t.dma)
                for c in range(2):
                    act.wait_ge(z_ready[c], t.now)
                    if c == 0:
                        act.wait_ge(heads_summed, t.back1)
                    act.activation(sq[:, c * CH:(c + 1) * CH], z_ps[c][:, :], ACT.Square
                                   ).then_inc(heads_squared, 1)
                act.wait_ge(z_ready[2], t.now)
                act.activation(z_sb[:, p, ZV:ZV + CH], z_ps[2][:, :], ACT.Copy).then_inc(z_taken[2], 1)
                if more:
                    norm_x(t.next)
                act.wait_ge(z_ready[3], t.now)
                act.activation(z_sb[:, p, ZBQ:ZBQ + CH], z_ps[BANK[3]][:, :], ACT.Copy).then_inc(z_taken[3], 1)
                act.wait_ge(z_ready[4], t.now)
                act.activation(z_sb[:, p, ZBV:ZBV + CH], z_ps[BANK[4]][:, :], ACT.Copy).then_inc(z_taken[4], 1)
                act.wait_ge(z_ready[5], t.now)
                act.wait_ge(z_taken[5], t.back1)
                act.activation(gate_t[:, 0, :], z_ps[BANK[5]][:, :], ACT.Exp, scale=-1.0).then_inc(gate_exp, 1)
                act.wait_ge(la_abs, t.now)
                act.activation(la_t[:, 1, :], la_t[:, 0, :], ACT.Exp, scale=-1.0)
                act.drain()
                act.activation(la_t[:, 1, :], la_t[:, 1, :], ACT.Ln, bias=1.0).then_inc(la_ln, 1)
                act.drain()
                act.wait_ge(heads_done, t.now)
                act.wait_ge(la_done, t.now)
                act.wait_ge(z_taken[5], t.now)
                act.dma_start(Z[t.t], z_sb[:, p, :]).then_inc(z_stored[p], 16)

            norm_x(at(act, 0))
            all_steps(act, NT, step, lambda t: step(t, False))
            for p, n in enumerate(((NT + 1) // 2, NT // 2)):
                act.wait_ge(z_stored[p], 16 * n + 16)

        @block.vector
        def _(dve):
            dve.wait_ge(const_in, 5 * 16)

            def scale_x(t):
                dve.wait_ge(x_loaded[t.p], t.dma)
                dve.wait_ge(x_summed, t.now)
                inverse_rms(dve, ss[:, 1:2], ss[:, 0:1], D, (tmp[:, 0, 0:1], tmp[:, 1, 0:1]))
                dve.drain()
                dve.wait_ge(x_turned[1], t.back1)
                dve.tensor_scalar(xs[:, :], x_sb[:, t.p, :], ss[:, 1:2], None, ALU.mult).then_inc(x_scaled, 1)

            def turn_x(t):
                for j in range(2):
                    dve.wait_ge(x_turned[j], t.now)
                    if j == 0:
                        dve.wait_ge(z_ready[5], t.back2)
                    ins = dve.tensor_tensor(xT[:, t.p, 4 * j:4 * j + 4, :],
                                            xT_ps[j][:, :].rearrange("p (k r) -> p k r", k=4),
                                            across(g1c[:, 4 * j:4 * j + 4], P), ALU.mult)
                ins.then_inc(xT_ready, 1)

            def step(t, more=True):
                p = t.p
                dve.wait_ge(rank_ready, t.now)
                dve.tensor_copy(lrT[0:RANK, :], sm_ps[0:RANK, 0:P]).then_inc(rank_taken, 1)
                dve.wait_ge(heads_squared, t.twice)
                dve.tensor_reduce(hss[:, :], sq[:, :].rearrange("p (h d) -> p h d", d=AD), AX.X, ALU.add
                                  ).then_inc(heads_summed, 1)
                dve.drain()
                inverse_rms(dve, hr[:, :], hss[:, :], AD, (tmp[:, 0, :], tmp[:, 1, :]))
                dve.drain()
                dve.wait_ge(z_stored[p], t.dma)
                for c in range(2):
                    ins = dve.tensor_tensor(
                        z_sb[:, p, c * CH:(c + 1) * CH].rearrange("p (h d) -> p h d", d=AD),
                        z_ps[c][:, :].rearrange("p (h d) -> p h d", d=AD),
                        across(hr[:, c * AH:(c + 1) * AH], AD), ALU.mult)
                    ins.then_inc(z_taken[c], 1)
                dve.drain()
                dve.sem_inc(heads_scaled, 1)
                dve.wait_ge(decay_ready, t.now)
                dve.wait_ge(la_done, t.back1)
                dve.wait_ge(la_ln, t.back1)
                a = sm_ps[:, 256:256 + BQK]
                dve.tensor_scalar(la_t[:, 2, :], a, 0.0, None, ALU.min)
                dve.drain()
                dve.scalar_tensor_tensor(la_t[:, 0, :], la_t[:, 2, :], -2.0, a, ALU.mult, ALU.add
                                         ).then_inc(la_abs, 1)
                if more:
                    scale_x(t.next)
                if more:
                    turn_x(t.next)
                dve.wait_ge(la_ln, t.now)
                dve.tensor_tensor(la_t[:, 1, :], la_t[:, 2, :], la_t[:, 1, :], ALU.subtract)
                dve.drain()
                dve.tensor_scalar(z_sb[:, p, ZLA:ZLA + BQK], la_t[:, 1, :], 1.0 / TEMP, None, ALU.mult
                                  ).then_inc(la_done, 1)
                dve.wait_ge(gate_exp, t.now)
                dve.tensor_scalar(gate_t[:, 1, :], gate_t[:, 0, :], 1.0, None, ALU.add)
                dve.drain()
                dve.reciprocal(gate_t[:, 1, :], gate_t[:, 1, :])
                dve.drain()
                dve.tensor_tensor(z_sb[:, p, ZBR:ZBR + BVW], z_ps[BANK[5]][:, :], gate_t[:, 1, :], ALU.mult
                                  ).then_inc(z_taken[5], 1)

            scale_x(at(dve, 0))
            turn_x(at(dve, 0))
            all_steps(dve, NT, step, lambda t: step(t, False))

        @block.tensor
        def _(pe):
            pe.wait_ge(consts, 1)
            pe.wait_ge(const_in, 5 * 16)
            pe.wait_ge(w_loaded, 3 * 16)

            def turn_x(t):
                pe.wait_ge(x_scaled, t.now)
                pe.wait_ge(xT_ready, t.back1)
                for j in range(2):
                    for k in range(4 * j, 4 * j + 4):
                        ins = pe.transpose(xT_ps[j][:, (k % 4) * P:(k % 4 + 1) * P], xs[:, k * P:(k + 1) * P],
                                           ident[:, :])
                    ins.then_inc(x_turned[j], 1)

            def step(t, more=True):
                p = t.p
                pe.wait_ge(xT_ready, t.now)
                pe.wait_ge(rank_taken, t.back1)
                for k in range(KD):
                    ins = pe.matmul(sm_ps[0:RANK, 0:P], w_sb[:, k, NC * CH:INW], xT[:, p, k, :],
                                    start=(k == 0), stop=(k == KD - 1))
                ins.then_inc(rank_ready, 1)
                for c in range(NC):
                    pe.wait_ge(*((z_taken[5], t.back1) if c == 2 else (z_taken[2], t.now) if c == 5 else
                                 (z_taken[c], t.back1)))
                    for k in range(KD):
                        ins = pe.matmul(z_ps[BANK[c]][:, :], xT[:, p, k, :], w_sb[:, k, c * CH:(c + 1) * CH],
                                        start=(k == 0), stop=(k == KD - 1))
                    ins.then_inc(z_ready[c], 1)
                    if c == 0:
                        pe.wait_ge(rank_taken, t.now)
                        pe.wait_ge(la_abs, t.back1)
                        pe.matmul(sm_ps[:, 256:256 + BQK], lrT[:, :], wa[:, :], start=True, stop=True
                                  ).then_inc(decay_ready, 1)
                    if c == 3 and more:
                        turn_x(t.next)

            turn_x(at(pe, 0))
            all_steps(pe, NT, step, lambda t: step(t, False))


def dilated(nc, Z, U, prompt_caches, sample_caches):
    SCALE = AD ** -0.5
    HH = AH // 2
    with ExitStack() as ctx:
        ph = Phase(nc, ctx, "dl")
        ident = ph.sb("ident", [P, P])
        bias = ph.sb("bias", [P, 2, 2, P])
        qkv = ph.sb("qkv", [P, 2, 2 * AW])
        v_sb = ph.sb("v", [P, 2, AW])
        qT = ph.sb("qT", [P, 2, 4, P])
        kT = ph.sb("kT", [P, 4, 2, P])
        sm = ph.sb("sm", [P, 2, HH, 2 * P])
        mx = ph.sb("mx", [P, 2, HH])
        pr = ph.sb("pr", [P, 2, HH, 2 * P])
        pT = ph.sb("pT", [P, 2, HH, 2, P])
        ms = ph.sb("ms", [P, 2, 2 * AH])
        u_sb = ph.sb("u", [P, 2, UW])
        t_ps = ph.ps("tps")
        s_ps = [ph.ps(f"sps{h}", 1024) for h in range(2)]
        pT_ps = ph.ps("pTps", 1024)
        o_ps = ph.ps("ops")

        consts, cached = ph.load("consts"), ph.load("cached")
        qk_loaded, v_loaded = ph.loads("qk_loaded"), ph.loads("v_loaded")
        u_stored, u_free = ph.loads("u_stored"), ph.event("u_free")
        q_turned, k_turned, qT_ready, kT_ready = (ph.event("q_turned"), ph.event("k_turned"),
                                                  ph.event("qT_ready"), ph.event("kT_ready"))
        scored = [ph.event(f"scored{h}") for h in range(2)]
        max_ready = [ph.event(f"max_ready{h}") for h in range(2)]
        masked = [ph.event(f"masked{h}") for h in range(2)]
        exps_done = [ph.event(f"exps_done{h}") for h in range(2)]
        p_turned = [ph.event(f"p_turned{h}") for h in range(2)]
        pT_ready = [ph.event(f"pT_ready{h}") for h in range(2)]
        o_ready, o_taken = ph.event("o_ready"), ph.event("o_taken")
        block = ctx.enter_context(nc.Block())

        def blocks(eng, step):
            done = 0
            for g, (_, dil) in enumerate(GROUPS):
                pairs = SEQ // (dil * P) // 2

                def head(r, n, last=False):
                    pair = Pair(eng, n)
                    step(Turn(pair, 0), g, r, True, 0 if g == 0 else 2, False)
                    step(Turn(pair, 1), g, r + P * dil, False, 1, last)

                def rest(r, n):
                    with eng.Fori(1, pairs) as m:
                        pair = Pair(eng, m + n)
                        for k in range(2):
                            step(Turn(pair, k), g, m * (2 * P * dil) + (r + k * P * dil), False, 2, False)

                if dil == 1:
                    head(0, done)
                    rest(0, done)
                elif pairs > 1:
                    with eng.Fori(0, dil) as r:
                        head(r, r * pairs + done)
                        rest(r, r * pairs + done)
                else:
                    with eng.Fori(0, dil - 1) as r:
                        head(r, r + done)
                    head(dil - 1, dil - 1 + done, last=True)
                done += dil * pairs
            return done

        def rows(ap, row, dil):
            return ap[bass.ds(row, P, step=dil), :]

        Zr = Z.rearrange("t r w -> (t r) w")

        @block.sync
        def _(sp):
            ph.grant(sp)
            for col, of_prompt, of_sample in zip((ZK, ZV), prompt_caches, sample_caches):
                sp.dma_start(of_prompt[0, 0].rearrange("r h d -> r (h d)"), Zr[SEQ - WBUF:SEQ, col:col + AW]
                             ).then_inc(cached, 16)
                sp.dma_start(of_sample[0][:, WBUF - DEC_T:WBUF].rearrange("b r h d -> b r (h d)"),
                             Zr[SEQ:TOKENS, col:col + AW].rearrange("(b r) w -> b r w", r=DEC_T)).then_inc(cached, 16)

            def step(t, g, row, first, before, last):
                dil = GROUPS[g][1]
                sp.wait_ge(k_turned, t.back2)
                sp.wait_ge(q_turned, t.back2)
                sp.dma_start(qkv[:, t.p, :], rows(Zr[:, 0:2 * AW], row, dil)).then_inc(qk_loaded[t.p], 16)

            blocks(sp, step)
            sp.wait_ge(cached, 64)

        @block.gpsimd
        def _(pool):
            make_identity(pool, ident)
            pool.memset(bias[:, :, :, :], 0.0)
            pool.drain()
            for p in range(2):
                pool.affine_select(out=bias[:, p, p, :], in_=bias[:, p, p, :], compare_op=ALU.is_ge, fill=NEG,
                                   base=0, pattern=[[-1, P]], channel_multiplier=1)
                pool.affine_select(out=bias[:, p, 1 - p, :], in_=bias[:, p, 1 - p, :], compare_op=ALU.is_ge,
                                   fill=NEG, base=0, pattern=[[1, P]], channel_multiplier=-1)
            pool.drain()
            pool.sem_inc(consts, 1)

            def step(t, g, row, first, before, last):
                pool.wait_ge(o_taken, t.now)
                pool.dma_start(rows(U[g], row, GROUPS[g][1]), u_sb[:, t.p, :]).then_inc(u_stored[t.p], 16)
                pool.wait_ge(u_stored[t.p], t.dma)
                pool.sem_inc(u_free, 1)

            blocks(pool, step)

        @block.scalar
        def _(act):
            def step(t, g, row, first, before, last):
                p = t.p
                if not last:
                    take_q(t.next)
                w = P if first else 2 * P
                for h in range(2):
                    act.wait_ge(max_ready[h], t.now)
                    act.wait_ge(p_turned[h], t.back1)
                    for j in range(HH):
                        a = AH + 2 * j + h
                        ins = act.activation(pr[:, h, j, 0:w], sm[:, h, j, 0:w], ACT.Exp,
                                             bias=ms[:, p, a - AH:a - AH + 1], scale=SCALE,
                                             accum_out=ms[:, p, a:a + 1])
                    ins.then_inc(exps_done[h], 1)
                    if h == 0 and not last:
                        take_k(t.next)
                if before:
                    finish(t.prev)
                act.dma_start(v_sb[:, p, :], rows(Zr[:, ZV:ZV + AW], row, GROUPS[g][1])).then_inc(v_loaded[p], 16)

            def finish(t):
                act.drain()
                act.wait_ge(o_ready, t.now)
                act.wait_ge(u_free, t.back2)
                act.activation(u_sb[:, t.p, AW:UW], ms[:, t.p, :], ACT.Copy)
                act.activation(u_sb[:, t.p, 0:AW], o_ps[:, :], ACT.Copy).then_inc(o_taken, 1)

            def take_q(t):
                act.wait_ge(q_turned, t.now)
                act.wait_ge(scored[1], t.back2)
                act.activation(qT[:, t.p, :, :], t_ps[:, :].rearrange("p (j r) -> p j r", j=4), ACT.Copy
                               ).then_inc(qT_ready, 1)

            def take_k(t):
                act.wait_ge(k_turned, t.now)
                act.wait_ge(scored[1], t.back1)
                act.activation(kT[:, :, t.p, :], t_ps[:, :].rearrange("p (j r) -> p j r", j=4), ACT.Copy
                               ).then_inc(kT_ready, 1)

            take_q(at(act, 0))
            take_k(at(act, 0))
            n = blocks(act, step)
            finish(at(act, 2 * n - 1))

        @block.vector
        def _(dve):
            dve.wait_ge(consts, 1)

            def step(t, g, row, first, before, last):
                p = t.p
                w = P if first else 2 * P
                dve.wait_ge(o_taken, t.back2)
                for h in range(2):
                    if before:
                        take_pT(t.prev, h, before)
                    dve.wait_ge(scored[h], t.now)
                    dve.wait_ge(exps_done[h], t.back1)
                    s = s_ps[h][:, :].rearrange("p (j k) -> p j k", j=HH)[:, :, 0:w]
                    b = bias[:, p, :, :].rearrange("p s k -> p (s k)")[:, 0:w].unsqueeze(1).to_broadcast([P, HH, w])
                    dve.tensor_tensor(sm[:, h, :, 0:w], s, b, ALU.add).then_inc(masked[h], 1)
                    dve.drain()
                    dve.tensor_reduce(mx[:, h, :], sm[:, h, :, 0:w], AX.X, ALU.max)
                    dve.drain()
                    dve.tensor_scalar(ms[:, p, h:AH:2], mx[:, h, :], -SCALE, None, ALU.mult
                                      ).then_inc(max_ready[h], 1)

            def take_pT(t, h, n):
                dve.wait_ge(p_turned[h], t.now)
                dve.wait_ge(o_ready, t.back1)
                dve.tensor_copy(pT[:, h, :, 0:n, :],
                                pT_ps[:, :].rearrange("p (j s r) -> p j s r", j=HH, s=2)[:, :, 0:n, :]
                                ).then_inc(pT_ready[h], 1)

            n = blocks(dve, step)
            for h in range(2):
                take_pT(at(dve, 2 * n - 1), h, 2)

        @block.tensor
        def _(pe):
            pe.wait_ge(consts, 1)

            def step(t, g, row, first, before, last):
                n = 1 if first else 2
                if not last:
                    turn_q(t.next)
                pe.wait_ge(kT_ready, t.now)
                for h in range(2):
                    if before:
                        turn_p(t.prev, h, before)
                    pe.wait_ge(masked[h], t.back1)
                    for j in range(HH):
                        hd = 2 * j + h
                        lo = h * AD
                        ins = pe.matmul(s_ps[h][:, j * 2 * P:j * 2 * P + n * P], qT[lo:lo + AD, t.p, hd // 2, :],
                                        kT[lo:lo + AD, hd // 2, 0:n, :], start=True, stop=True)
                    ins.then_inc(scored[h], 1)
                    if h == 0 and not last:
                        turn_k(t.next)
                if before:
                    weigh_values(t.prev, before)

            def turn_q(t):
                pe.wait_ge(qk_loaded[t.p], t.dma)
                pe.wait_ge(kT_ready, t.back1)
                for j in range(4):
                    ins = pe.transpose(t_ps[:, j * P:(j + 1) * P], qkv[:, t.p, j * P:(j + 1) * P], ident[:, :])
                ins.then_inc(q_turned, 1)

            def turn_k(t):
                pe.wait_ge(qT_ready, t.now)
                for j in range(4, 8):
                    ins = pe.transpose(t_ps[:, (j - 4) * P:(j - 3) * P], qkv[:, t.p, j * P:(j + 1) * P], ident[:, :])
                ins.then_inc(k_turned, 1)

            def turn_p(t, h, n):
                pe.wait_ge(exps_done[h], t.now)
                if h == 0:
                    pe.wait_ge(pT_ready[1], t.back1)
                else:
                    pe.wait_ge(pT_ready[0], t.now)
                for j in range(HH):
                    for s in range(n):
                        ins = pe.transpose(pT_ps[:, (2 * j + s) * P:(2 * j + s + 1) * P],
                                           pr[:, h, j, s * P:(s + 1) * P], ident[:, :])
                ins.then_inc(p_turned[h], 1)

            def weigh_values(t, n):
                pe.wait_ge(v_loaded[t.p], t.dma)
                pe.wait_ge(o_taken, t.back1)
                for h in range(2):
                    pe.wait_ge(pT_ready[h], t.now)
                    for j in range(HH):
                        hd = 2 * j + h
                        for s in range(n):
                            ins = pe.matmul(o_ps[:, hd * AD:(hd + 1) * AD], pT[:, h, j, s, :],
                                            v_sb[:, s, hd * AD:(hd + 1) * AD], start=(s == 0), stop=(s == n - 1))
                ins.then_inc(o_ready, 1)

            turn_q(at(pe, 0))
            turn_k(at(pe, 0))
            n = blocks(pe, step)
            t = at(pe, 2 * n - 1)
            for h in range(2):
                turn_p(t, h, 2)
            weigh_values(t, 2)


def gla(nc, Z, out_g, state0, OB, new_prompt, new_sample):
    VW = 2 * BV
    NP = BH // 2
    CQ, CK, CV, CR, CL = (z - ZBQ for z in (ZBQ, ZBK, ZBV, ZBR, ZLA))
    NTP = NT - 1
    with ExitStack() as ctx:
        ph = Phase(nc, ctx, "gl")
        ident = ph.sb("ident", [P, P])
        tri = ph.sb("tri", [P, P])
        tric = ph.sb("tric", [P, P])
        cuts = ph.sb("cuts", [P, 3])
        halves = ph.sb("halves", [P, NP, 2, BV])
        gout = ph.sb("gout", [P, BH, BV])
        tmp = ph.sb("tmp", [P, 2, BH])
        z_sb = ph.sb("z", [P, 2, ZW - ZBQ])
        eb = ph.sb("eb", [P, 2, BQK])
        ec = ph.sb("ec", [P, NP, 8])
        qk = ph.sb("qk", [P, 2, BQK])
        qkT = ph.sb("qkT", [P, 2 * NP, P])
        att = ph.sb("att", [P, BH, P])
        sc = ph.sb("sc", [P, NP, VW])
        st = ph.sb("st", [P, NP, VW])
        dm = ph.sb("dm", [P, NP, VW])
        osq = ph.sb("osq", [P, BVW])
        oss = ph.sb("oss", [P, BH])
        ors = ph.sb("ors", [P, BH])
        gr = ph.sb("gr", [P, 2, BVW])
        o1 = ph.sb("o1", [P, BVW])
        ob = ph.sb("ob", [P, 2, BVW])
        b_ps, c_ps, qkT_ps, o_ps, d_ps = (ph.ps(n) for n in ("bps", "cps", "qkTps", "ops", "dps"))
        att_ps = [ph.ps(f"attps{i}") for i in range(2)]
        same = ph.sb("same", [SAMPLE, DEC_B, DEC_T])
        tri8 = ph.sb("tri8", [SAMPLE, SAMPLE])
        seq1 = ph.sb("seq1", [SAMPLE, DEC_B])
        cols8 = ph.sb("cols8", [P, DEC_B, SAMPLE])
        qTm = ph.sb("qTm", [P, NP, DEC_B, SAMPLE])
        km = ph.sb("km", [SAMPLE, DEC_B, BQK])
        sts = ph.sb("sts", [P, DEC_B, NP, VW])
        nst = ph.sb("nst", [P, DEC_B, NP, VW])

        const_in, consts, state_in = ph.load("const_in"), ph.load("consts"), ph.load("state_in")
        z_loaded = ph.loads("z_loaded")
        o_stored = ph.stores("o_stored")
        s_stored = ph.load("s_stored")
        b_ready, b_exp, scaled, qk_turned, qkT_ready = (ph.event(n) for n in (
            "b_ready", "b_exp", "scaled", "qk_turned", "qkT_ready"))
        att_ready, att_masked, sc_ready, o_ready, d_ready = (ph.event(n) for n in (
            "att_ready", "att_masked", "sc_ready", "o_ready", "d_ready"))
        st_ready, o_squared, o_summed, gr_ready, ob_ready = (ph.event(n) for n in (
            "st_ready", "o_squared", "o_summed", "gr_ready", "ob_ready"))
        q_masked, d8_ready, d8_used = ph.load("q_masked"), ph.load("d8_ready"), ph.load("d8_used")
        block = ctx.enter_context(nc.Block())

        @block.sync
        def _(sp):
            ph.grant(sp)
            sp.dma_start(gout[:, :, :], out_g[0].unsqueeze(0).unsqueeze(0).to_broadcast([P, BH, BV])
                         ).then_inc(const_in, 16)

            def step(t, last=False):
                n = SAMPLE if last else P
                sp.wait_ge(d_ready, t.back2)
                sp.wait_ge(gr_ready, t.back2)
                sp.wait_ge(o_ready, t.back2)
                sp.dma_start(z_sb[0:n, t.p, :], Z[t.t][0:n, ZBQ:ZW]).then_inc(z_loaded[t.p], 16)

            all_steps(sp, NT, step, lambda t: step(t, True))
            sp.wait_ge(consts, 2)
            for e in range(2):
                sp.dma_start(sts[e * BK:(e + 1) * BK, :, :, e * BV:(e + 1) * BV].rearrange("k b j v -> k (b j) v"),
                             state0[0].rearrange("b (j e) k v -> e k (b j) v", e=2)[e]).then_inc(state_in, 16)
            sp.wait_ge(st_ready, at(sp, NTP - 1).now)
            for e in range(2):
                sp.dma_start(new_prompt[0, 0].rearrange("(j e) k v -> e k j v", e=2)[e],
                             st[e * BK:(e + 1) * BK, :, e * BV:(e + 1) * BV]).then_inc(s_stored, 16)
            sp.wait_ge(d8_used, DEC_B)
            for e in range(2):
                sp.dma_start(new_sample[0].rearrange("b (j e) k v -> e k (b j) v", e=2)[e],
                             nst[e * BK:(e + 1) * BK, :, :, e * BV:(e + 1) * BV].rearrange("k b j v -> k (b j) v")
                             ).then_inc(s_stored, 16)
            sp.wait_ge(s_stored, 64)

        @block.gpsimd
        def _(pool):
            make_identity(pool, ident)
            for m in (tri, halves, same, cols8):
                pool.memset(m[tuple(slice(None) for _ in m.shape)], 1.0)
            pool.memset(cuts[:, :], 1.0)
            pool.memset(st[:, :, :], 0.0)
            pool.memset(sts[:, :, :, :], 0.0)
            pool.drain()
            pool.affine_select(out=tri[:, :], in_=tri[:, :], compare_op=ALU.is_ge, fill=0.0, base=0,
                               pattern=[[1, P]], channel_multiplier=-1)
            pool.affine_select(out=cuts[:, 0:1], in_=cuts[:, 0:1], compare_op=ALU.is_ge, fill=0.0,
                               base=P // 2 - 1, pattern=[[0, 1]], channel_multiplier=-1)
            pool.affine_select(out=cuts[:, 2:3], in_=cuts[:, 2:3], compare_op=ALU.is_ge, fill=0.0,
                               base=-P // 2, pattern=[[0, 1]], channel_multiplier=1)
            for e in range(2):
                pool.affine_select(out=halves[:, :, e, :], in_=halves[:, :, e, :], compare_op=ALU.is_ge, fill=0.0,
                                   base=(BK - 1) * (1 - e) - BK * e, pattern=[[0, NP], [0, BV]],
                                   channel_multiplier=2 * e - 1)
            for b0, b1, m in ((0, -DEC_T, 1), (DEC_T - 1, DEC_T, -1)):
                pool.affine_select(out=same[:, :, :], in_=same[:, :, :], compare_op=ALU.is_ge, fill=0.0, base=b0,
                                   pattern=[[b1, DEC_B], [0, DEC_T]], channel_multiplier=m)
                pool.affine_select(out=cols8[:, :, :], in_=cols8[:, :, :], compare_op=ALU.is_ge, fill=0.0, base=b0,
                                   pattern=[[b1, DEC_B], [m, SAMPLE]], channel_multiplier=0)
                pool.drain()
            pool.tensor_scalar(tric[:, :], tri[:, :], cuts[:, 0:1], None, ALU.subtract)
            pool.tensor_tensor(tri8[:, :], tri[0:SAMPLE, 0:SAMPLE], same[:, :, :].rearrange("s b t -> s (b t)"),
                               ALU.mult)
            pool.tensor_copy(seq1[:, :], same[:, :, 0])
            pool.drain()
            pool.sem_inc(consts, 2)
            pool.wait_ge(const_in, 16)

            def step(t):
                pool.wait_ge(z_loaded[t.p], t.dma)
                pool.wait_ge(ob_ready, t.back2)
                pool.tensor_tensor(gr[:, t.p, :], z_sb[:, t.p, CR:CR + BVW],
                                   gout[:, :, :].rearrange("p h v -> p (h v)"), ALU.mult).then_inc(gr_ready, 1)

            all_steps(pool, NT, step)

        @block.scalar
        def _(act):
            act.wait_ge(consts, 1)

            def step(t, last=False):
                p, n = t.p, SAMPLE if last else P
                act.wait_ge(b_ready, t.now)
                act.wait_ge(scaled, t.back1)
                act.wait_ge(st_ready, t.back1)
                act.activation(eb[0:n, 0, :], b_ps[0:n, 0:BQK], ACT.Exp)
                act.activation(eb[0:n, 1, :], b_ps[0:n, 0:BQK], ACT.Exp, scale=-1.0)
                w = DEC_B if last else 3
                act.activation(ec[:, :, 0:w], c_ps[:, 0:NP * w].rearrange("p (j c) -> p j c", j=NP), ACT.Exp
                               ).then_inc(b_exp, 1)
                act.wait_ge(qk_turned, t.now)
                act.wait_ge(d_ready, t.back1)
                act.activation(qkT[:, :, 0:n], qkT_ps[:, :].rearrange("p (j r) -> p j r", r=P)[:, :, 0:n], ACT.Copy
                               ).then_inc(qkT_ready, 1)
                act.wait_ge(o_ready, t.now)
                act.wait_ge(o_summed, t.back1)
                act.activation(osq[0:n, :], o_ps[0:n, :], ACT.Square).then_inc(o_squared, 1)
                act.wait_ge(ob_ready, t.now)
                act.dma_start(OB[t.t][0:n], ob[0:n, p, :]).then_inc(o_stored[p], 16)

            all_steps(act, NT, step, lambda t: step(t, True))
            for p, n in enumerate(((NT + 1) // 2, NT // 2)):
                act.wait_ge(o_stored[p], 16 * n + 16)

        @block.vector
        def _(dve):
            dve.wait_ge(consts, 1)

            def scale_qk(t, n):
                dve.wait_ge(z_loaded[t.p], t.dma)
                dve.wait_ge(b_exp, t.now)
                dve.wait_ge(d_ready, t.back1)
                dve.scalar_tensor_tensor(qk[0:n, 0, :], z_sb[0:n, t.p, CQ:CQ + BQK], BK ** -0.5, eb[0:n, 0, :],
                                         ALU.mult, ALU.mult)
                dve.tensor_tensor(qk[0:n, 1, :], z_sb[0:n, t.p, CK:CK + BQK], eb[0:n, 1, :], ALU.mult
                                  ).then_inc(scaled, 1)

            def mask_att(t, n, mask):
                dve.wait_ge(att_ready, t.now)
                dve.wait_ge(o_ready, t.back1)
                for e in range(2):
                    ins = dve.tensor_tensor(att[0:n, e:BH:2, 0:n],
                                            att_ps[e][0:n, 0:2 * P].rearrange("s (j t) -> s j t", j=NP)[:, :, 0:n],
                                            mask.unsqueeze(1).to_broadcast([n, NP, n]), ALU.mult)
                ins.then_inc(att_masked, 1)

            def outputs(t, n):
                dve.wait_ge(o_squared, t.now)
                dve.tensor_reduce(oss[0:n, :], osq[0:n, :].rearrange("p (h v) -> p h v", v=BV), AX.X, ALU.add
                                  ).then_inc(o_summed, 1)
                dve.drain()
                inverse_rms(dve, ors[0:n, :], oss[0:n, :], BV, (tmp[0:n, 0, :], tmp[0:n, 1, :]))
                dve.drain()
                dve.tensor_tensor(o1[0:n, :].rearrange("p (h v) -> p h v", v=BV),
                                  o_ps[0:n, :].rearrange("p (h v) -> p h v", v=BV), across(ors[0:n, :], BV), ALU.mult)
                dve.drain()
                dve.wait_ge(gr_ready, t.now)
                dve.wait_ge(o_stored[t.p], t.dma)
                dve.tensor_tensor(ob[0:n, t.p, :], o1[0:n, :], gr[0:n, t.p, :], ALU.mult).then_inc(ob_ready, 1)

            def step(t):
                scale_qk(t, P)
                dve.wait_ge(o_ready, t.back1)
                dve.tensor_tensor(sc[:, :, :], st[:, :, :], ec[:, :, 0:1].to_broadcast([P, NP, VW]), ALU.mult
                                  ).then_inc(sc_ready, 1)
                dve.wait_ge(d_ready, t.now)
                dve.tensor_tensor(dm[:, :, :], d_ps[:, :].rearrange("p (j v) -> p j v", j=NP),
                                  halves[:, :, :, :].rearrange("p j e v -> p j (e v)"), ALU.mult)
                dve.drain()
                dve.tensor_tensor(dm[:, :, :], dm[:, :, :], ec[:, :, 2:3].to_broadcast([P, NP, VW]), ALU.mult)
                for j in range(NP):
                    if j == 0:
                        dve.drain()
                    ins = dve.scalar_tensor_tensor(st[:, j, :], st[:, j, :], ec[:, j, 1:2], dm[:, j, :],
                                                   ALU.mult, ALU.add)
                ins.then_inc(st_ready, 1)
                mask_att(t, P, tri[:, :])
                outputs(t, P)
                dve.drain()

            def sample(t):
                scale_qk(t, SAMPLE)
                for b in range(DEC_B):
                    if b == 0:
                        dve.drain()
                    dve.tensor_scalar(km[:, b, :], qk[0:SAMPLE, 1, :], seq1[:, b:b + 1], None, ALU.mult)
                dve.wait_ge(qkT_ready, t.now)
                for j in range(NP):
                    ins = dve.tensor_tensor(qTm[:, j, :, :], cols8[:, :, :],
                                            qkT[:, j, 0:SAMPLE].unsqueeze(1).to_broadcast([P, DEC_B, SAMPLE]),
                                            ALU.mult)
                ins.then_inc(q_masked, 1)
                mask_att(t, SAMPLE, tri8[:, :])
                dve.wait_ge(state_in, 32)
                for b in range(DEC_B):
                    d = (dm, sc)[b % 2]
                    dve.wait_ge(d8_ready, b + 1)
                    dve.tensor_tensor(d[:, :, :], (d_ps, b_ps)[b % 2][:, :].rearrange("p (j v) -> p j v", j=NP),
                                      halves[:, :, :, :].rearrange("p j e v -> p j (e v)"), ALU.mult)
                    dve.drain()
                    dve.tensor_tensor(d[:, :, :], d[:, :, :], sts[:, b, :, :], ALU.add)
                    dve.drain()
                    dve.tensor_tensor(nst[:, b, :, :], d[:, :, :], ec[:, :, b:b + 1].to_broadcast([P, NP, VW]),
                                      ALU.mult).then_inc(d8_used, 1)
                outputs(t, SAMPLE)

            all_steps(dve, NT, step, sample)

        @block.tensor
        def _(pe):
            pe.wait_ge(consts, 1)

            def sums(t, n, m, cut):
                la = z_sb[0:n, t.p, CL:CL + BQK]
                pe.wait_ge(z_loaded[t.p], t.dma)
                pe.wait_ge(b_exp, t.back1)
                pe.matmul(b_ps[0:n, 0:BQK], m, la, start=True, stop=True)
                w = cut.shape[1]
                for j in range(NP):
                    ins = pe.matmul(c_ps[:, j * w:(j + 1) * w], la[:, j * P:(j + 1) * P], cut, start=True, stop=True)
                ins.then_inc(b_ready, 1)

            def turn_qk(t, n):
                pe.wait_ge(scaled, t.now)
                pe.wait_ge(qkT_ready, t.back1)
                for j in range(2 * NP):
                    ins = pe.transpose(qkT_ps[:, j * P:j * P + n], qk[0:n, j // NP, (j % NP) * P:(j % NP + 1) * P],
                                       ident[0:n, 0:n])
                ins.then_inc(qk_turned, 1)

            def scores(t, n):
                pe.wait_ge(qkT_ready, t.now)
                pe.wait_ge(att_masked, t.back1)
                for h in range(BH):
                    lo, j = h % 2 * BK, h // 2
                    ins = pe.matmul(att_ps[h % 2][0:n, j * P:j * P + n], qkT[lo:lo + BK, NP + j, 0:n],
                                    qkT[lo:lo + BK, j, 0:n], start=True, stop=True)
                ins.then_inc(att_ready, 1)

            def step(t):
                p = t.p
                sums(t, P, tric[:, :], cuts[:, :])
                turn_qk(t, P)
                pe.wait_ge(st_ready, t.back1)
                for j in range(NP):
                    ins = pe.matmul(d_ps[:, j * VW:(j + 1) * VW], qk[:, 1, j * P:(j + 1) * P],
                                    z_sb[:, p, CV + j * VW:CV + (j + 1) * VW], start=True, stop=True)
                ins.then_inc(d_ready, 1)
                scores(t, P)
                pe.wait_ge(sc_ready, t.now)
                pe.wait_ge(att_masked, t.now)
                pe.wait_ge(ob_ready, t.back1)
                for j in range(NP):
                    pe.matmul(o_ps[:, j * VW:(j + 1) * VW], qkT[:, j, :], sc[:, j, :], start=True, stop=False,
                              skip_group_check=True)
                    for e in range(2):
                        h = 2 * j + e
                        ins = pe.matmul(o_ps[:, h * BV:(h + 1) * BV], att[:, h, :],
                                        z_sb[:, p, CV + h * BV:CV + (h + 1) * BV], start=False, stop=True,
                                        skip_group_check=True)
                ins.then_inc(o_ready, 1)

            def sample(t):
                p, n = t.p, SAMPLE
                sums(t, n, tri8[:, :], seq1[:, :])
                turn_qk(t, n)
                scores(t, n)
                pe.wait_ge(q_masked, 1)
                pe.wait_ge(b_exp, t.now)
                pe.wait_ge(st_ready, t.back1)
                for b in range(DEC_B):
                    if b >= 2:
                        pe.wait_ge(d8_used, b - 1)
                    for j in range(NP):
                        ins = pe.matmul((d_ps, b_ps)[b % 2][:, j * VW:(j + 1) * VW], km[:, b, j * P:(j + 1) * P],
                                        z_sb[0:n, p, CV + j * VW:CV + (j + 1) * VW], start=True, stop=True)
                    ins.then_inc(d8_ready, 1)
                pe.wait_ge(state_in, 32)
                pe.wait_ge(att_masked, t.now)
                pe.wait_ge(ob_ready, t.back1)
                for j in range(NP):
                    for b in range(DEC_B):
                        pe.matmul(o_ps[0:n, j * VW:(j + 1) * VW], qTm[:, j, b, :], sts[:, b, j, :],
                                  start=(b == 0), stop=False, skip_group_check=True)
                    for e in range(2):
                        h = 2 * j + e
                        ins = pe.matmul(o_ps[0:n, h * BV:(h + 1) * BV], att[0:n, h, 0:n],
                                        z_sb[0:n, p, CV + h * BV:CV + (h + 1) * BV], start=False, stop=True,
                                        skip_group_check=True)
                ins.then_inc(o_ready, 1)

            all_steps(pe, NT, step, sample)


def dilated_sample(nc, Z, cache_k, cache_v, OAS):
    SCALE = AD ** -0.5
    NTL = 11
    CT = 10 * P
    NK = CT + DEC_T
    R = AH * DEC_T
    F0 = WBUF - 512
    with ExitStack() as ctx:
        ph = Phase(nc, ctx, "ds")
        ident = ph.sb("ident", [P, P])
        dist_i = ph.sb("dist_i", [R, NK], I32)
        tok_i = ph.sb("tok_i", [R, 1], I32)
        tok_f = ph.sb("tok_f", [R, 1])
        low_i = ph.sb("low_i", [R, NK], I32)
        dist = ph.sb("dist", [R, NK])
        past = ph.sb("past", [R, NK])
        part = ph.sb("part", [R, NK])
        mult = ph.sb("mult", [R, NK])
        bias = ph.sb("bias", [R, NK])
        diag = ph.sb("diag", [R, AH, AD])
        pick = ph.sb("pick", [R, DEC_T])
        tok8 = ph.sb("tok8", [R, DEC_T])
        new = ph.sb("new", [DEC_T, 2, 3 * AW])
        k_sb = ph.sb("k", [P, 2, 10, AW])
        v_sb = ph.sb("v", [P, 2, 10, AW])
        kT = ph.sb("kT", [P, 4, NK])
        qbd = ph.sb("qbd", [P, 4 * 80])
        sm = ph.sb("sm", [R, NK])
        pr = ph.sb("pr", [R, NK])
        stat = ph.sb("stat", [R, 4])
        pT = ph.sb("pT", [P, NTL, R])
        o_sb = ph.sb("o", [R, AW])
        out = ph.sb("out", [DEC_T, 2, AW])
        t_ps = [ph.ps(f"tps{i}") for i in range(2)]
        s_ps = ph.ps("sps", 1536)
        pT_ps = ph.ps("pTps", 1024)
        o_ps = ph.ps("ops")

        consts, masks = ph.load("consts"), ph.load("masks")
        new_loaded, k_loaded, v_loaded = ph.loads("new_loaded"), ph.loads("k_loaded"), ph.loads("v_loaded")
        out_stored = ph.stores("out_stored")
        q_turned, q_taken = ph.event("q_turned"), ph.event("q_taken")
        k_turned = [ph.event(f"k_turned{i}") for i in range(2)]
        k_taken = [ph.event(f"k_taken{i}") for i in range(2)]
        scored, masked, max_ready, exps_done, p_ready = (ph.event(n) for n in (
            "scored", "masked", "max_ready", "exps_done", "p_ready"))
        p_turned, pT_ready, o_ready, o_scaled, out_ready, out_taken = (ph.event(n) for n in (
            "p_turned", "pT_ready", "o_ready", "o_scaled", "out_ready", "out_taken"))
        block = ctx.enter_context(nc.Block())

        @block.sync
        def _(sp):
            ph.grant(sp)
            Zs = Z[NT - 1]

            def step(t):
                p = t.p
                sp.wait_ge(o_ready, t.back2)
                for src, dst, loaded in ((cache_k, k_sb, k_loaded), (cache_v, v_sb, v_loaded)):
                    rows = src[0][bass.ds(t.t, 1)].rearrange("o (p c) h d -> p (o c) (h d)", c=16)
                    sp.dma_start(dst[:, p, 0:8, :], rows[:, 0:8, :]).then_inc(loaded[p], 16)
                    late = rows[F0 // 16:P, 8:16, :].rearrange("p (u i) n -> i p u n", i=4)
                    for i in range(4):
                        sp.dma_start(dst[32 * i:32 * i + 32, p, 8:10, :], late[i]).then_inc(loaded[p], 16)
                    if src is cache_k:
                        sp.dma_start(new[:, p, :], Zs[bass.ds(t.t * DEC_T, DEC_T), 0:3 * AW]
                                     ).then_inc(new_loaded[p], 16)

            all_steps(sp, DEC_B, step)

        @block.gpsimd
        def _(pool):
            make_identity(pool, ident)
            pool.memset(qbd[:, :], 0.0)
            pool.memset(diag[:, :, :], 1.0)
            pool.iota(dist_i[:, 0:8 * P], [[-1, 8], [-16, P]], base=WBUF, channel_multiplier=0)
            pool.iota(dist_i[:, 8 * P:CT], [[-4, 2], [-1, 4], [-16, 32]], base=WBUF - F0 - 8, channel_multiplier=0)
            pool.iota(dist_i[:, CT:NK], [[-1, DEC_T]], base=0, channel_multiplier=0)
            pool.iota(tok_i[:, :], [[0, 1]], base=0, channel_multiplier=1)
            pool.iota(tok8[:, :], [[1, DEC_T]], base=0, channel_multiplier=0, allow_small_or_imprecise_dtypes=True)
            pool.drain()
            for b0, b1, m in ((0, -DEC_T, 1), (DEC_T - 1, DEC_T, -1)):
                pool.affine_select(out=diag[:, :, :], in_=diag[:, :, :], compare_op=ALU.is_ge, fill=0.0, base=b0,
                                   pattern=[[b1, AH], [0, AD]], channel_multiplier=m)
                pool.drain()
            pool.sem_inc(consts, 1)

        @block.scalar
        def _(act):
            def step(t):
                p = t.p
                for k in range(6):
                    w = P if k < 5 else DEC_T
                    act.wait_ge(k_turned[0], t.of(6, k))
                    if k == 0:
                        act.wait_ge(scored, t.back1)
                    act.activation(kT[:, :, 2 * k * P:2 * k * P + w],
                                   t_ps[0][:, :].rearrange("p (j r) -> p j r", j=4)[:, :, 0:w], ACT.Copy
                                   ).then_inc(k_taken[0], 1)
                act.wait_ge(max_ready, t.now)
                act.activation(pr[:, :], sm[:, :], ACT.Exp, bias=stat[:, 1:2], scale=SCALE).then_inc(exps_done, 1)
                act.wait_ge(out_ready, t.now)
                act.wait_ge(out_stored[p], t.dma)
                act.activation(out[:, p, :], t_ps[1][0:DEC_T, :], ACT.Copy).then_inc(out_taken, 1)
                act.wait_ge(out_taken, t.now)
                act.dma_start(OAS[bass.ds(t.t * DEC_T, DEC_T), :], out[:, p, :]).then_inc(out_stored[p], 16)

            all_steps(act, DEC_B, step)
            for p in range(2):
                act.wait_ge(out_stored[p], 16 * (DEC_B // 2) + 16)

        @block.vector
        def _(dve):
            dve.wait_ge(consts, 1)
            dve.tensor_scalar(tok_i[:, :], tok_i[:, :], DEC_T - 1, None, ALU.bitwise_and)
            dve.drain()
            dve.tensor_copy(tok_f[:, :], tok_i[:, :])
            dve.drain()
            dve.tensor_scalar(dist[:, :], dist_i[:, :], tok_f[:, :], None, ALU.add)
            dve.tensor_scalar(pick[:, :], tok8[:, :], tok_f[:, :], None, ALU.is_equal)
            dve.drain()
            dve.tensor_copy(dist_i[:, :], dist[:, :])
            dve.tensor_scalar(past[:, :], dist[:, :], 0.0, None, ALU.is_ge)
            dve.drain()
            for g, (window, dil) in enumerate(GROUPS):
                if dil > 1:
                    dve.tensor_scalar(low_i[:, :], dist_i[:, :], dil - 1, None, ALU.bitwise_and)
                    dve.drain()
                    dve.tensor_copy(part[:, :], low_i[:, :])
                    dve.drain()
                    dve.tensor_scalar(part[:, :], part[:, :], 0.0, None, ALU.is_equal)
                    dve.drain()
                    dve.scalar_tensor_tensor(part[:, :], dist[:, :], float(window), part[:, :], ALU.is_le, ALU.mult)
                    dve.drain()
                    dve.tensor_tensor(mult[:, :], mult[:, :], part[:, :], ALU.add)
                else:
                    dve.tensor_scalar(mult[:, :], dist[:, :], float(window), None, ALU.is_le)
                dve.drain()
            dve.tensor_tensor(mult[:, :], mult[:, :], past[:, :], ALU.mult)
            dve.drain()
            dve.tensor_scalar(bias[:, :], mult[:, :], 0.0, NEG, ALU.is_equal, ALU.mult)
            dve.drain()

            def step(t):
                p = t.p
                dve.wait_ge(q_turned, t.now)
                dve.wait_ge(scored, t.back1)
                for e in range(2):
                    ins = dve.tensor_copy(
                        qbd[e * AD:(e + 1) * AD, :].rearrange("p (j x) -> p j x", x=80)[:, :, e * 8:e * 8 + 8],
                        pT_ps[e * AD:(e + 1) * AD, 0:4 * DEC_T].rearrange("p (j x) -> p j x", x=DEC_T))
                ins.then_inc(q_taken, 1)
                for k in range(5):
                    dve.wait_ge(k_turned[1], t.of(5, k))
                    dve.tensor_copy(kT[:, :, (2 * k + 1) * P:(2 * k + 2) * P],
                                    t_ps[1][:, :].rearrange("p (j r) -> p j r", j=4)).then_inc(k_taken[1], 1)
                dve.wait_ge(scored, t.now)
                dve.wait_ge(exps_done, t.back1)
                dve.tensor_tensor(sm[:, :], s_ps[0:R, 0:NK], bias[:, :], ALU.add).then_inc(masked, 1)
                dve.drain()
                dve.tensor_reduce(stat[:, 0:1], sm[:, :], AX.X, ALU.max)
                dve.drain()
                dve.tensor_scalar(stat[:, 1:2], stat[:, 0:1], -SCALE, None, ALU.mult).then_inc(max_ready, 1)
                dve.wait_ge(exps_done, t.now)
                dve.scalar_tensor_tensor(pr[:, :], pr[:, :], 1.0, mult[:, :], ALU.mult, ALU.mult,
                                         accum_out=stat[:, 2:3]).then_inc(p_ready, 1)
                dve.drain()
                dve.reciprocal(stat[:, 3:4], stat[:, 2:3])
                dve.wait_ge(p_turned, t.now)
                dve.tensor_copy(pT[:, 0:10, :], pT_ps[:, 0:10 * R].rearrange("p (c r) -> p c r", r=R))
                dve.tensor_copy(pT[0:DEC_T, 10, :], pT_ps[0:DEC_T, 10 * R:11 * R]).then_inc(pT_ready, 1)
                dve.drain()
                dve.wait_ge(o_ready, t.now)
                dve.scalar_tensor_tensor(o_sb[:, :], o_ps[0:R, :], stat[:, 3:4],
                                         diag[:, :, :].rearrange("r h d -> r (h d)"), ALU.mult, ALU.mult
                                         ).then_inc(o_scaled, 1)

            all_steps(dve, DEC_B, step)

        @block.tensor
        def _(pe):
            pe.wait_ge(consts, 1)

            def step(t):
                p = t.p
                pe.wait_ge(new_loaded[p], t.dma)
                pe.wait_ge(pT_ready, t.back1)
                pe.wait_ge(k_loaded[p], t.dma5)
                pe.wait_ge(out_taken, t.back1)
                for c in range(NTL):
                    half, k = c % 2, c // 2
                    if c < 10:
                        pe.wait_ge(k_taken[half], t.of(6 - half, k - 1))
                    if c == 9:
                        pe.wait_ge(k_taken[0], t.of(6, 4))
                    for j in range(4):
                        if c < 10:
                            ins = pe.transpose(t_ps[half][:, j * P:(j + 1) * P], k_sb[:, p, c, j * P:(j + 1) * P],
                                               ident[:, :])
                        else:
                            ins = pe.transpose(t_ps[half][:, j * P:j * P + DEC_T],
                                               new[:, p, AW + j * P:AW + (j + 1) * P], ident[0:DEC_T, 0:DEC_T])
                    ins.then_inc(k_turned[half], 1)
                    if c == 0:
                        for j in range(4):
                            ins = pe.transpose(pT_ps[:, j * DEC_T:(j + 1) * DEC_T], new[:, p, j * P:(j + 1) * P],
                                               ident[0:DEC_T, 0:DEC_T])
                        ins.then_inc(q_turned, 1)
                pe.wait_ge(q_taken, t.now)
                pe.wait_ge(masked, t.back1)
                for lo, hi, a, b in ((0, 512, t.of(6, 1), t.of(5, 1)), (512, 1024, t.of(6, 3), t.of(5, 3)),
                                     (1024, NK, t.of(6, 5), t.of(5, 4))):
                    pe.wait_ge(k_taken[0], a)
                    pe.wait_ge(k_taken[1], b)
                    for j in range(4):
                        ins = pe.matmul(s_ps[0:R, lo:hi], qbd[:, j * R:(j + 1) * R], kT[:, j, lo:hi],
                                        start=(j == 0), stop=(j == 3))
                ins.then_inc(scored, 1)
                pe.wait_ge(consts, 1)
                pe.wait_ge(p_ready, t.now)
                for c in range(10):
                    pe.transpose(pT_ps[:, c * R:(c + 1) * R], pr[:, c * P:(c + 1) * P], ident[0:R, 0:R])
                pe.transpose(pT_ps[0:DEC_T, 10 * R:11 * R], pr[:, CT:NK], ident[0:R, 0:R]).then_inc(p_turned, 1)
                pe.wait_ge(pT_ready, t.now)
                pe.wait_ge(v_loaded[p], t.dma5)
                for c in range(10):
                    pe.matmul(o_ps[0:R, :], pT[:, c, :], v_sb[:, p, c, :], start=(c == 0), stop=False)
                pe.matmul(o_ps[0:R, :], pT[0:DEC_T, 10, :], new[:, p, 2 * AW:3 * AW], start=False, stop=True
                          ).then_inc(o_ready, 1)
                pe.wait_ge(consts, 1)
                pe.wait_ge(o_scaled, t.now)
                pe.matmul(t_ps[1][0:DEC_T, :], pick[:, :], o_sb[:, :], start=True, stop=True).then_inc(out_ready, 1)

            all_steps(pe, DEC_B, step)


def memory_kv(nc, mem, mem_g, w_k, w_v, k_g, new_k, new_v):
    NM = NMEM // P
    with ExitStack() as ctx:
        ph = Phase(nc, ctx, "mk")
        ident = ph.sb("ident", [P, P])
        gc = ph.sb("gc", [P, KD])
        kg = ph.sb("kg", [P, MH, MD])
        w = [ph.sb(f"w{i}", [P, KD, MW]) for i in range(2)]
        x = ph.sb("x", [P, NM, D])
        sq = ph.sb("sq", [P, D])
        tmp = ph.sb("tmp", [P, 2, MH])
        ss = ph.sb("ss", [P, NM, 2])
        xs = ph.sb("xs", [P, NM, D])
        xT = ph.sb("xT", [P, NM, KD, P])
        hs = ph.sb("hs", [P, NM, 2, MH])
        y = ph.sb("y", [P, NM, 2, MW])
        xT_ps = [ph.ps(f"xTps{i}", 1024) for i in range(NM)]
        y_ps = [[ph.ps(f"yps{i}{m}") for i in range(2)] for m in range(NM)]
        loaded, w_loaded, consts, stored = (ph.load(n) for n in ("loaded", "w_loaded", "consts", "stored"))
        x_summed, scaled, turned, xT_ready, projected, squared, summed, k_done, v_done = (
            ph.load(n) for n in ("x_summed", "scaled", "turned", "xT_ready", "projected", "squared", "summed",
                                 "k_done", "v_done"))
        block = ctx.enter_context(nc.Block())

        @block.sync
        def _(sp):
            sp.dma_start(x[:, :, :], mem[0].rearrange("(m p) d -> p m d", p=P)).then_inc(loaded, 16)
            sp.dma_start(gc[:, :], mem_g[0].rearrange("(k p) -> p k", p=P), allow_slow_non_contiguous=True
                         ).then_inc(loaded, 16)
            sp.dma_start(kg[:, :, :], k_g[0].unsqueeze(0).unsqueeze(0).to_broadcast([P, MH, MD])).then_inc(loaded, 16)
            for i, src in enumerate((w_k, w_v)):
                sp.dma_start(w[i][:, :, :], src[0].rearrange("(k p) n -> p k n", p=P)).then_inc(w_loaded, 16)
            for m in range(NM):
                for i, (done, out) in enumerate(((k_done, new_k), (v_done, new_v))):
                    sp.wait_ge(done, m + 1)
                    sp.dma_start(out[0, 0].rearrange("(m p) h d -> m p (h d)", p=P)[m], y[:, m, i, :]
                                 ).then_inc(stored, 16)
            sp.wait_ge(stored, 64)

        @block.gpsimd
        def _(pool):
            make_identity(pool, ident)
            pool.drain()
            pool.sem_inc(consts, 1)

        @block.scalar
        def _(act):
            act.wait_ge(consts, 1)
            act.wait_ge(loaded, 48)
            for m in range(NM):
                act.drain()
                act.activation(sq[:, :], x[:, m, :], ACT.Square, accum_out=ss[:, m, 0:1]).then_inc(x_summed, 1)
            for m in range(NM):
                act.wait_ge(projected, m + 1)
                if m:
                    act.wait_ge(summed, m)
                act.activation(sq[:, 0:MW], y_ps[m][0][:, :], ACT.Square).then_inc(squared, 1)
                act.activation(y[:, m, 1, :], y_ps[m][1][:, :], ACT.Copy).then_inc(v_done, 1)

        @block.vector
        def _(dve):
            for m in range(NM):
                dve.wait_ge(x_summed, m + 1)
                inverse_rms(dve, ss[:, m, 1:2], ss[:, m, 0:1], D, (tmp[:, 0, 0:1], tmp[:, 1, 0:1]))
                dve.drain()
                dve.tensor_scalar(xs[:, m, :], x[:, m, :], ss[:, m, 1:2], None, ALU.mult).then_inc(scaled, 1)
            for m in range(NM):
                dve.wait_ge(turned, m + 1)
                dve.tensor_tensor(xT[:, m, :, :], xT_ps[m][:, :].rearrange("p (k r) -> p k r", r=P),
                                  across(gc[:, :], P), ALU.mult).then_inc(xT_ready, 1)
            for m in range(NM):
                dve.wait_ge(squared, m + 1)
                dve.tensor_reduce(hs[:, m, 0, :], sq[:, 0:MW].rearrange("p (h d) -> p h d", d=MD), AX.X, ALU.add
                                  ).then_inc(summed, 1)
                dve.drain()
                inverse_rms(dve, hs[:, m, 1, :], hs[:, m, 0, :], MD, (tmp[:, 0, :], tmp[:, 1, :]))
                dve.drain()
                k = y[:, m, 0, :].rearrange("p (h d) -> p h d", d=MD)
                dve.tensor_tensor(k, y_ps[m][0][:, :].rearrange("p (h d) -> p h d", d=MD),
                                  across(hs[:, m, 1, :], MD), ALU.mult)
                dve.drain()
                dve.tensor_tensor(k, k, kg[:, :, :], ALU.mult).then_inc(k_done, 1)

        @block.tensor
        def _(pe):
            pe.wait_ge(consts, 1)
            for m in range(NM):
                pe.wait_ge(scaled, m + 1)
                for k in range(KD):
                    ins = pe.transpose(xT_ps[m][:, k * P:(k + 1) * P], xs[:, m, k * P:(k + 1) * P], ident[:, :])
                ins.then_inc(turned, 1)
            pe.wait_ge(w_loaded, 32)
            for m in range(NM):
                pe.wait_ge(xT_ready, m + 1)
                for i in range(2):
                    for k in range(KD):
                        ins = pe.matmul(y_ps[m][i][:, :], xT[:, m, k, :], w[i][:, k, :], start=(k == 0),
                                        stop=(k == KD - 1))
                ins.then_inc(projected, 1)


def mix_attend_route(nc, x_prompt, x_sample, U, OB, OAS, w_out, norm2_g, w_q, q_g, w_o, norm3_g, router_w, router_b,
                     mem_k, mem_v, cache_k, cache_v, H, XN, RT):
    SCALE = MD ** -0.5
    NC = NMEM // P
    with ExitStack() as ctx:
        ph = Phase(nc, ctx, "mx")
        ident = ph.sb("ident", [P, P])
        tmp = ph.sb("tmp", [P, 2, MH])
        wo_sb = ph.sb("wout", [P, KD, D])
        wq_sb = ph.sb("wq", [P, KD, MW])
        wm_sb = ph.sb("wm", [P, MH, D])
        wr_sb = ph.sb("wr", [P, KD, NE])
        g2c, g3c = ph.sb("g2c", [P, KD]), ph.sb("g3c", [P, KD])
        qg = ph.sb("qg", [P, MH, MD])
        rb = ph.sb("rb", [P, NE])
        kv = ph.sb("kv", [P, 2, NC, MW])
        vs = ph.sb("vs", [P, 2, NC, MW])
        kT = ph.sb("kT", [P, MH, NMEM])
        seq = ph.sb("seq", [SAMPLE, DEC_B])
        u = ph.sb("u", [P, 2, 3, UW])
        wt = ph.sb("wt", [P, 8, AH])
        t1 = ph.sb("t1", [P, 2, AW])
        cat = ph.sb("cat", [P, 2, D])
        catT = ph.sb("catT", [P, KD, P])
        x_sb = ph.sb("x", [P, 2, D])
        h = ph.sb("h", [P, 2, D])
        h2 = ph.sb("h2", [P, 2, D])
        sq = ph.sb("sq", [P, D])
        qsq = ph.sb("qsq", [P, MW])
        ss = ph.sb("ss", [P, 4])
        hs = ph.sb("hs", [P, D])
        hT = ph.sb("hT", [P, KD, P])
        qss = ph.sb("qss", [P, 2, MH])
        q = ph.sb("q", [P, 2, MW])
        qT = ph.sb("qT", [P, MH, P])
        sst = ph.sb("sst", [P, 4, MH])
        pr = ph.sb("pr", [P, MH, NMEM])
        pT = ph.sb("pT", [P, MH, NC, P])
        oT = ph.sb("oT", [P, MH, P])
        xn = ph.sb("xn", [P, 2, D])
        xT = ph.sb("xT", [P, KD, P])
        lg = ph.sb("lg", [P, NE])
        top = ph.sb("top", [P, 8])
        tix = ph.sb("tix", [P, 8], U32)
        gt = ph.sb("gt", [P, 8])
        rt = ph.sb("rt", [P, 2, 8])
        zeros = ph.sb("zeros", [P, 512])
        t_ps = [ph.ps(f"tps{i}") for i in range(2)]
        y_ps = ph.ps("yps", 1024)
        s_ps = ph.ps("sps", 1024)
        q_ps = ph.ps("qps")
        m_ps = ph.ps("mps")

        mk_turned, mk_ready = ph.load("mk_turned"), ph.load("mk_ready")
        const_in, w_loaded, consts, mem_in = (ph.load(n) for n in ("const_in", "w_loaded", "consts", "mem_in"))
        in_loaded, b_loaded = ph.loads("in_loaded"), ph.loads("b_loaded")
        rt_stored, h_stored, xn_stored = ph.stores("rt_stored"), ph.stores("h_stored"), ph.stores("xn_stored")
        ev = {n: ph.event(n) for n in (
            "weights", "weights_exp", "cat_ready", "cat_turned", "catT0", "catT1", "y_ready", "h_ready",
            "h_summed", "hs_ready", "h_turned", "hT_ready", "h_kept", "q_ready", "q_squared", "q_summed", 
            "q_scaled", "q_done", "q_turned", "qT_ready", "scored", "max_ready", "exps_done", "p_ready", "p_turned",
            "pT0", "pT1", "o_ready", "oT_ready", "yo_ready", "h2_ready", "h2_summed", "xn_ready", "x_turned",
            "xT_ready", "lg_ready", "lg_taken", "top_ready", "gates_exp", "rt_ready")}
        sq_ev = {n: ph.event("s_" + n) for n in ("k_turned", "kT_ready", "scored", "max_ready", "exps_done",
                                                 "p_ready", "p_turned", "pT_ready", "o_ready")}
        block = ctx.enter_context(nc.Block())

        def steps(eng, step):
            step(at(eng, 0), True, False, False, False)
            step(at(eng, 1), True, True, False, False)
            step(at(eng, 2), True, True, True, False)
            step(at(eng, 3), True, True, True, True)
            with eng.Fori(2, (NT - 1) // 2 - 1) as it:
                pair = Pair(eng, it)
                for k in range(2):
                    step(Turn(pair, k), True, True, True, True)
            for s in range(NT - 3, NT):
                step(at(eng, s), True, True, True, True)
            step(at(eng, NT), False, True, True, True)
            step(at(eng, NT + 1), False, False, True, True)
            step(at(eng, NT + 2), False, False, False, True)

        def is_sample(t):
            return isinstance(t.pair.it, int) and t.t == NT - 1

        @block.sync
        def _(sp):
            ph.grant(sp)
            sp.dma_start(qg[:, :, :], q_g[0].unsqueeze(0).unsqueeze(0).to_broadcast([P, MH, MD])).then_inc(const_in, 16)
            sp.dma_start(rb[:, :], router_b[0].unsqueeze(0).to_broadcast([P, NE])).then_inc(const_in, 16)
            for g, col in ((norm2_g, g2c), (norm3_g, g3c)):
                sp.dma_start(col[:, :], g[0].rearrange("(k p) -> p k", p=P), allow_slow_non_contiguous=True
                             ).then_inc(const_in, 16)

            xr = x_prompt[0].rearrange("(t r) d -> t r d", r=P)
            Ur = [m.rearrange("(t r) w -> t r w", r=P) for m in U]

            def load(t):
                sp.wait_ge(ev["cat_turned"], t.back2)
                for g in range(3):
                    sp.dma_start(u[:, t.p, g, :], Ur[g][t.t]).then_inc(in_loaded[t.p], 16)
                sp.dma_start(cat[:, t.p, AW:D], OB[t.t]).then_inc(in_loaded[t.p], 16)
                sp.wait_ge(ev["h_ready"], t.back2)
                sp.dma_start(x_sb[:, t.p, :], xr[t.t]).then_inc(in_loaded[t.p], 16)

            with sp.Fori(0, (NT - 1) // 2) as it:
                pair = Pair(sp, it)
                for k in range(2):
                    load(Turn(pair, k))
            t = at(sp, NT - 1)
            sp.wait_ge(ev["cat_turned"], t.back2)
            sp.wait_ge(ev["h_ready"], t.back2)
            sp.dma_start(cat[0:SAMPLE, 0, 0:AW], OAS).then_inc(in_loaded[0], 16)
            sp.dma_start(cat[0:SAMPLE, 0, AW:D], OB[NT - 1][0:SAMPLE]).then_inc(in_loaded[0], 16)
            sp.dma_start(x_sb[0:SAMPLE, 0, :], x_sample.rearrange("b t d -> (b t) d")).then_inc(in_loaded[0], 16)
            sp.wait_ge(ev["o_ready"], at(sp, NT - 2).now)
            with sp.Fori(0, DEC_B // 2) as it:
                pair = Pair(sp, it)
                for k in range(2):
                    b = Turn(pair, k)
                    sp.wait_ge(sq_ev["o_ready"], b.back2)
                    for src, dst in ((cache_k, kv), (cache_v, vs)):
                        sp.dma_start(dst[:, b.p, :, :], src[0][b.t].rearrange("(c p) h d -> p c (h d)", p=P)
                                     ).then_inc(b_loaded[b.p], 16)

        @block.gpsimd
        def _(pool):
            make_identity(pool, ident)
            pool.memset(seq[:, :], 1.0)
            pool.memset(zeros[:, :], 0.0)
            pool.drain()
            for b0, b1, m in ((0, -DEC_T, 1), (DEC_T - 1, DEC_T, -1)):
                pool.affine_select(out=seq[:, :], in_=seq[:, :], compare_op=ALU.is_ge, fill=0.0, base=b0,
                                   pattern=[[b1, DEC_B]], channel_multiplier=m)
                pool.drain()
            pool.sem_inc(consts, 1)
            pool.wait_ge(const_in, 4 * 16)

            def step(s, a, b, c, d):
                if b:
                    t = s.prev
                    pool.wait_ge(h_stored[t.p], t.dma)
                    pool.wait_ge(ev["xn_ready"], t.back2)
                    pool.wait_ge(ev["h_ready"], t.now)
                    pool.wait_ge(ev["q_scaled"], t.now)
                    pool.tensor_tensor(q[:, t.p, :], q[:, t.p, :], qg[:, :, :].rearrange("p h d -> p (h d)"),
                                       ALU.mult).then_inc(ev["q_done"], 1)
                    pool.tensor_copy(h2[:, t.p, :], h[:, t.p, :]).then_inc(ev["h_kept"], 1)

            steps(pool, step)

        @block.scalar
        def _(act):
            for src, dst in ((w_out, wo_sb), (w_q, wq_sb), (w_o, wm_sb), (router_w, wr_sb)):
                act.dma_start(dst[:, :, :], src[0].rearrange("(k p) n -> p k n", p=P)).then_inc(w_loaded, 16)
            for i, src in enumerate((mem_k, mem_v)):
                act.dma_start(kv[:, i, :, :], src[0, 0].rearrange("(c p) h d -> p c (h d)", p=P)).then_inc(mem_in, 16)
            act.wait_ge(consts, 1)

            act.wait_ge(mk_turned, 1)
            for j in range(2):
                ins = act.activation(kT[:, 2 * j:2 * j + 2, :], t_ps[j][:, :].rearrange("p (h k) -> p h k", h=2),
                                     ACT.Copy)
            ins.then_inc(mk_ready, 1)

            def exps(rows, ready, value):
                act.wait_ge(ready, value)
                for j in range(MH):
                    ins = act.activation(pr[0:rows, j, :], s_ps[0:rows, j * NMEM:(j + 1) * NMEM], ACT.Exp,
                                         bias=sst[0:rows, 1, j:j + 1], scale=SCALE, accum_out=sst[0:rows, 2, j:j + 1])
                return ins

            def step(s, a, b, c, d):
                if a:
                    act.wait_ge(ev["cat_turned"], s.now)
                    act.wait_ge(ev["y_ready"], s.back1)
                    act.activation(catT[:, 0:4, :], t_ps[0][:, :].rearrange("p (k r) -> p k r", r=P), ACT.Copy
                                   ).then_inc(ev["catT0"], 1)
                if d:
                    r = s.prev.prev.prev
                    act.drain()
                    act.wait_ge(ev["h2_ready"], r.now)
                    act.wait_ge(ev["xn_ready"], r.back1)
                    act.activation(sq[:, :], h2[:, r.p, :], ACT.Square, accum_out=ss[:, 2:3]
                                   ).then_inc(ev["h2_summed"], 1)
                    act.dma_start(H[r.t], h2[:, r.p, :]).then_inc(h_stored[r.p], 16)
                if c:
                    t = s.prev.prev
                    act.wait_ge(ev["q_turned"], t.now)
                    act.wait_ge(ev["scored"], t.back1)
                    act.activation(qT[:, :, :], m_ps[:, :].rearrange("p (k r) -> p k r", r=P), ACT.Copy
                                   ).then_inc(ev["qT_ready"], 1)
                if a and not is_sample(s) and not is_sample(s.next):
                    weigh(s.next)
                if d:
                    act.wait_ge(ev["xn_ready"], r.now)
                    act.dma_start(XN[r.t], xn[:, r.p, :]).then_inc(xn_stored[r.p], 16)
                if a:
                    act.drain()
                    act.wait_ge(ev["h_ready"], s.now)
                    act.wait_ge(ev["hs_ready"], s.back1)
                    act.activation(sq[:, :], h[:, s.p, :], ACT.Square, accum_out=ss[:, 0:1]
                                   ).then_inc(ev["h_summed"], 1)
                if c:
                    if is_sample(t):

                        def sequence(b):
                            act.wait_ge(sq_ev["k_turned"], b.now)
                            act.wait_ge(sq_ev["scored"], b.back1)
                            act.activation(kT[:, 0:2, :], t_ps[0][:, :].rearrange("p (h k) -> p h k", h=2), ACT.Copy)
                            act.activation(kT[:, 2:4, :], t_ps[1][:, :].rearrange("p (h k) -> p h k", h=2), ACT.Copy
                                           ).then_inc(sq_ev["kT_ready"], 1)
                            act.wait_ge(sq_ev["p_turned"], b.back1)
                            exps(SAMPLE, sq_ev["max_ready"], b.now).then_inc(sq_ev["exps_done"], 1)

                        all_steps(act, DEC_B, sequence)
                    else:
                        act.wait_ge(ev["p_turned"], t.back1)
                        exps(P, ev["max_ready"], t.now).then_inc(ev["exps_done"], 1)
                if b:
                    act.wait_ge(ev["q_ready"], s.prev.now)
                    act.wait_ge(ev["q_summed"], s.prev.back1)
                    act.activation(qsq[:, :], q_ps[:, :], ACT.Square).then_inc(ev["q_squared"], 1)
                if c:
                    if not is_sample(t):
                        act.wait_ge(ev["p_turned"], t.now)
                        act.wait_ge(ev["o_ready"], t.back1)
                        act.activation(pT[:, 0:2, :, :], t_ps[0][:, :].rearrange("p (h c r) -> p h c r", h=2, c=NC),
                                       ACT.Copy).then_inc(ev["pT0"], 1)
                    act.wait_ge(ev["o_ready"], t.now)
                    act.wait_ge(ev["yo_ready"], t.back1)
                    act.activation(oT[:, :, :], m_ps[:, :].rearrange("p (k r) -> p k r", r=P), ACT.Copy
                                   ).then_inc(ev["oT_ready"], 1)
                if d:
                    act.wait_ge(ev["top_ready"], r.now)
                    act.activation(gt[:, 0:4], top[:, 0:4], ACT.Exp, bias=gt[:, 4:5], accum_out=gt[:, 5:6]
                                   ).then_inc(ev["gates_exp"], 1)
                    act.wait_ge(ev["rt_ready"], r.now)
                    act.dma_start(RT[r.t], rt[:, r.p, :]).then_inc(rt_stored[r.p], 16)

            def weigh(t):
                act.wait_ge(ev["weights"], t.now)
                act.activation(wt[:, 1:4, :], wt[:, 1:4, :], ACT.Exp).then_inc(ev["weights_exp"], 1)

            weigh(at(act, 0))
            steps(act, step)
            for p, n in enumerate(((NT + 1) // 2, NT // 2)):
                for s in (rt_stored[p], h_stored[p], xn_stored[p]):
                    act.wait_ge(s, 16 * n + 16)

        @block.vector
        def _(dve):
            dve.wait_ge(consts, 1)
            dve.wait_ge(const_in, 4 * 16)

            def combine(t):
                if is_sample(t):
                    dve.wait_ge(in_loaded[0], 80 * (NT // 2) + 48)
                    dve.sem_inc(ev["cat_ready"], 1)
                    return
                p = t.p
                dve.wait_ge(in_loaded[p], t.dma5)
                dve.wait_ge(ev["weights_exp"], t.back1)
                nm = [u[:, p, g, AW:AW + AH] for g in range(3)]
                sums = [u[:, p, g, AW + AH:UW] for g in range(3)]
                dve.tensor_tensor(wt[:, 0, :], nm[0], nm[1], ALU.min)
                dve.drain()
                dve.tensor_tensor(wt[:, 0, :], wt[:, 0, :], nm[2], ALU.min)
                dve.drain()
                for g in range(3):
                    ins = dve.tensor_tensor(wt[:, 1 + g, :], wt[:, 0, :], nm[g], ALU.subtract)
                ins.then_inc(ev["weights"], 1)
                dve.wait_ge(ev["weights_exp"], t.now)
                for g in range(3):
                    dve.tensor_tensor(wt[:, 4 + g, :], wt[:, 1 + g, :], sums[g], ALU.mult)
                dve.drain()
                dve.tensor_tensor(wt[:, 4, :], wt[:, 4, :], wt[:, 5, :], ALU.add)
                dve.drain()
                dve.tensor_tensor(wt[:, 4, :], wt[:, 4, :], wt[:, 6, :], ALU.add)
                dve.drain()
                dve.reciprocal(wt[:, 7, :], wt[:, 4, :])
                dve.drain()
                dve.tensor_tensor(wt[:, 1:4, :], wt[:, 1:4, :],
                                  wt[:, 7, :].unsqueeze(1).to_broadcast([P, 3, AH]), ALU.mult)
                dve.drain()
                dve.wait_ge(ev["cat_turned"], t.back2)

                def weighted(out, g):
                    return dve.tensor_tensor(out.rearrange("p (h d) -> p h d", d=AD),
                                             u[:, p, g, 0:AW].rearrange("p (h d) -> p h d", d=AD),
                                             across(wt[:, 1 + g, :], AD), ALU.mult)

                weighted(t1[:, 0, :], 0)
                weighted(t1[:, 1, :], 1)
                dve.drain()
                dve.tensor_tensor(cat[:, p, 0:AW], t1[:, 0, :], t1[:, 1, :], ALU.add)
                dve.drain()
                weighted(t1[:, 0, :], 2)
                dve.drain()
                dve.tensor_tensor(cat[:, p, 0:AW], cat[:, p, 0:AW], t1[:, 0, :], ALU.add).then_inc(ev["cat_ready"], 1)

            def maxima(rows, scored, value, free, freed):
                dve.wait_ge(scored, value)
                dve.wait_ge(free, freed)
                dve.tensor_reduce(sst[0:rows, 0, :], s_ps[0:rows, :].rearrange("p (h k) -> p h k", h=MH), AX.X, ALU.max)
                dve.drain()
                return dve.tensor_scalar(sst[0:rows, 1, :], sst[0:rows, 0, :], -SCALE, None, ALU.mult)

            def turned_gain(dst, gain, turned, value, free, freed):
                dve.wait_ge(turned, value)
                dve.wait_ge(free, freed)
                for j in range(2):
                    ins = dve.tensor_tensor(dst[:, 4 * j:4 * j + 4, :], t_ps[j][:, :].rearrange("p (k r) -> p k r", r=P),
                                            across(gain[:, 4 * j:4 * j + 4], P), ALU.mult)
                return ins

            def sequence(b):
                n = SAMPLE
                maxima(n, sq_ev["scored"], b.now, sq_ev["p_ready"], b.back1).then_inc(sq_ev["max_ready"], 1)
                dve.wait_ge(sq_ev["exps_done"], b.now)
                dve.reciprocal(sst[0:n, 3, :], sst[0:n, 2, :])
                dve.drain()
                dve.tensor_tensor(sst[0:n, 3, :], sst[0:n, 3, :],
                                  seq[:, bass.ds(b.t, 1)].to_broadcast([n, MH]), ALU.mult)
                dve.drain()
                dve.tensor_tensor(pr[0:n, :, :], pr[0:n, :, :], across(sst[0:n, 3, :], NMEM), ALU.mult
                                  ).then_inc(sq_ev["p_ready"], 1)
                dve.wait_ge(sq_ev["p_turned"], b.now)
                dve.wait_ge(sq_ev["o_ready"], b.back1)
                for j in range(2):
                    ins = dve.tensor_copy(pT[:, 2 * j:2 * j + 2, :, 0:n],
                                          t_ps[j][:, :].rearrange("p (h c r) -> p h c r", h=2, c=NC)[:, :, :, 0:n])
                ins.then_inc(sq_ev["pT_ready"], 1)

            def step(s, a, b, c, d):
                if d:
                    r = s.prev.prev.prev
                    dve.wait_ge(ev["yo_ready"], r.now)
                    dve.wait_ge(ev["h_kept"], r.now)
                    dve.tensor_tensor(h2[:, r.p, :], y_ps[:, :], h2[:, r.p, :], ALU.add).then_inc(ev["h2_ready"], 1)
                if a:
                    dve.wait_ge(ev["cat_turned"], s.now)
                    dve.wait_ge(ev["y_ready"], s.back1)
                    dve.tensor_copy(catT[:, 4:8, :], t_ps[1][:, :].rearrange("p (k r) -> p k r", r=P)
                                    ).then_inc(ev["catT1"], 1)
                if d:
                    dve.wait_ge(ev["h2_summed"], r.now)
                    inverse_rms(dve, ss[:, 3:4], ss[:, 2:3], D, (tmp[:, 0, 0:1], tmp[:, 1, 0:1]))
                    dve.drain()
                    dve.wait_ge(ev["x_turned"], r.back2)
                    dve.wait_ge(xn_stored[r.p], r.dma)
                    dve.tensor_scalar(xn[:, r.p, :], h2[:, r.p, :], ss[:, 3:4], None, ALU.mult
                                      ).then_inc(ev["xn_ready"], 1)
                if b:
                    t = s.prev
                    dve.wait_ge(ev["h_summed"], t.now)
                    inverse_rms(dve, ss[:, 1:2], ss[:, 0:1], D, (tmp[:, 0, 1:2], tmp[:, 1, 1:2]))
                    dve.drain()
                    dve.wait_ge(ev["h_turned"], t.back1)
                    dve.tensor_scalar(hs[:, :], h[:, t.p, :], ss[:, 1:2], None, ALU.mult).then_inc(ev["hs_ready"], 1)
                if a and not is_sample(s):
                    combine(s.next)
                if d:
                    turned_gain(xT, g3c, ev["x_turned"], r.now, ev["lg_ready"], r.back1).then_inc(ev["xT_ready"], 1)
                if a:
                    dve.wait_ge(ev["y_ready"], s.now)
                    dve.wait_ge(ev["hs_ready"], s.back2)
                    dve.wait_ge(ev["h_kept"], s.back2)
                    dve.tensor_tensor(h[:, s.p, :], y_ps[:, :], x_sb[:, s.p, :], ALU.add).then_inc(ev["h_ready"], 1)
                if c and not is_sample(s.prev.prev):
                    t = s.prev.prev
                    maxima(P, ev["scored"], t.now, ev["p_ready"], t.back1).then_inc(ev["max_ready"], 1)
                if b:
                    t = s.prev
                    turned_gain(hT, g2c, ev["h_turned"], t.now, ev["q_ready"], t.back1).then_inc(ev["hT_ready"], 1)
                if d:
                    dve.wait_ge(ev["gates_exp"], r.back1)
                    dve.wait_ge(ev["lg_ready"], r.now)
                    dve.tensor_tensor(lg[:, :], m_ps[:, 0:NE], rb[:, :], ALU.add).then_inc(ev["lg_taken"], 1)
                    dve.drain()
                    dve.max(top[:, :], lg[:, :])
                    dve.drain()
                    dve.max_index(tix[:, :], top[:, :], lg[:, :])
                    dve.tensor_scalar(gt[:, 4:5], top[:, 0:1], -1.0, None, ALU.mult).then_inc(ev["top_ready"], 1)
                if c:
                    t = s.prev.prev
                    if is_sample(t):
                        all_steps(dve, DEC_B, sequence)
                    else:
                        dve.wait_ge(ev["exps_done"], t.now)
                        dve.reciprocal(sst[:, 3, :], sst[:, 2, :])
                        dve.drain()
                        dve.tensor_tensor(pr[:, :, :], pr[:, :, :], across(sst[:, 3, :], NMEM), ALU.mult
                                          ).then_inc(ev["p_ready"], 1)
                        dve.wait_ge(ev["p_turned"], t.now)
                        dve.wait_ge(ev["o_ready"], t.back1)
                        dve.tensor_copy(pT[:, 2:4, :, :], t_ps[1][:, :].rearrange("p (h c r) -> p h c r", h=2, c=NC)
                                        ).then_inc(ev["pT1"], 1)
                if b:
                    t = s.prev
                    dve.wait_ge(ev["q_squared"], t.now)
                    dve.tensor_reduce(qss[:, 0, :], qsq[:, :].rearrange("p (h d) -> p h d", d=MD), AX.X, ALU.add
                                      ).then_inc(ev["q_summed"], 1)
                    dve.drain()
                    inverse_rms(dve, qss[:, 1, :], qss[:, 0, :], MD, (tmp[:, 0, :], tmp[:, 1, :]))
                    dve.drain()
                    dve.wait_ge(ev["q_turned"], t.back2)
                    dve.tensor_tensor(q[:, t.p, :].rearrange("p (h d) -> p h d", d=MD),
                                      q_ps[:, :].rearrange("p (h d) -> p h d", d=MD), across(qss[:, 1, :], MD),
                                      ALU.mult).then_inc(ev["q_scaled"], 1)
                if d:
                    dve.drain()
                    dve.wait_ge(rt_stored[r.p], r.dma)
                    dve.tensor_copy(rt[:, r.p, 4:8], tix[:, 0:4])
                    dve.wait_ge(ev["gates_exp"], r.now)
                    dve.reciprocal(gt[:, 6:7], gt[:, 5:6])
                    dve.drain()
                    dve.tensor_scalar(rt[:, r.p, 0:4], gt[:, 0:4], gt[:, 6:7], None, ALU.mult
                                      ).then_inc(ev["rt_ready"], 1)

            combine(at(dve, 0))
            steps(dve, step)

        @block.tensor
        def _(pe):
            pe.wait_ge(consts, 1)
            pe.wait_ge(mem_in, 32)
            pe.wait_ge(w_loaded, 64)

            def turn8(src):
                for k in range(KD):
                    ins = pe.transpose(t_ps[k // 4][:, k % 4 * P:(k % 4 + 1) * P], src[:, k * P:(k + 1) * P],
                                       ident[:, :])
                return ins

            def turn_k(half):
                for j in range(MH):
                    for c in range(NC):
                        ins = pe.transpose(t_ps[j // 2][:, (j % 2) * NMEM + c * P:(j % 2) * NMEM + (c + 1) * P],
                                           kv[:, half, c, j * MD:(j + 1) * MD], ident[:, :])
                return ins

            def scores(rows):
                for j in range(MH):
                    ins = pe.matmul(s_ps[0:rows, j * NMEM:(j + 1) * NMEM], qT[:, j, 0:rows], kT[:, j, :],
                                    start=True, stop=True)
                return ins

            def turn_p(rows):
                for j in range(MH):
                    for c in range(NC):
                        a = (j % 2) * NMEM + c * P
                        ins = pe.transpose(t_ps[j // 2][:, a:a + rows], pr[0:rows, j, c * P:(c + 1) * P],
                                           ident[0:rows, 0:rows])
                return ins

            def project(out, lhs, w, n):
                for c in range(2):
                    for k in range(n):
                        ins = pe.matmul(out[:, c * 512:(c + 1) * 512], lhs[:, k, :], w[:, k, c * 512:(c + 1) * 512],
                                        start=(k == 0), stop=(k == n - 1))
                return ins

            def sequence(b):
                pe.wait_ge(b_loaded[b.p], b.dma2)
                pe.wait_ge(sq_ev["pT_ready"], b.back1)
                turn_k(b.p).then_inc(sq_ev["k_turned"], 1)
                pe.wait_ge(sq_ev["kT_ready"], b.now)
                pe.wait_ge(sq_ev["exps_done"], b.back1)
                scores(SAMPLE).then_inc(sq_ev["scored"], 1)
                pe.wait_ge(consts, 1)
                pe.wait_ge(sq_ev["p_ready"], b.now)
                turn_p(SAMPLE).then_inc(sq_ev["p_turned"], 1)
                pe.wait_ge(sq_ev["pT_ready"], b.now)
                for j in range(MH):
                    for c in range(NC):
                        ins = pe.matmul(m_ps[:, j * P:j * P + SAMPLE], vs[:, b.p, c, j * MD:(j + 1) * MD],
                                        pT[:, j, c, 0:SAMPLE], start=False, stop=True, skip_group_check=True)
                ins.then_inc(sq_ev["o_ready"], 1)

            turn_k(0).then_inc(mk_turned, 1)
            pe.wait_ge(mk_ready, 1)

            def step(s, a, b, c, d):
                t, r = s.prev.prev, s.prev.prev.prev
                if a:
                    pe.wait_ge(ev["cat_ready"], s.now)
                    turn8(cat[:, s.p, :]).then_inc(ev["cat_turned"], 1)
                if c:
                    pe.wait_ge(ev["q_done"], t.now)
                    pe.wait_ge(ev["oT_ready"], t.back1)
                    for j in range(MH):
                        ins = pe.transpose(m_ps[:, j * P:(j + 1) * P], q[:, t.p, j * MD:(j + 1) * MD], ident[:, :])
                    ins.then_inc(ev["q_turned"], 1)
                if a:
                    pe.wait_ge(ev["catT0"], s.now)
                    pe.wait_ge(ev["catT1"], s.now)
                    pe.wait_ge(ev["h_ready"], s.back1)
                    if d:
                        pe.wait_ge(ev["h2_ready"], r.now)
                    project(y_ps, catT, wo_sb, KD).then_inc(ev["y_ready"], 1)
                if d:
                    pe.wait_ge(ev["xn_ready"], r.now)
                    turn8(xn[:, r.p, :]).then_inc(ev["x_turned"], 1)
                if c:
                    pe.wait_ge(ev["qT_ready"], t.now)
                    if not is_sample(t):
                        pe.wait_ge(ev["exps_done"], t.back1)
                        scores(P).then_inc(ev["scored"], 1)
                if b:
                    if d:
                        pe.wait_ge(ev["xT_ready"], r.now)
                    pe.wait_ge(ev["hs_ready"], s.prev.now)
                    turn8(hs).then_inc(ev["h_turned"], 1)
                if d:
                    pe.wait_ge(ev["xT_ready"], r.now)
                    pe.wait_ge(ev["oT_ready"], r.now)
                    for k in range(KD):
                        ins = pe.matmul(m_ps[:, 0:NE], xT[:, k, :], wr_sb[:, k, :], start=(k == 0), stop=(k == KD - 1))
                    ins.then_inc(ev["lg_ready"], 1)
                if b:
                    pe.wait_ge(ev["hT_ready"], s.prev.now)
                    pe.wait_ge(ev["q_scaled"], s.prev.back1)
                    for k in range(KD):
                        ins = pe.matmul(q_ps[:, :], hT[:, k, :], wq_sb[:, k, :], start=(k == 0), stop=(k == KD - 1))
                    ins.then_inc(ev["q_ready"], 1)
                if c:
                    if not is_sample(t):
                        pe.wait_ge(ev["p_ready"], t.now)
                        turn_p(P).then_inc(ev["p_turned"], 1)
                        pe.wait_ge(ev["pT0"], t.now)
                        pe.wait_ge(ev["pT1"], t.now)
                        pe.wait_ge(ev["lg_taken"], t.back1)
                        for j in range(MH):
                            for c_ in range(NC):
                                ins = pe.matmul(m_ps[:, j * P:(j + 1) * P], kv[:, 1, c_, j * MD:(j + 1) * MD],
                                                pT[:, j, c_, :], start=(c_ == 0), stop=(c_ == NC - 1))
                        ins.then_inc(ev["o_ready"], 1)
                    else:
                        pe.wait_ge(ev["lg_taken"], t.back1)
                        pe.matmul(m_ps[:, :], zeros[:, 0:P], zeros[:, :], start=True, stop=True, skip_group_check=True)
                        all_steps(pe, DEC_B, sequence)
                        pe.wait_ge(sq_ev["o_ready"], at(pe, DEC_B - 1).now)
                        pe.sem_inc(ev["o_ready"], 1)
                    pe.wait_ge(ev["oT_ready"], t.now)
                    pe.wait_ge(ev["h2_ready"], t.back1)
                    if a:
                        pe.wait_ge(ev["h_ready"], s.now)
                    project(y_ps, oT, wm_sb, MH).then_inc(ev["yo_ready"], 1)

            steps(pe, step)


def slots(nc, RT, TBL, SL, TE):
    NK = NT * TOPK
    N3 = NT * NE // 3
    with ExitStack() as ctx:
        ph = Phase(nc, ctx, "sl")
        rt = ph.sb("rt", [P, NT, 8])
        before = ph.sb("before", [P, P])
        ones = ph.sb("ones", [P, P])
        ie = ph.sb("ie", [P, NE])
        it_ = ph.sb("it", [1, NTL])
        hot = ph.sb("hot", [P, NK, NE])
        hit = ph.sb("hit", [P, NT, NE])
        pos = ph.sb("pos", [P, NT, NE])
        cnt = ph.sb("cnt", [P, NT, NE])
        base = ph.sb("base", [P, NT + 1, NE])
        n_f, n_i, end, first = (ph.sb("n_f", [P, NE]), ph.sb("n_i", [P, NE], I32), ph.sb("end", [P, NE]),
                                ph.sb("first", [P, NE]))
        sl_f = ph.sb("sl_f", [P, NK])
        sl_i = ph.sb("sl_i", [P, NK], I32)
        low, high, low_f, high_f = (ph.sb("low", [P, NK], I32), ph.sb("high", [P, NK], I32),
                                    ph.sb("low_f", [P, NK]), ph.sb("high_f", [P, NK]))
        cell = ph.sb("cell", [P, NK], I32)
        ends = ph.sb("ends", [1, NTL, NE])
        te_f = ph.sb("te_f", [1, 2, NTL])
        te_i = ph.sb("te_i", [1, 2, NTL], I32)
        tok = ph.sb("tok", [P, NT], I32)
        zero = ph.sb("zero", [P, NTL], I32)
        st_cell = ph.sb("st_cell", [P, 2, TOPK], I32)
        st_tok = ph.sb("st_tok", [P, 2], I32)
        r_ps = [ph.ps(f"rps{i}") for i in range(3)]
        c_ps = [ph.ps(f"cps{i}") for i in range(3)]
        loaded, consts, hits, ranked, zeroed, stored, ready, tiles_ready = (ph.load(n) for n in (
            "loaded", "consts", "hits", "ranked", "zeroed", "stored", "ready", "tiles_ready"))
        scattered = [ph.load(f"scattered{i}") for i in range(2)]
        cells_ready = ph.load("cells_ready")
        free = ph.event("free")
        block = ctx.enter_context(nc.Block())

        @block.sync
        def _(sp):
            ph.grant(sp)
            sp.dma_start(rt[:, :, :], RT.rearrange("t p c -> p t c")).then_inc(loaded, 16)
            sp.wait_ge(consts, 1)
            sp.dma_start(TBL, zero[:, :]).then_inc(zeroed, 16)
            sp.wait_ge(ready, 1)
            sp.dma_start(SL, sl_i[:, :]).then_inc(stored, 16)
            sp.wait_ge(tiles_ready, 1)
            sp.dma_start(TE.unsqueeze(0), te_i[:, :, :]).then_inc(stored, 16)
            sp.wait_ge(stored, 32)

        @block.gpsimd
        def _(pool):
            pool.memset(ones[:, :], 1.0)
            pool.memset(before[:, :], 1.0)
            pool.memset(zero[:, :], 0)
            pool.iota(ie[:, :], [[1, NE]], base=0, channel_multiplier=0, allow_small_or_imprecise_dtypes=True)
            pool.iota(it_[:, :], [[1, NTL]], base=0, channel_multiplier=0, allow_small_or_imprecise_dtypes=True)
            pool.iota(tok[:, :], [[P, NT]], base=0, channel_multiplier=1)
            pool.drain()
            pool.affine_select(out=before[:, :], in_=before[:, :], compare_op=ALU.is_gt, fill=0.0, base=0,
                               pattern=[[1, P]], channel_multiplier=-1)
            pool.drain()
            pool.sem_inc(consts, 1)
            pool.wait_ge(zeroed, 16)
            pool.wait_ge(cells_ready, 1)

            def scatter(t, last=False):
                n = SAMPLE if last else P
                pool.wait_ge(free, t.back2)
                pool.tensor_copy(st_cell[:, t.p, :], cell[:, bass.ds(t.t * TOPK, TOPK)])
                pool.tensor_copy(st_tok[:, t.p:t.p + 1], tok[:, bass.ds(t.t, 1)])
                pool.drain()
                for k in range(TOPK):
                    pool.indirect_dma_start(
                        out=TBL.rearrange("p i -> (p i)").unsqueeze(1),
                        out_offset=bass.IndirectOffsetOnAxis(ap=st_cell[0:n, t.p, k:k + 1], axis=0),
                        in_=st_tok[0:n, t.p:t.p + 1], in_offset=None).then_inc(scattered[t.p], 16)
                pool.wait_ge(scattered[t.p], t.dma4)
                pool.sem_inc(free, 1)

            all_steps(pool, NT, scatter, lambda t: scatter(t, True))

        @block.vector
        def _(dve):
            dve.wait_ge(consts, 1)
            dve.wait_ge(loaded, 16)
            for k in range(TOPK):
                dve.tensor_tensor(hot[:, k:NK:TOPK, :], rt[:, :, 4 + k:5 + k].to_broadcast([P, NT, NE]),
                                  ie[:, :].unsqueeze(1).to_broadcast([P, NT, NE]), ALU.is_equal)
            dve.drain()
            dve.memset(hot[SAMPLE:P, NK - TOPK:NK, :], 0.0)
            dve.drain()
            dve.tensor_reduce(hit[:, :, :], hot[:, :, :].rearrange("p (t k) e -> p t e k", k=TOPK), AX.X, ALU.add
                              ).then_inc(hits, 1)
            dve.memset(base[:, 0, :], 0.0)
            dve.wait_ge(ranked, 1)
            cf = cnt[:, :, :].rearrange("p t e -> p (t e)")
            pf = pos[:, :, :].rearrange("p t e -> p (t e)")
            for i in range(3):
                dve.tensor_copy(cf[:, i * N3:(i + 1) * N3], c_ps[i][:, 0:N3])
                dve.tensor_copy(pf[:, i * N3:(i + 1) * N3], r_ps[i][:, 0:N3])
            dve.drain()
            with dve.Fori(0, NT) as t:
                dve.tensor_tensor(base[:, bass.ds(t + 1, 1), :], base[:, bass.ds(t, 1), :],
                                  cnt[:, bass.ds(t, 1), :], ALU.add)
                dve.drain()
            dve.tensor_scalar(n_f[:, :], base[:, NT, :], float(P - 1), None, ALU.add)
            dve.drain()
            dve.tensor_copy(n_i[:, :], n_f[:, :])
            dve.drain()
            dve.tensor_scalar(n_i[:, :], n_i[:, :], 7, None, ALU.logical_shift_right)
            dve.drain()
            dve.tensor_copy(n_f[:, :], n_i[:, :])
            dve.drain()
            dve.tensor_tensor_scan(end[:, :], ones[:, 0:NE], n_f[:, :], 0.0, ALU.mult, ALU.add)
            dve.drain()
            dve.tensor_tensor(first[:, :], end[:, :], n_f[:, :], ALU.subtract)
            dve.drain()
            dve.tensor_scalar(first[:, :], first[:, :], float(P), None, ALU.mult)
            dve.tensor_tensor(pos[:, :, :], pos[:, :, :], base[:, 0:NT, :], ALU.add)
            dve.drain()
            dve.tensor_tensor(pos[:, :, :], pos[:, :, :], first[:, :].unsqueeze(1).to_broadcast([P, NT, NE]), ALU.add)
            dve.drain()
            for k in range(TOPK):
                dve.tensor_tensor(hot[:, k:NK:TOPK, :], hot[:, k:NK:TOPK, :], pos[:, :, :], ALU.mult)
            dve.drain()
            dve.tensor_reduce(sl_f[:, :], hot[:, :, :], AX.X, ALU.add)
            dve.drain()
            dve.tensor_copy(sl_i[:, :], sl_f[:, :]).then_inc(ready, 1)
            dve.drain()
            dve.tensor_scalar(low[:, :], sl_i[:, :], P - 1, None, ALU.bitwise_and)
            dve.tensor_scalar(high[:, :], sl_i[:, :], 7, None, ALU.logical_shift_right)
            dve.drain()
            dve.tensor_copy(low_f[:, :], low[:, :])
            dve.tensor_copy(high_f[:, :], high[:, :])
            dve.drain()
            dve.scalar_tensor_tensor(low_f[:, :], low_f[:, :], float(NTL), high_f[:, :], ALU.mult, ALU.add)
            dve.drain()
            dve.tensor_copy(cell[:, :], low_f[:, :]).then_inc(cells_ready, 1)
            dve.tensor_tensor(ends[:, :, :], it_[:, :].unsqueeze(2).to_broadcast([1, NTL, NE]),
                              end[0:1, :].unsqueeze(1).to_broadcast([1, NTL, NE]), ALU.is_ge)
            dve.drain()
            dve.tensor_reduce(te_f[:, 0, :], ends[:, :, :], AX.X, ALU.add)
            dve.drain()
            dve.tensor_scalar(te_f[:, 0, :], te_f[:, 0, :], float(NE - 1), None, ALU.min)
            dve.memset(te_f[:, 1, :], 1.0)
            dve.drain()
            dve.tensor_tensor(te_f[:, 1, 1:NTL], te_f[:, 0, 1:NTL], te_f[:, 0, 0:NTL - 1], ALU.not_equal)
            dve.drain()
            dve.tensor_copy(te_i[:, :, :], te_f[:, :, :]).then_inc(tiles_ready, 1)

        @block.tensor
        def _(pe):
            pe.wait_ge(hits, 1)
            hf = hit[:, :, :].rearrange("p t e -> p (t e)")
            for i in range(3):
                pe.matmul(r_ps[i][:, 0:N3], before[:, :], hf[:, i * N3:(i + 1) * N3], start=True, stop=True)
                ins = pe.matmul(c_ps[i][:, 0:N3], ones[:, :], hf[:, i * N3:(i + 1) * N3], start=True, stop=True)
            ins.then_inc(ranked, 1)


def experts(nc, XN, norm3_g, TBL, TE, w1, b1, w2, b2, YS):
    with ExitStack() as ctx:
        ph = Phase(nc, ctx, "ex")
        ident = ph.sb("ident", [P, P])
        gc = ph.sb("gc", [P, KD])
        tbl = ph.sb("tbl", [P, NTL], I32)
        te = ph.sb("te", [1, 2, NTL], I32)
        idx = ph.sb("idx", [P, 2], I32)
        w1_sb = ph.sb("w1", [P, KD, 2 * FF])
        w2_sb = ph.sb("w2", [P, KD, D])
        b1_sb = ph.sb("b1", [P, 2 * FF])
        b2_sb = ph.sb("b2", [P, D])
        xg = ph.sb("xg", [P, 2, D])
        xT = ph.sb("xT", [P, 2, KD, P])
        hb = ph.sb("hb", [P, 2 * FF])
        glu, sig, lin = ph.sb("glu", [P, FF]), ph.sb("sig", [P, FF]), ph.sb("lin", [P, FF])
        aT = ph.sb("aT", [P, KD, P])
        y = ph.sb("y", [P, 2, D])
        h_ps = [ph.ps(f"hps{i}") for i in range(4)]
        t_ps = [ph.ps(f"tps{i}") for i in range(2)]
        y_ps = ph.ps("yps", 1024)
        const_in, tbl_in, te_in, consts = (ph.load(n) for n in ("const_in", "tbl_in", "te_in", "consts"))
        w1_in, w2_in = ph.loads("w1_in", KD), ph.loads("w2_in", KD)
        b1_in, b2_in = ph.load("b1_in"), ph.load("b2_in")
        x_in = ph.loads("x_in")
        y_stored = ph.stores("y_stored")
        idx_ready = ph.event("idx_ready")
        w1_used, w2_used = ph.event("w1_used"), ph.event("w2_used")
        x_turned, xT_ready, h_ready, h_taken, glu_ready, sig_ready, a_ready, a_turned, aT_ready, y_ready, y_taken = (
            ph.event(n) for n in ("x_turned", "xT_ready", "h_ready", "h_taken", "glu_ready", "sig_ready", "a_ready",
                                  "a_turned", "aT_ready", "y_ready", "y_taken"))
        block = ctx.enter_context(nc.Block())

        def lagged(eng, step):
            step(at(eng, 0), True, False)
            step(at(eng, 1), True, True)
            with eng.Fori(1, NTL // 2) as it:
                pair = Pair(eng, it)
                for k in range(2):
                    step(Turn(pair, k), True, True)
            if NTL % 2:
                step(at(eng, NTL - 1), True, True)
            step(at(eng, NTL), False, True)

        @block.sync
        def _(sp):
            ph.grant(sp)
            sp.dma_start(gc[:, :], norm3_g[0].rearrange("(k p) -> p k", p=P), allow_slow_non_contiguous=True
                         ).then_inc(const_in, 16)
            sp.dma_start(te[:, :, :], TE.unsqueeze(0)).then_inc(te_in, 16)
            sp.wait_ge(te_in, 16)

            def is_first(t):
                return isinstance(t.pair.it, int) and t.t == 0

            def row(which, i):
                return te[0:1, which, bass.ds(i, 1)]

            def load(i, t, first):
                e = sp.value_load(row(0, i), min_val=0, max_val=NE - 1)
                new = sp.value_load(row(1, i), min_val=0, max_val=1)
                return e, new

            def first_weights(t):
                e, new = load(t.t, t, True)
                for k in range(KD):
                    if not is_first(t):
                        sp.wait_ge(w1_used, t.of(8, k - 8))
                    sp.dma_start(w1_sb[:, k, :], w1[0][bass.ds(e, 1), k * P:(k + 1) * P, :].rearrange("o p n -> p (o n)"),
                                 cond=new).then_inc(w1_in[k], 16)
                sp.wait_ge(h_taken, t.back1)
                sp.dma_start(b1_sb[:, :], b1[0][bass.ds(e, 1), :].to_broadcast([P, 2 * FF]), cond=new
                             ).then_inc(b1_in, 16)

            def second_weights(t):
                e, new = load(t.t, t, False)
                for k in range(KD):
                    if not is_first(t):
                        sp.wait_ge(w2_used, t.of(8, k - 8))
                    sp.dma_start(w2_sb[:, k, :], w2[0][bass.ds(e, 1), k * P:(k + 1) * P, :].rearrange("o p n -> p (o n)"),
                                 cond=new).then_inc(w2_in[k], 16)
                sp.wait_ge(y_taken, t.back1)
                sp.dma_start(b2_sb[:, :], b2[0][bass.ds(e, 1), :].to_broadcast([P, D]), cond=new).then_inc(b2_in, 16)

            def step(t):
                first_weights(t)
                if not (isinstance(t.pair.it, int) and t.t == 0):
                    second_weights(t.prev)

            step(at(sp, 0))
            step(at(sp, 1))
            with sp.Fori(1, NTL // 2) as it:
                pair = Pair(sp, it)
                for k in range(2):
                    step(Turn(pair, k))
            if NTL % 2:
                step(at(sp, NTL - 1))
            second_weights(at(sp, NTL - 1))

        @block.gpsimd
        def _(pool):
            make_identity(pool, ident)
            pool.dma_start(tbl[:, :], TBL).then_inc(tbl_in, 16)
            pool.wait_ge(tbl_in, 16)
            pool.drain()
            pool.sem_inc(consts, 1)

            def step(t):
                pool.wait_ge(x_turned, t.back2)
                pool.tensor_copy(idx[:, t.p:t.p + 1], tbl[:, bass.ds(t.t, 1)])
                pool.drain()
                pool.indirect_dma_start(out=xg[:, t.p, :], out_offset=None, in_=XN.rearrange("t p d -> (t p) d"),
                                        in_offset=bass.IndirectOffsetOnAxis(ap=idx[:, t.p:t.p + 1], axis=0)
                                        ).then_inc(x_in[t.p], 16)

            all_steps(pool, NTL, step)

        @block.scalar
        def _(act):
            def step(t, this, before):
                if before:
                    b = t.prev
                    act.wait_ge(a_turned, b.now)
                    act.wait_ge(y_ready, b.back1)
                    for j in range(2):
                        ins = act.activation(aT[:, 4 * j:4 * j + 4, :], t_ps[j][:, :].rearrange("p (k r) -> p k r", r=P),
                                             ACT.Copy)
                    ins.then_inc(aT_ready, 1)
                if this:
                    act.wait_ge(glu_ready, t.now)
                    act.wait_ge(a_ready, t.back1)
                    act.activation(sig[:, :], glu[:, :], ACT.Sigmoid, scale=ALPHA).then_inc(sig_ready, 1)
                if before:
                    act.wait_ge(y_taken, b.now)
                    act.dma_start(YS[b.t], y[:, b.p, :]).then_inc(y_stored[b.p], 16)

            lagged(act, step)
            for p, n in enumerate(((NTL + 1) // 2, NTL // 2)):
                act.wait_ge(y_stored[p], 16 * n + 16)

        @block.vector
        def _(dve):
            dve.wait_ge(const_in, 16)

            def turn_x(t):
                dve.wait_ge(x_turned, t.now)
                dve.wait_ge(h_ready, t.back2)
                for j in range(2):
                    ins = dve.tensor_tensor(xT[:, t.p, 4 * j:4 * j + 4, :], t_ps[j][:, :].rearrange("p (k r) -> p k r", r=P),
                                            across(gc[:, 4 * j:4 * j + 4], P), ALU.mult)
                ins.then_inc(xT_ready, 1)

            def step(t, this, before):
                if this:
                    dve.wait_ge(h_ready, t.now)
                    dve.wait_ge(b1_in, t.dma1)
                    for c in range(4):
                        ins = dve.tensor_tensor(hb[:, c * 512:(c + 1) * 512], h_ps[c][:, :], b1_sb[:, c * 512:(c + 1) * 512],
                                                ALU.add)
                    ins.then_inc(h_taken, 1)
                    dve.drain()
                    dve.wait_ge(sig_ready, t.back1)
                    dve.wait_ge(a_turned, t.back1)
                    dve.tensor_scalar(glu[:, :], hb[:, 0:2 * FF:2], LIMIT, None, ALU.min).then_inc(glu_ready, 1)
                    dve.tensor_scalar(lin[:, :], hb[:, 1:2 * FF:2], LIMIT, -LIMIT, ALU.min, ALU.max)
                    dve.drain()
                    dve.scalar_tensor_tensor(lin[:, :], lin[:, :], 1.0, glu[:, :], ALU.add, ALU.mult)
                if before:
                    b = t.prev
                    dve.wait_ge(y_ready, b.now)
                    dve.wait_ge(b2_in, b.dma1)
                    dve.wait_ge(y_stored[b.p], b.dma)
                    dve.tensor_tensor(y[:, b.p, :], y_ps[:, :], b2_sb[:, :], ALU.add).then_inc(y_taken, 1)
                if this:
                    if not (isinstance(t.pair.it, int) and t.t == NTL - 1):
                        turn_x(t.next)
                    dve.drain()
                    dve.wait_ge(sig_ready, t.now)
                    dve.tensor_tensor(lin[:, :], lin[:, :], sig[:, :], ALU.mult).then_inc(a_ready, 1)

            turn_x(at(dve, 0))
            lagged(dve, step)

        @block.tensor
        def _(pe):
            pe.wait_ge(consts, 1)

            def turn8(src):
                for k in range(KD):
                    ins = pe.transpose(t_ps[k // 4][:, k % 4 * P:(k % 4 + 1) * P], src[:, k * P:(k + 1) * P], ident[:, :])
                return ins

            def turn_x(t):
                pe.wait_ge(x_in[t.p], t.dma)
                turn8(xg[:, t.p, :]).then_inc(x_turned, 1)

            def step(t, this, before):
                b = t.prev
                if this:
                    pe.wait_ge(xT_ready, t.now)
                    pe.wait_ge(h_taken, t.back1)
                    for k in range(KD):
                        pe.wait_ge(w1_in[k], t.dma1)
                        for c in range(4):
                            ins = pe.matmul(h_ps[c][:, :], xT[:, t.p, k, :], w1_sb[:, k, c * 512:(c + 1) * 512],
                                            start=(k == 0), stop=(k == KD - 1))
                        ins.then_inc(w1_used, 1)
                        if k == 3 and before:
                            pe.wait_ge(a_ready, b.now)
                            turn8(lin).then_inc(a_turned, 1)
                    pe.wait_ge(w1_used, t.of(8, 7))
                    pe.sem_inc(h_ready, 1)
                elif before:
                    pe.wait_ge(a_ready, b.now)
                    turn8(lin).then_inc(a_turned, 1)
                if before:
                    pe.wait_ge(aT_ready, b.now)
                    pe.wait_ge(y_taken, b.back1)
                if this and not (isinstance(t.pair.it, int) and t.t == NTL - 1):
                    turn_x(t.next)
                if before:
                    for k in range(KD):
                        pe.wait_ge(w2_in[k], b.dma1)
                        for c in range(2):
                            ins = pe.matmul(y_ps[:, c * 512:(c + 1) * 512], aT[:, k, :],
                                            w2_sb[:, k, c * 512:(c + 1) * 512], start=(k == 0), stop=(k == KD - 1),
                                            skip_group_check=True)
                        ins.then_inc(w2_used, 1)
                    pe.wait_ge(w2_used, b.of(8, 7))
                    pe.sem_inc(y_ready, 1)

            turn_x(at(pe, 0))
            lagged(pe, step)


def combine_experts(nc, H, RT, SL, YS, y_prompt, y_sample):
    with ExitStack() as ctx:
        ph = Phase(nc, ctx, "cb")
        sl = ph.sb("sl", [P, NT * TOPK], I32)
        idx = ph.sb("idx", [P, 2, TOPK], I32)
        gt = ph.sb("gt", [P, NT, 8])
        h = ph.sb("h", [P, 2, D])
        r = ph.sb("r", [P, 2, TOPK, D])
        y = ph.sb("y", [P, 2, D])
        sl_in, gt_in = ph.load("sl_in"), ph.load("gt_in")
        h_in, r_in = ph.loads("h_in"), ph.loads("r_in")
        y_stored = ph.stores("y_stored")
        idx_ready, y_ready = ph.event("idx_ready"), ph.event("y_ready")
        block = ctx.enter_context(nc.Block())

        @block.sync
        def _(sp):
            ph.grant(sp)
            sp.dma_start(sl[:, :], SL).then_inc(sl_in, 16)
            sp.dma_start(gt[:, :, :], RT.rearrange("t p c -> p t c")).then_inc(gt_in, 16)

            def step(t):
                sp.wait_ge(y_ready, t.back2)
                sp.dma_start(h[:, t.p, :], H[t.t]).then_inc(h_in[t.p], 16)

            all_steps(sp, NT, step)

        @block.gpsimd
        def _(pool):
            pool.wait_ge(sl_in, 16)

            def step(t, n=P):
                pool.wait_ge(y_ready, t.back2)
                pool.tensor_copy(idx[:, t.p, :], sl[:, bass.ds(t.t * TOPK, TOPK)])
                pool.drain()
                for k in range(TOPK):
                    pool.indirect_dma_start(out=r[0:n, t.p, k, :], out_offset=None, in_=YS.rearrange("t p d -> (t p) d"),
                                            in_offset=bass.IndirectOffsetOnAxis(ap=idx[0:n, t.p, k:k + 1], axis=0)
                                            ).then_inc(r_in[t.p], 16)

            all_steps(pool, NT, step, lambda t: step(t, SAMPLE))

        @block.scalar
        def _(act):
            yr = y_prompt[0].rearrange("(t r) d -> t r d", r=P)

            def step(t, last=False):
                act.wait_ge(y_ready, t.now)
                if last:
                    act.dma_start(y_sample.rearrange("b t d -> (b t) d"), y[0:SAMPLE, t.p, :]).then_inc(y_stored[t.p], 16)
                else:
                    act.dma_start(yr[t.t], y[:, t.p, :]).then_inc(y_stored[t.p], 16)

            all_steps(act, NT, step, lambda t: step(t, True))
            for p, n in enumerate(((NT + 1) // 2, NT // 2)):
                act.wait_ge(y_stored[p], 16 * n + 16)

        @block.vector
        def _(dve):
            dve.wait_ge(gt_in, 16)

            def step(t, n=P):
                dve.wait_ge(h_in[t.p], t.dma)
                dve.wait_ge(r_in[t.p], t.dma4)
                dve.wait_ge(y_stored[t.p], t.dma)
                for k in range(TOPK):
                    src = h[0:n, t.p, :] if k == 0 else y[0:n, t.p, :]
                    ins = dve.scalar_tensor_tensor(y[0:n, t.p, :], r[0:n, t.p, k, :], gt[0:n, bass.ds(t.t, 1), k],
                                                   src, ALU.mult, ALU.add)
                    if k < TOPK - 1:
                        dve.drain()
                ins.then_inc(y_ready, 1)

            all_steps(dve, NT, step, lambda t: step(t, SAMPLE))


def decoder_step(nc, i, o):
    y_prompt, y_sample, k_prompt, v_prompt, gla_prompt, mk, mv, k_sample, v_sample, gla_sample = o

    def scratch(name, shape, dt=F32):
        return nc.dram_tensor(name, shape, dt, kind="Internal").ap()

    Z = scratch("z_rows", (NT, P, ZW))
    U = [scratch(f"u_rows{g}", (SEQ, UW)) for g in range(len(GROUPS))]
    OB, OAS = scratch("b_rows", (NT, P, BVW)), scratch("a_rows_sample", (SAMPLE, AW))
    H, XN, RT = scratch("h_rows", (NT, P, D)), scratch("x_rows", (NT, P, D)), scratch("routes", (NT, P, 8))
    TBL, SL = scratch("slot_tokens", (P, NTL), I32), scratch("token_slots", (P, NT * TOPK), I32)
    TE, YS = scratch("tile_experts", (2, NTL), I32), scratch("slot_rows", (NTL, P, D))

    project(nc, i["x_prompt"], i["x_sample"], i["norm1_g"], i["w_in"], i["a_q_norm_g"], i["a_k_norm_g"],
            i["gla_w_alpha"], i["gla_b_alpha"], Z,
            ((i["cache_swa_k"], k_sample), (i["cache_swa_v"], v_sample)))
    dilated(nc, Z, U, (k_prompt, v_prompt), (k_sample, v_sample))
    gla(nc, Z, i["gla_out_norm_g"], i["state_gla"], OB, gla_prompt, gla_sample)
    dilated_sample(nc, Z, i["cache_swa_k"], i["cache_swa_v"], OAS)
    memory_kv(nc, i["mem_prompt"], i["mem_norm_g"], i["mem_w_k"], i["mem_w_v"], i["mem_k_norm_g"], mk, mv)
    mix_attend_route(nc, i["x_prompt"], i["x_sample"], U, OB, OAS, i["w_out"], i["norm2_g"], i["mem_w_q"],
                     i["mem_q_norm_g"], i["mem_w_o"], i["norm3_g"], i["router_w"], i["router_b"], mk, mv,
                     i["cache_mem_k"], i["cache_mem_v"], H, XN, RT)
    slots(nc, RT, TBL, SL, TE)
    experts(nc, XN, i["norm3_g"], TBL, TE, i["exp_w1"], i["exp_b1"], i["exp_w2"], i["exp_b2"], YS)
    combine_experts(nc, H, RT, SL, YS, y_prompt, y_sample)


_OUTS = [(1, SEQ, D), (DEC_B, DEC_T, D), (1, 1, WBUF, AH, AD), (1, 1, WBUF, AH, AD), (1, 1, BH, BK, BV),
         (1, 1, NMEM, MH, MD), (1, 1, NMEM, MH, MD), (1, DEC_B, WBUF, AH, AD), (1, DEC_B, WBUF, AH, AD),
         (1, DEC_B, BH, BK, BV)]


def kernel(**inputs):
    import numpy as np
    import concourse.bacc as bacc
    from concourse.bass_utils import run_bass_kernel_spmd as run

    nc = bacc.Bacc("TRN2", target_bir_lowering=False, num_devices=1)
    arrays, ins = {}, {}
    for name, a in inputs.items():
        arrays[f"in_{name}"] = np.ascontiguousarray(a)
        ins[name] = nc.dram_tensor(f"in_{name}", a.shape, F32, kind="ExternalInput").ap()
    outs = [nc.dram_tensor(f"out_{k}", s, F32, kind="ExternalOutput").ap() for k, s in enumerate(_OUTS)]
    decoder_step(nc, ins, outs)
    r = run(nc, [arrays], core_ids=[0])
    return tuple(r.results[0][f"out_{k}"] for k in range(len(_OUTS)))
```

```python
import math
from contextlib import ExitStack

import concourse.bass as bass
from concourse import mybir
from concourse.alu_op_type import AluOpType as ALU

F32 = mybir.dt.float32
I32 = mybir.dt.int32
U32 = mybir.dt.uint32
ACT = mybir.ActivationFunctionType
AX = mybir.AxisListType

P = 128
D = 1024
KD = D // P
SEQ, DEC_B, DEC_T, PAST = 4096, 8, 8, 4096
SAMPLE = DEC_B * DEC_T
NT = SEQ // P + 1
TOKENS = SEQ + SAMPLE
AH, AD = 8, 64
AW = AH * AD
GROUPS = ((128, 1), (512, 4), (2048, 16))
WBUF = 2048
BH, BK, BV = 4, 64, 128
BQK, BVW = BH * BK, BH * BV
RANK, TEMP = 16, 16.0
NMEM, MH, MD = 256, 4, 128
MW = MH * MD
NE, TOPK, FF = 32, 4, 1024
ALPHA, LIMIT, EPS = 1.702, 7.0, 1e-6
NEG = -1.0e30
ZQ, ZK, ZV, ZBQ, ZBK, ZBV, ZBR, ZLA = 0, 512, 1024, 1536, 1792, 2048, 2560, 3072
ZW = 3328
NTL = (TOKENS * TOPK + NE * (P - 1)) // P
UW = AW + 2 * AH


class Pair:

    def __init__(self, eng, it):
        self.eng, self.it, self.kept = eng, it, {}

    def value(self, by, add):
        if isinstance(self.it, int):
            return by * self.it + add
        if (by, add) not in self.kept:
            self.kept[by, add] = self.eng.snap(self.it * by + add)
        return self.kept[by, add]


class Turn:

    def __init__(self, pair, n):
        self.pair, self.n, self.p = pair, n, n % 2

    @property
    def t(self):
        return self.pair.value(2, self.n)

    @property
    def now(self):
        return self.pair.value(2, self.n + 3)

    @property
    def back1(self):
        return self.pair.value(2, self.n + 2)

    @property
    def back2(self):
        return self.pair.value(2, self.n + 1)

    @property
    def twice(self):
        return self.pair.value(4, 2 * self.n + 4)

    @property
    def dma(self):
        return self.pair.value(16, 16 + 16 * (self.n // 2))

    @property
    def dma1(self):
        return self.pair.value(32, 16 + 16 * self.n)

    @property
    def dma2(self):
        return self.pair.value(32, 32 + 32 * (self.n // 2))

    @property
    def dma4(self):
        return self.pair.value(64, 64 + 64 * (self.n // 2))

    @property
    def dma5(self):
        return self.pair.value(80, 80 + 80 * (self.n // 2))

    def of(self, per, k):
        return self.pair.value(2 * per, per * self.n + k + 3)

    @property
    def prev(self):
        return Turn(self.pair, self.n - 1)

    @property
    def next(self):
        return Turn(self.pair, self.n + 1)


def at(eng, t):
    return Turn(Pair(eng, t // 2), t % 2)


def all_steps(eng, n, step, last=None):
    with eng.Fori(0, n // 2) as it:
        pair = Pair(eng, it)
        for k in range(2):
            step(Turn(pair, k))
    if n % 2:
        (last or step)(at(eng, n - 1))


class Phase:

    def __init__(self, nc, ctx, name):
        self.nc, self.ctx, self.name = nc, ctx, name
        self.granted, self.semaphores = [], []
        ctx.callback(self.clear)

    def clear(self):
        self.nc.clear_and_free_semaphores(self.semaphores)
        self.nc.all_engine_barrier()

    def semaphore(self, name):
        s = self.nc.alloc_semaphore(name=f"{self.name}_{name}")
        self.semaphores.append(s)
        return s

    def sb(self, name, shape, dt=F32):
        return self.ctx.enter_context(self.nc.sbuf_tensor(f"{self.name}_{name}", shape, dt))

    def ps(self, name, width=512):
        return self.ctx.enter_context(self.nc.psum_tensor(f"{self.name}_{name}", [P, width], F32))

    def event(self, name):
        s = self.semaphore(name)
        self.granted.append((s, 2))
        return s

    def loads(self, name, n=2):
        return [self.semaphore(f"{name}{i}") for i in range(n)]

    def load(self, name):
        return self.loads(name, 1)[0]

    def stores(self, name, n=2):
        s = self.loads(name, n)
        self.granted += [(x, 16) for x in s]
        return s

    def grant(self, eng):
        for s, v in self.granted:
            eng.sem_inc(s, v)


def make_identity(pool, ident):
    pool.memset(ident[:, :], 0.0)
    pool.drain()
    pool.affine_select(out=ident[:, :], in_=ident[:, :], compare_op=ALU.not_equal, fill=1.0, base=0,
                       pattern=[[-1, P]], channel_multiplier=1)


def across(ap, n):
    return ap.unsqueeze(2).to_broadcast([ap.shape[0], ap.shape[1], n])


def inverse_rms(dve, out, sums, width, tmp):
    half, t = tmp
    dve.tensor_scalar(half, sums, -0.5 / width, -0.5 * EPS, ALU.mult, ALU.add)
    dve.tensor_scalar(out, sums, 1.0 / width, EPS, ALU.mult, ALU.add)
    dve.drain()
    dve.tensor_scalar(out.bitcast(I32), out.bitcast(I32), -0.5, float(0x5F3759DF), ALU.mult, ALU.add)
    for _ in range(3):
        dve.drain()
        dve.tensor_tensor(t, out, out, ALU.mult)
        dve.drain()
        dve.tensor_tensor(t, t, half, ALU.mult)
        dve.drain()
        ins = dve.scalar_tensor_tensor(out, t, 1.5, out, ALU.add, ALU.mult)
    return ins


def project(nc, part, x_prompt, x_sample, norm1_g, w_in, a_q_g, a_k_g, w_alpha, b_alpha, Z, shifts):
    CH = 512
    NC = 3
    WC = NC * CH + (RANK if part else 0)
    W0 = NC * CH * part
    ZC = ZW - W0 if part else NC * CH
    F32R = mybir.dt.float32r
    with ExitStack() as ctx:
        ph = Phase(nc, ctx, f"p{part}")
        ident = ph.sb("ident", [P, P])
        w_raw = ph.sb("w_raw", [P, 2, KD, CH])
        w_hi, w_lo = ph.sb("w_hi", [P, KD, WC], F32R), ph.sb("w_lo", [P, KD, WC], F32R)
        g1c = ph.sb("g1c", [P, KD])
        x_sb = ph.sb("x", [P, 2, D])
        xs = ph.sb("xs", [P, D])
        xsq = ph.sb("xsq", [P, D])
        ss = ph.sb("ss", [P, 2])
        tmp = ph.sb("tmp", [P, 2, 2 * AH])
        xT_hi, xT_lo = ph.sb("xT_hi", [P, 2, KD, P], F32R), ph.sb("xT_lo", [P, 2, KD, P], F32R)
        z_sb = ph.sb("z", [P, 2, ZC])
        z_ps = [ph.ps(f"zps{i}") for i in range(NC)]
        xT_ps = [ph.ps(f"xTps{i}") for i in range(2)]
        if part:
            wa = ph.sb("wa", [RANK + 1, BQK])
            lrT = ph.sb("lrT", [RANK + 1, P])
            gate_t = ph.sb("gate_t", [P, 2, BVW])
            la_t = ph.sb("la_t", [P, 3, BQK])
            sm_ps = ph.ps("smps")
        else:
            qkg = ph.sb("qkg", [P, 2 * AW])
            sq = ph.sb("sq", [P, 2 * AW])
            hss = ph.sb("hss", [P, 2 * AH])
            hr = ph.sb("hr", [P, 2 * AH])

        const_in, w_loaded, w_split = ph.load("const_in"), ph.loads("w_loaded"), ph.load("w_split")
        consts, shifted = ph.load("consts"), ph.load("shifted")
        x_loaded = ph.loads("x_loaded")
        z_stored = ph.stores("z_stored")
        x_summed, x_scaled = ph.event("x_summed"), ph.event("x_scaled")
        x_turned = [ph.event(f"x_turned{i}") for i in range(2)]
        hi_ready, xT_ready = ph.event("hi_ready"), ph.event("xT_ready")
        z_ready = [ph.event(f"z_ready{i}") for i in range(NC)]
        z_taken = [ph.event(f"z_taken{i}") for i in range(NC)]
        if part:
            rank_ready, rank_taken = ph.event("rank_ready"), ph.event("rank_taken")
            decay_ready = ph.event("decay_ready")
            gate_exp = ph.event("gate_exp")
            la_abs, la_ln, la_done = ph.event("la_abs"), ph.event("la_ln"), ph.event("la_done")
        else:
            heads_squared, heads_summed = ph.event("heads_squared"), ph.event("heads_summed")
            heads_scaled, heads_done = ph.event("heads_scaled"), ph.event("heads_done")
        CONSTS_IN = 3 * 16
        block = ctx.enter_context(nc.Block())

        def weight_chunks():
            parts = [(NC * CH, RANK)] * part + [(c * CH, CH) for c in range(NC)]
            return [(i, lo, n) for i, (lo, n) in enumerate(parts)]

        @block.sync
        def _(sp):
            ph.grant(sp)
            sp.dma_start(g1c[:, :], norm1_g[0].rearrange("(k p) -> p k", p=P),
                         allow_slow_non_contiguous=True).then_inc(const_in, 16)
            if part:
                sp.dma_start(wa[0:RANK, :], w_alpha[0]).then_inc(const_in, 16)
                sp.dma_start(wa[RANK:RANK + 1, :], b_alpha).then_inc(const_in, 16)
            else:
                for i, g in enumerate((a_q_g, a_k_g)):
                    sp.dma_start(qkg[:, i * AW:(i + 1) * AW].rearrange("p (h d) -> p h d", h=AH),
                                 g[0].unsqueeze(0).unsqueeze(0).to_broadcast([P, AH, AD])).then_inc(const_in, 16)

            def load_x(p, rows):
                sp.dma_start(x_sb[:rows.shape[0], p, :], rows).then_inc(x_loaded[p], 16)

            xr = x_prompt[0].rearrange("(t r) d -> t r d", r=P)

            def pair_of_loads(it, shift):
                pair = Pair(sp, it)
                for k in range(2):
                    t = Turn(pair, k)
                    sp.wait_ge(x_scaled, t.back2)
                    load_x(k, xr[t.t])
                    if shift:
                        old, new = shifts[k]
                        sp.dma_start(new[0, bass.ds(it, 1), 0:WBUF - DEC_T].rearrange("o r h d -> (o r) (h d)"),
                                     old[0, bass.ds(it, 1), DEC_T:WBUF].rearrange("o r h d -> (o r) (h d)")
                                     ).then_inc(shifted, 16)

            shifting = DEC_B if shifts else 0
            if shifts:
                with sp.Fori(0, DEC_B) as it:
                    pair_of_loads(it, True)
            with sp.Fori(shifting, (NT - 1) // 2) as it:
                pair_of_loads(it, False)
            sp.wait_ge(x_scaled, at(sp, NT - 1).back2)
            load_x(0, x_sample.rearrange("b t d -> (b t) d"))
            if shifts:
                sp.wait_ge(shifted, 2 * 16 * DEC_B)

        @block.gpsimd
        def _(pool):
            make_identity(pool, ident)
            if part:
                pool.memset(lrT[:, :], 1.0)
            pool.drain()
            pool.sem_inc(consts, 1)
            if not part:
                pool.wait_ge(const_in, CONSTS_IN)

                def step(t):
                    pool.wait_ge(heads_scaled, t.now)
                    qk = z_sb[:, t.p, 0:2 * AW]
                    pool.tensor_tensor(qk, qk, qkg[:, :], ALU.mult).then_inc(heads_done, 1)

                all_steps(pool, NT, step)

        @block.scalar
        def _(act):
            def load_weights(c, lo, n):
                act.dma_start(w_raw[:, c % 2, :, 0:n], w_in[0][:, W0 + lo:W0 + lo + n].rearrange("(k p) n -> p k n", p=P)
                              ).then_inc(w_loaded[c % 2], 16)

            def norm_x(t):
                act.wait_ge(x_loaded[t.p], t.dma)
                act.wait_ge(x_scaled, t.back1)
                act.activation(xsq[:, :], x_sb[:, t.p, :], ACT.Square, accum_out=ss[:, 0:1]
                               ).then_inc(x_summed, 1)
                act.drain()

            def take_x(t):
                for j in range(2):
                    act.wait_ge(x_turned[j], t.now)
                    if j == 0:
                        act.wait_ge(z_ready[NC - 1], t.back2)
                    ins = act.activation(xT_hi[:, t.p, 4 * j:4 * j + 4, :],
                                         xT_ps[j][:, :].rearrange("p (k r) -> p k r", k=4), ACT.Copy)
                ins.then_inc(hi_ready, 1)

            def step_a(t, more=True):
                if more:
                    norm_x(t.next)
                for c in range(2):
                    act.wait_ge(z_ready[c], t.now)
                    if c == 0:
                        act.wait_ge(heads_summed, t.back1)
                    act.activation(sq[:, c * CH:(c + 1) * CH], z_ps[c][:, :], ACT.Square
                                   ).then_inc(heads_squared, 1)
                if more:
                    take_x(t.next)
                act.wait_ge(z_ready[2], t.now)
                act.wait_ge(z_stored[t.p], t.dma)
                act.activation(z_sb[:, t.p, ZV:ZV + CH], z_ps[2][:, :], ACT.Copy).then_inc(z_taken[2], 1)
                act.drain()
                act.wait_ge(heads_done, t.now)
                act.dma_start(Z[t.t][:, 0:ZC], z_sb[:, t.p, :]).then_inc(z_stored[t.p], 16)

            def step_b(t, more=True):
                p = t.p
                if more:
                    norm_x(t.next)
                act.wait_ge(z_ready[0], t.now)
                act.wait_ge(z_stored[p], t.dma)
                act.activation(z_sb[:, p, ZBQ - W0:ZBQ - W0 + CH], z_ps[0][:, :], ACT.Copy).then_inc(z_taken[0], 1)
                act.wait_ge(la_abs, t.now)
                act.activation(la_t[:, 1, :], la_t[:, 0, :], ACT.Exp, scale=-1.0)
                act.drain()
                act.activation(la_t[:, 1, :], la_t[:, 1, :], ACT.Ln, bias=1.0).then_inc(la_ln, 1)
                act.wait_ge(z_ready[1], t.now)
                act.activation(z_sb[:, p, ZBV - W0:ZBV - W0 + CH], z_ps[1][:, :], ACT.Copy).then_inc(z_taken[1], 1)
                if more:
                    take_x(t.next)
                act.wait_ge(z_ready[2], t.now)
                act.wait_ge(z_taken[2], t.back1)
                act.activation(gate_t[:, 0, :], z_ps[2][:, :], ACT.Exp, scale=-1.0).then_inc(gate_exp, 1)
                act.drain()
                act.wait_ge(la_done, t.now)
                act.wait_ge(z_taken[2], t.now)
                act.dma_start(Z[t.t][:, W0:ZW], z_sb[:, p, :]).then_inc(z_stored[p], 16)

            chunks = weight_chunks()
            for chunk in chunks[0:2]:
                load_weights(*chunk)
            norm_x(at(act, 0))
            take_x(at(act, 0))
            for chunk in chunks[2:]:
                act.wait_ge(w_split, chunk[0] - 1)
                load_weights(*chunk)
            step = step_b if part else step_a
            all_steps(act, NT, step, lambda t: step(t, False))
            for p, n in enumerate(((NT + 1) // 2, NT // 2)):
                act.wait_ge(z_stored[p], 16 * n + 16)

        @block.vector
        def _(dve):
            def scale_x(t):
                dve.wait_ge(x_loaded[t.p], t.dma)
                dve.wait_ge(x_summed, t.now)
                inverse_rms(dve, ss[:, 1:2], ss[:, 0:1], D, (tmp[:, 0, 0:1], tmp[:, 1, 0:1]))
                dve.drain()
                dve.wait_ge(x_turned[1], t.back1)
                dve.tensor_scalar(xs[:, :], x_sb[:, t.p, :], ss[:, 1:2], None, ALU.mult).then_inc(x_scaled, 1)

            def take_x(t):
                dve.wait_ge(hi_ready, t.now)
                for j in range(2):
                    ins = dve.tensor_tensor(xT_lo[:, t.p, 4 * j:4 * j + 4, :],
                                            xT_ps[j][:, :].rearrange("p (k r) -> p k r", k=4),
                                            xT_hi[:, t.p, 4 * j:4 * j + 4, :], ALU.subtract)
                ins.then_inc(xT_ready, 1)

            def step_a(t, more=True):
                p = t.p
                if more:
                    scale_x(t.next)
                dve.wait_ge(heads_squared, t.twice)
                dve.tensor_reduce(hss[:, :], sq[:, :].rearrange("p (h d) -> p h d", d=AD), AX.X, ALU.add
                                  ).then_inc(heads_summed, 1)
                dve.drain()
                inverse_rms(dve, hr[:, :], hss[:, :], AD, (tmp[:, 0, :], tmp[:, 1, :]))
                dve.drain()
                if more:
                    take_x(t.next)
                dve.wait_ge(z_stored[p], t.dma)
                for c in range(2):
                    dve.tensor_tensor(z_sb[:, p, c * CH:(c + 1) * CH].rearrange("p (h d) -> p h d", d=AD),
                                      z_ps[c][:, :].rearrange("p (h d) -> p h d", d=AD),
                                      across(hr[:, c * AH:(c + 1) * AH], AD), ALU.mult).then_inc(z_taken[c], 1)
                dve.drain()
                dve.sem_inc(heads_scaled, 1)

            def step_b(t, more=True):
                dve.wait_ge(rank_ready, t.now)
                dve.tensor_copy(lrT[0:RANK, :], sm_ps[0:RANK, 0:P]).then_inc(rank_taken, 1)
                if more:
                    scale_x(t.next)
                dve.wait_ge(decay_ready, t.now)
                dve.wait_ge(la_ln, t.back1)
                a = sm_ps[:, 256:256 + BQK]
                dve.tensor_scalar(la_t[:, 2, :], a, 0.0, None, ALU.min)
                dve.drain()
                dve.scalar_tensor_tensor(la_t[:, 0, :], la_t[:, 2, :], -2.0, a, ALU.mult, ALU.add
                                         ).then_inc(la_abs, 1)
                dve.wait_ge(la_ln, t.now)
                dve.tensor_tensor(la_t[:, 1, :], la_t[:, 2, :], la_t[:, 1, :], ALU.subtract)
                dve.drain()
                dve.wait_ge(z_stored[t.p], t.dma)
                dve.tensor_scalar(z_sb[:, t.p, ZLA - W0:ZLA - W0 + BQK], la_t[:, 1, :], 1.0 / TEMP, None, ALU.mult
                                  ).then_inc(la_done, 1)
                if more:
                    take_x(t.next)
                dve.wait_ge(gate_exp, t.now)
                dve.tensor_scalar(gate_t[:, 1, :], gate_t[:, 0, :], 1.0, None, ALU.add)
                dve.drain()
                dve.reciprocal(gate_t[:, 1, :], gate_t[:, 1, :])
                dve.drain()
                dve.tensor_tensor(z_sb[:, t.p, ZBR - W0:ZBR - W0 + BVW], z_ps[2][:, :], gate_t[:, 1, :], ALU.mult
                                  ).then_inc(z_taken[2], 1)

            dve.wait_ge(const_in, CONSTS_IN)
            scale_x(at(dve, 0))
            take_x(at(dve, 0))
            for c, lo, n in weight_chunks():
                dve.wait_ge(w_loaded[c % 2], 16 * (c // 2 + 1))
                for k in range(KD):
                    dve.tensor_scalar(w_hi[:, k, lo:lo + n], w_raw[:, c % 2, k, 0:n], g1c[:, k:k + 1], None, ALU.mult)
                dve.drain()
                for k in range(KD):
                    ins = dve.scalar_tensor_tensor(w_lo[:, k, lo:lo + n], w_raw[:, c % 2, k, 0:n], g1c[:, k:k + 1],
                                                   w_hi[:, k, lo:lo + n], ALU.mult, ALU.subtract)
                ins.then_inc(w_split, 1)
            step = step_b if part else step_a
            all_steps(dve, NT, step, lambda t: step(t, False))

        @block.tensor
        def _(pe):
            pe.wait_ge(consts, 1)

            def turn_x(t):
                pe.wait_ge(x_scaled, t.now)
                pe.wait_ge(xT_ready, t.back1)
                for j in range(2):
                    for k in range(4 * j, 4 * j + 4):
                        ins = pe.transpose(xT_ps[j][:, (k % 4) * P:(k % 4 + 1) * P], xs[:, k * P:(k + 1) * P],
                                           ident[:, :])
                    ins.then_inc(x_turned[j], 1)

            def step(t, more=True):
                p = t.p
                pe.wait_ge(xT_ready, t.now)
                if part:
                    pe.wait_ge(w_split, 1)
                    pe.wait_ge(rank_taken, t.back1)
                    for k in range(KD):
                        for i, (w, x) in enumerate(((w_hi, xT_hi), (w_hi, xT_lo), (w_lo, xT_hi))):
                            ins = pe.matmul(sm_ps[0:RANK, 0:P], w[:, k, NC * CH:WC], x[:, p, k, :],
                                            start=(k == 0 and i == 0), stop=(k == KD - 1 and i == 2))
                    ins.then_inc(rank_ready, 1)
                for c in range(NC):
                    pe.wait_ge(w_split, part + c + 1)
                    pe.wait_ge(z_taken[c], t.back1)
                    for k in range(KD):
                        for i, (w, x) in enumerate(((w_hi, xT_hi), (w_lo, xT_hi), (w_hi, xT_lo))):
                            ins = pe.matmul(z_ps[c][:, :], x[:, p, k, :], w[:, k, c * CH:(c + 1) * CH],
                                            start=(k == 0 and i == 0), stop=(k == KD - 1 and i == 2))
                    ins.then_inc(z_ready[c], 1)
                    if part and c == 0:
                        pe.wait_ge(rank_taken, t.now)
                        pe.wait_ge(la_abs, t.back1)
                        pe.matmul(sm_ps[:, 256:256 + BQK], lrT[:, :], wa[:, :], start=True, stop=True
                                  ).then_inc(decay_ready, 1)
                    if c == 1 and more:
                        turn_x(t.next)

            turn_x(at(pe, 0))
            pe.wait_ge(const_in, CONSTS_IN)
            all_steps(pe, NT, step, lambda t: step(t, False))


def dilated(nc, Z, U, prompt_caches, sample_caches):
    SCALE = AD ** -0.5
    HH = AH // 2
    with ExitStack() as ctx:
        ph = Phase(nc, ctx, "dl")
        ident = ph.sb("ident", [P, P])
        bias = ph.sb("bias", [P, 2, 2, P])
        qkv = ph.sb("qkv", [P, 2, 2 * AW])
        v_sb = ph.sb("v", [P, 2, AW])
        qT = ph.sb("qT", [P, 2, 4, P])
        kT = ph.sb("kT", [P, 4, 2, P])
        sm = ph.sb("sm", [P, 2, HH, 2 * P])
        mx = ph.sb("mx", [P, 2, HH])
        pr = ph.sb("pr", [P, 2, HH, 2 * P])
        pT = ph.sb("pT", [P, 2, HH, 2, P])
        ms = ph.sb("ms", [P, 2, 2 * AH])
        u_sb = ph.sb("u", [P, 2, UW])
        t_ps = ph.ps("tps")
        s_ps = [ph.ps(f"sps{h}", 1024) for h in range(2)]
        pT_ps = ph.ps("pTps", 1024)
        o_ps = ph.ps("ops")

        consts, cached = ph.load("consts"), ph.load("cached")
        qk_loaded, v_loaded = ph.loads("qk_loaded"), ph.loads("v_loaded")
        u_stored, u_free = ph.loads("u_stored"), ph.event("u_free")
        q_turned, k_turned, qT_ready, kT_ready = (ph.event("q_turned"), ph.event("k_turned"),
                                                  ph.event("qT_ready"), ph.event("kT_ready"))
        scored = [ph.event(f"scored{h}") for h in range(2)]
        max_ready = [ph.event(f"max_ready{h}") for h in range(2)]
        masked = [ph.event(f"masked{h}") for h in range(2)]
        exps_done = [ph.event(f"exps_done{h}") for h in range(2)]
        p_turned = [ph.event(f"p_turned{h}") for h in range(2)]
        pT_ready = [ph.event(f"pT_ready{h}") for h in range(2)]
        o_ready, o_taken = ph.event("o_ready"), ph.event("o_taken")
        block = ctx.enter_context(nc.Block())

        def blocks(eng, step):
            done = 0
            for g, (_, dil) in enumerate(GROUPS):
                pairs = SEQ // (dil * P) // 2

                def head(r, n, last=False):
                    pair = Pair(eng, n)
                    step(Turn(pair, 0), g, r, True, 0 if g == 0 else 2, False)
                    step(Turn(pair, 1), g, r + P * dil, False, 1, last)

                def rest(r, n):
                    with eng.Fori(1, pairs) as m:
                        pair = Pair(eng, m + n)
                        for k in range(2):
                            step(Turn(pair, k), g, m * (2 * P * dil) + (r + k * P * dil), False, 2, False)

                if dil == 1:
                    head(0, done)
                    rest(0, done)
                elif pairs > 1:
                    with eng.Fori(0, dil) as r:
                        head(r, r * pairs + done)
                        rest(r, r * pairs + done)
                else:
                    with eng.Fori(0, dil - 1) as r:
                        head(r, r + done)
                    head(dil - 1, dil - 1 + done, last=True)
                done += dil * pairs
            return done

        def rows(ap, row, dil):
            return ap[bass.ds(row, P, step=dil), :]

        Zr = Z.rearrange("t r w -> (t r) w")

        @block.sync
        def _(sp):
            ph.grant(sp)
            for col, of_prompt, of_sample in zip((ZK, ZV), prompt_caches, sample_caches):
                sp.dma_start(of_prompt[0, 0].rearrange("r h d -> r (h d)"), Zr[SEQ - WBUF:SEQ, col:col + AW]
                             ).then_inc(cached, 16)
                sp.dma_start(of_sample[0][:, WBUF - DEC_T:WBUF].rearrange("b r h d -> b r (h d)"),
                             Zr[SEQ:TOKENS, col:col + AW].rearrange("(b r) w -> b r w", r=DEC_T)).then_inc(cached, 16)

            def step(t, g, row, first, before, last):
                dil = GROUPS[g][1]
                sp.wait_ge(k_turned, t.back2)
                sp.wait_ge(q_turned, t.back2)
                sp.dma_start(qkv[:, t.p, :], rows(Zr[:, 0:2 * AW], row, dil)).then_inc(qk_loaded[t.p], 16)

            blocks(sp, step)
            sp.wait_ge(cached, 64)

        @block.gpsimd
        def _(pool):
            make_identity(pool, ident)
            pool.memset(bias[:, :, :, :], 0.0)
            pool.drain()
            for p in range(2):
                pool.affine_select(out=bias[:, p, p, :], in_=bias[:, p, p, :], compare_op=ALU.is_ge, fill=NEG,
                                   base=0, pattern=[[-1, P]], channel_multiplier=1)
                pool.affine_select(out=bias[:, p, 1 - p, :], in_=bias[:, p, 1 - p, :], compare_op=ALU.is_ge,
                                   fill=NEG, base=0, pattern=[[1, P]], channel_multiplier=-1)
            pool.drain()
            pool.sem_inc(consts, 1)

            def step(t, g, row, first, before, last):
                pool.wait_ge(o_taken, t.now)
                pool.dma_start(rows(U[g], row, GROUPS[g][1]), u_sb[:, t.p, :]).then_inc(u_stored[t.p], 16)
                pool.wait_ge(u_stored[t.p], t.dma)
                pool.sem_inc(u_free, 1)

            blocks(pool, step)

        @block.scalar
        def _(act):
            def step(t, g, row, first, before, last):
                p = t.p
                if not last:
                    take_q(t.next)
                w = P if first else 2 * P
                for h in range(2):
                    act.wait_ge(max_ready[h], t.now)
                    act.wait_ge(p_turned[h], t.back1)
                    for j in range(HH):
                        a = AH + 2 * j + h
                        ins = act.activation(pr[:, h, j, 0:w], sm[:, h, j, 0:w], ACT.Exp,
                                             bias=ms[:, p, a - AH:a - AH + 1], scale=SCALE,
                                             accum_out=ms[:, p, a:a + 1])
                    ins.then_inc(exps_done[h], 1)
                    if h == 0 and not last:
                        take_k(t.next)
                if before:
                    finish(t.prev)
                act.dma_start(v_sb[:, p, :], rows(Zr[:, ZV:ZV + AW], row, GROUPS[g][1])).then_inc(v_loaded[p], 16)

            def finish(t):
                act.drain()
                act.wait_ge(o_ready, t.now)
                act.wait_ge(u_free, t.back2)
                act.activation(u_sb[:, t.p, AW:UW], ms[:, t.p, :], ACT.Copy)
                act.activation(u_sb[:, t.p, 0:AW], o_ps[:, :], ACT.Copy).then_inc(o_taken, 1)

            def take_q(t):
                act.wait_ge(q_turned, t.now)
                act.wait_ge(scored[1], t.back2)
                act.activation(qT[:, t.p, :, :], t_ps[:, :].rearrange("p (j r) -> p j r", j=4), ACT.Copy
                               ).then_inc(qT_ready, 1)

            def take_k(t):
                act.wait_ge(k_turned, t.now)
                act.wait_ge(scored[1], t.back1)
                act.activation(kT[:, :, t.p, :], t_ps[:, :].rearrange("p (j r) -> p j r", j=4), ACT.Copy
                               ).then_inc(kT_ready, 1)

            take_q(at(act, 0))
            take_k(at(act, 0))
            n = blocks(act, step)
            finish(at(act, 2 * n - 1))

        @block.vector
        def _(dve):
            dve.wait_ge(consts, 1)

            def step(t, g, row, first, before, last):
                p = t.p
                w = P if first else 2 * P
                dve.wait_ge(o_taken, t.back2)
                for h in range(2):
                    if before:
                        take_pT(t.prev, h, before)
                    dve.wait_ge(scored[h], t.now)
                    dve.wait_ge(exps_done[h], t.back1)
                    s = s_ps[h][:, :].rearrange("p (j k) -> p j k", j=HH)[:, :, 0:w]
                    b = bias[:, p, :, :].rearrange("p s k -> p (s k)")[:, 0:w].unsqueeze(1).to_broadcast([P, HH, w])
                    dve.tensor_tensor(sm[:, h, :, 0:w], s, b, ALU.add).then_inc(masked[h], 1)
                    dve.drain()
                    dve.tensor_reduce(mx[:, h, :], sm[:, h, :, 0:w], AX.X, ALU.max)
                    dve.drain()
                    dve.tensor_scalar(ms[:, p, h:AH:2], mx[:, h, :], -SCALE, None, ALU.mult
                                      ).then_inc(max_ready[h], 1)

            def take_pT(t, h, n):
                dve.wait_ge(p_turned[h], t.now)
                dve.wait_ge(o_ready, t.back1)
                dve.tensor_copy(pT[:, h, :, 0:n, :],
                                pT_ps[:, :].rearrange("p (j s r) -> p j s r", j=HH, s=2)[:, :, 0:n, :]
                                ).then_inc(pT_ready[h], 1)

            n = blocks(dve, step)
            for h in range(2):
                take_pT(at(dve, 2 * n - 1), h, 2)

        @block.tensor
        def _(pe):
            pe.wait_ge(consts, 1)

            def step(t, g, row, first, before, last):
                n = 1 if first else 2
                if not last:
                    turn_q(t.next)
                pe.wait_ge(kT_ready, t.now)
                for h in range(2):
                    if before:
                        turn_p(t.prev, h, before)
                    pe.wait_ge(masked[h], t.back1)
                    for j in range(HH):
                        hd = 2 * j + h
                        lo = h * AD
                        ins = pe.matmul(s_ps[h][:, j * 2 * P:j * 2 * P + n * P], qT[lo:lo + AD, t.p, hd // 2, :],
                                        kT[lo:lo + AD, hd // 2, 0:n, :], start=True, stop=True)
                    ins.then_inc(scored[h], 1)
                    if h == 0 and not last:
                        turn_k(t.next)
                if before:
                    weigh_values(t.prev, before)

            def turn_q(t):
                pe.wait_ge(qk_loaded[t.p], t.dma)
                pe.wait_ge(kT_ready, t.back1)
                for j in range(4):
                    ins = pe.transpose(t_ps[:, j * P:(j + 1) * P], qkv[:, t.p, j * P:(j + 1) * P], ident[:, :])
                ins.then_inc(q_turned, 1)

            def turn_k(t):
                pe.wait_ge(qT_ready, t.now)
                for j in range(4, 8):
                    ins = pe.transpose(t_ps[:, (j - 4) * P:(j - 3) * P], qkv[:, t.p, j * P:(j + 1) * P], ident[:, :])
                ins.then_inc(k_turned, 1)

            def turn_p(t, h, n):
                pe.wait_ge(exps_done[h], t.now)
                if h == 0:
                    pe.wait_ge(pT_ready[1], t.back1)
                else:
                    pe.wait_ge(pT_ready[0], t.now)
                for j in range(HH):
                    for s in range(n):
                        ins = pe.transpose(pT_ps[:, (2 * j + s) * P:(2 * j + s + 1) * P],
                                           pr[:, h, j, s * P:(s + 1) * P], ident[:, :])
                ins.then_inc(p_turned[h], 1)

            def weigh_values(t, n):
                pe.wait_ge(v_loaded[t.p], t.dma)
                pe.wait_ge(o_taken, t.back1)
                for h in range(2):
                    pe.wait_ge(pT_ready[h], t.now)
                    for j in range(HH):
                        hd = 2 * j + h
                        for s in range(n):
                            ins = pe.matmul(o_ps[:, hd * AD:(hd + 1) * AD], pT[:, h, j, s, :],
                                            v_sb[:, s, hd * AD:(hd + 1) * AD], start=(s == 0), stop=(s == n - 1))
                ins.then_inc(o_ready, 1)

            turn_q(at(pe, 0))
            turn_k(at(pe, 0))
            n = blocks(pe, step)
            t = at(pe, 2 * n - 1)
            for h in range(2):
                turn_p(t, h, 2)
            weigh_values(t, 2)


def gla(nc, Z, out_g, state0, OB, new_prompt, new_sample):
    VW = 2 * BV
    NP = BH // 2
    ZF = 3 * BQK
    CQ, CK, CL, CV, CR = 0, BQK, 2 * BQK, 0, BVW
    NTP = NT - 1
    with ExitStack() as ctx:
        ph = Phase(nc, ctx, "gl")
        ident = ph.sb("ident", [P, P])
        tri = ph.sb("tri", [P, P])
        tric = ph.sb("tric", [P, P])
        cuts = ph.sb("cuts", [P, 3])
        halves = ph.sb("halves", [P, NP, 2, BV])
        gout = ph.sb("gout", [P, BH, BV])
        tmp = ph.sb("tmp", [P, 2, BH])
        zf = ph.sb("zf", [P, 2, ZF])
        zb = ph.sb("zb", [P, 2, 2 * BVW])
        eb = ph.sb("eb", [P, 2, BQK])
        ec = ph.sb("ec", [P, 2, NP, 8])
        qk = ph.sb("qk", [P, 2, 2, BQK])
        qkT = ph.sb("qkT", [P, 2 * NP, P])
        att = ph.sb("att", [P, BH, P])
        sc = ph.sb("sc", [P, NP, VW])
        st = ph.sb("st", [P, NP, VW])
        dm = ph.sb("dm", [P, NP, VW])
        osq = ph.sb("osq", [P, BVW])
        oss = ph.sb("oss", [P, BH])
        ors = ph.sb("ors", [P, BH])
        gr = ph.sb("gr", [P, 2, BVW])
        o1 = ph.sb("o1", [P, BVW])
        ob = ph.sb("ob", [P, 2, BVW])
        b_ps, c_ps, qkT_ps, d_ps = (ph.ps(n) for n in ("bps", "cps", "qkTps", "dps"))
        o_ps = [ph.ps(f"ops{i}") for i in range(2)]
        att_ps = [ph.ps(f"attps{i}") for i in range(2)]
        same = ph.sb("same", [SAMPLE, DEC_B, DEC_T])
        tri8 = ph.sb("tri8", [SAMPLE, SAMPLE])
        seq1 = ph.sb("seq1", [SAMPLE, DEC_B])
        cols8 = ph.sb("cols8", [P, DEC_B, SAMPLE])
        qTm = ph.sb("qTm", [P, NP, DEC_B, SAMPLE])
        km = ph.sb("km", [SAMPLE, DEC_B, BQK])
        sts = ph.sb("sts", [P, DEC_B, NP, VW])
        nst = ph.sb("nst", [P, DEC_B, NP, VW])

        const_in, consts, state_in = ph.load("const_in"), ph.load("consts"), ph.load("state_in")
        zf_loaded, zb_loaded = ph.loads("zf_loaded"), ph.loads("zb_loaded")
        o_stored = ph.stores("o_stored")
        s_stored = ph.load("s_stored")
        b_ready, b_exp, scaled, qk_turned, qkT_ready = (ph.event(n) for n in (
            "b_ready", "b_exp", "scaled", "qk_turned", "qkT_ready"))
        att_ready, att_masked, sc_ready, o_ready, d_ready = (ph.event(n) for n in (
            "att_ready", "att_masked", "sc_ready", "o_ready", "d_ready"))
        st_ready, o_squared, o_summed, gr_ready, ob_ready = (ph.event(n) for n in (
            "st_ready", "o_squared", "o_summed", "gr_ready", "ob_ready"))
        q_masked, d8_ready, d8_used = ph.load("q_masked"), ph.load("d8_ready"), ph.load("d8_used")
        block = ctx.enter_context(nc.Block())

        def tiles(eng, step):
            step(at(eng, 0))
            step(at(eng, 1))
            with eng.Fori(1, (NT - 1) // 2 - 1) as it:
                pair = Pair(eng, it)
                for k in range(2):
                    step(Turn(pair, k))
            for s in range(NT - 3, NT):
                step(at(eng, s))

        def number(t):
            return t.t if isinstance(t.pair.it, int) else None

        def is_sample(t):
            return number(t) == NT - 1

        @block.sync
        def _(sp):
            ph.grant(sp)
            sp.dma_start(gout[:, :, :], out_g[0].unsqueeze(0).unsqueeze(0).to_broadcast([P, BH, BV])
                         ).then_inc(const_in, 16)

            def step(t):
                n = SAMPLE if is_sample(t) else P
                sp.wait_ge(b_ready, t.back2)
                sp.wait_ge(scaled, t.back2)
                sp.dma_start(zf[0:n, t.p, 0:CL], Z[t.t][0:n, ZBQ:ZBV]).then_inc(zf_loaded[t.p], 16)
                sp.dma_start(zf[0:n, t.p, CL:ZF], Z[t.t][0:n, ZLA:ZW]).then_inc(zf_loaded[t.p], 16)
                sp.wait_ge(d_ready, t.back2)
                sp.wait_ge(gr_ready, t.back2)
                sp.wait_ge(o_ready, t.back2)
                sp.dma_start(zb[0:n, t.p, :], Z[t.t][0:n, ZBV:ZLA]).then_inc(zb_loaded[t.p], 16)

            tiles(sp, step)
            sp.wait_ge(consts, 2)
            for e in range(2):
                sp.dma_start(sts[e * BK:(e + 1) * BK, :, :, e * BV:(e + 1) * BV].rearrange("k b j v -> k (b j) v"),
                             state0[0].rearrange("b (j e) k v -> e k (b j) v", e=2)[e]).then_inc(state_in, 16)
            sp.wait_ge(st_ready, at(sp, NTP - 1).now)
            for e in range(2):
                sp.dma_start(new_prompt[0, 0].rearrange("(j e) k v -> e k j v", e=2)[e],
                             st[e * BK:(e + 1) * BK, :, e * BV:(e + 1) * BV]).then_inc(s_stored, 16)
            sp.wait_ge(d8_used, DEC_B)
            for e in range(2):
                sp.dma_start(new_sample[0].rearrange("b (j e) k v -> e k (b j) v", e=2)[e],
                             nst[e * BK:(e + 1) * BK, :, :, e * BV:(e + 1) * BV].rearrange("k b j v -> k (b j) v")
                             ).then_inc(s_stored, 16)
            sp.wait_ge(s_stored, 64)

        @block.gpsimd
        def _(pool):
            make_identity(pool, ident)
            for m in (tri, halves, same, cols8):
                pool.memset(m[tuple(slice(None) for _ in m.shape)], 1.0)
            pool.memset(cuts[:, :], 1.0)
            pool.memset(st[:, :, :], 0.0)
            pool.memset(sts[:, :, :, :], 0.0)
            pool.drain()
            pool.affine_select(out=tri[:, :], in_=tri[:, :], compare_op=ALU.is_ge, fill=0.0, base=0,
                               pattern=[[1, P]], channel_multiplier=-1)
            pool.affine_select(out=cuts[:, 0:1], in_=cuts[:, 0:1], compare_op=ALU.is_ge, fill=0.0,
                               base=P // 2 - 1, pattern=[[0, 1]], channel_multiplier=-1)
            pool.affine_select(out=cuts[:, 2:3], in_=cuts[:, 2:3], compare_op=ALU.is_ge, fill=0.0,
                               base=-P // 2, pattern=[[0, 1]], channel_multiplier=1)
            for e in range(2):
                pool.affine_select(out=halves[:, :, e, :], in_=halves[:, :, e, :], compare_op=ALU.is_ge, fill=0.0,
                                   base=(BK - 1) * (1 - e) - BK * e, pattern=[[0, NP], [0, BV]],
                                   channel_multiplier=2 * e - 1)
            for b0, b1, m in ((0, -DEC_T, 1), (DEC_T - 1, DEC_T, -1)):
                pool.affine_select(out=same[:, :, :], in_=same[:, :, :], compare_op=ALU.is_ge, fill=0.0, base=b0,
                                   pattern=[[b1, DEC_B], [0, DEC_T]], channel_multiplier=m)
                pool.affine_select(out=cols8[:, :, :], in_=cols8[:, :, :], compare_op=ALU.is_ge, fill=0.0, base=b0,
                                   pattern=[[b1, DEC_B], [m, SAMPLE]], channel_multiplier=0)
                pool.drain()
            pool.tensor_scalar(tric[:, :], tri[:, :], cuts[:, 0:1], None, ALU.subtract)
            pool.tensor_tensor(tri8[:, :], tri[0:SAMPLE, 0:SAMPLE], same[:, :, :].rearrange("s b t -> s (b t)"),
                               ALU.mult)
            pool.tensor_copy(seq1[:, :], same[:, :, 0])
            pool.drain()
            pool.sem_inc(consts, 2)
            pool.wait_ge(const_in, 16)

            def step(t):
                pool.wait_ge(zb_loaded[t.p], t.dma)
                pool.wait_ge(ob_ready, t.back2)
                pool.tensor_tensor(gr[:, t.p, :], zb[:, t.p, CR:CR + BVW],
                                   gout[:, :, :].rearrange("p h v -> p (h v)"), ALU.mult).then_inc(gr_ready, 1)

            all_steps(pool, NT, step)

        @block.scalar
        def _(act):
            act.wait_ge(consts, 1)

            def exps(t):
                n, w = (SAMPLE, DEC_B) if is_sample(t) else (P, 3)
                act.wait_ge(b_ready, t.now)
                act.wait_ge(scaled, t.back1)
                act.wait_ge(st_ready, t.back2)
                act.activation(eb[0:n, 0, :], b_ps[0:n, 0:BQK], ACT.Exp)
                act.activation(eb[0:n, 1, :], b_ps[0:n, 0:BQK], ACT.Exp, scale=-1.0)
                act.activation(ec[:, t.p, :, 0:w], c_ps[:, 0:NP * w].rearrange("p (j c) -> p j c", j=NP), ACT.Exp
                               ).then_inc(b_exp, 1)

            def take_qkT(t):
                n = SAMPLE if is_sample(t) else P
                act.wait_ge(qk_turned, t.now)
                act.wait_ge(o_ready, t.back1)
                act.activation(qkT[:, :, 0:n], qkT_ps[:, :].rearrange("p (j r) -> p j r", r=P)[:, :, 0:n], ACT.Copy
                               ).then_inc(qkT_ready, 1)

            def square(t):
                n = SAMPLE if is_sample(t) else P
                act.wait_ge(o_ready, t.now)
                act.wait_ge(o_summed, t.back1)
                act.activation(osq[0:n, :], o_ps[t.p][0:n, :], ACT.Square).then_inc(o_squared, 1)

            def store(t):
                n = SAMPLE if is_sample(t) else P
                act.wait_ge(ob_ready, t.now)
                act.dma_start(OB[t.t][0:n], ob[0:n, t.p, :]).then_inc(o_stored[t.p], 16)

            def step(t):
                if number(t) != 0:
                    square(t.prev)
                if not is_sample(t):
                    exps(t.next)
                    take_qkT(t.next)
                if number(t) != 0:
                    store(t.prev)

            exps(at(act, 0))
            take_qkT(at(act, 0))
            tiles(act, step)
            square(at(act, NT - 1))
            store(at(act, NT - 1))
            for p, n in enumerate(((NT + 1) // 2, NT // 2)):
                act.wait_ge(o_stored[p], 16 * n + 16)

        @block.vector
        def _(dve):
            dve.wait_ge(consts, 1)

            def scale_qk(t):
                n = SAMPLE if is_sample(t) else P
                dve.wait_ge(zf_loaded[t.p], t.dma2)
                dve.wait_ge(b_exp, t.now)
                dve.wait_ge(d_ready, t.back2)
                dve.wait_ge(qk_turned, t.back2)
                dve.scalar_tensor_tensor(qk[0:n, t.p, 0, :], zf[0:n, t.p, CQ:CQ + BQK], BK ** -0.5, eb[0:n, 0, :],
                                         ALU.mult, ALU.mult)
                dve.tensor_tensor(qk[0:n, t.p, 1, :], zf[0:n, t.p, CK:CK + BQK], eb[0:n, 1, :], ALU.mult
                                  ).then_inc(scaled, 1)

            def mask_att(t, n, mask):
                dve.wait_ge(att_ready, t.now)
                dve.wait_ge(o_ready, t.back1)
                for e in range(2):
                    ins = dve.tensor_tensor(att[0:n, e:BH:2, 0:n],
                                            att_ps[e][0:n, 0:2 * P].rearrange("s (j t) -> s j t", j=NP)[:, :, 0:n],
                                            mask.unsqueeze(1).to_broadcast([n, NP, n]), ALU.mult)
                ins.then_inc(att_masked, 1)

            def outputs(t, n):
                dve.wait_ge(o_squared, t.now)
                dve.tensor_reduce(oss[0:n, :], osq[0:n, :].rearrange("p (h v) -> p h v", v=BV), AX.X, ALU.add
                                  ).then_inc(o_summed, 1)
                dve.drain()
                inverse_rms(dve, ors[0:n, :], oss[0:n, :], BV, (tmp[0:n, 0, :], tmp[0:n, 1, :]))
                dve.drain()
                dve.tensor_tensor(o1[0:n, :].rearrange("p (h v) -> p h v", v=BV),
                                  o_ps[t.p][0:n, :].rearrange("p (h v) -> p h v", v=BV), across(ors[0:n, :], BV), ALU.mult)
                dve.drain()
                dve.wait_ge(gr_ready, t.now)
                dve.wait_ge(o_stored[t.p], t.dma)
                dve.tensor_tensor(ob[0:n, t.p, :], o1[0:n, :], gr[0:n, t.p, :], ALU.mult).then_inc(ob_ready, 1)

            def step(t):
                if is_sample(t):
                    outputs(t.prev, P)
                    dve.drain()
                    sample(t)
                    return
                e = ec[:, t.p, :, :]
                dve.wait_ge(b_exp, t.now)
                dve.wait_ge(o_ready, t.back1)
                dve.tensor_tensor(sc[:, :, :], st[:, :, :], e[:, :, 0:1].to_broadcast([P, NP, VW]), ALU.mult
                                  ).then_inc(sc_ready, 1)
                mask_att(t, P, tri[:, :])
                scale_qk(t.next)
                dve.wait_ge(d_ready, t.now)
                dve.tensor_tensor(dm[:, :, :], d_ps[:, :].rearrange("p (j v) -> p j v", j=NP),
                                  halves[:, :, :, :].rearrange("p j e v -> p j (e v)"), ALU.mult)
                dve.drain()
                dve.tensor_tensor(dm[:, :, :], dm[:, :, :], e[:, :, 2:3].to_broadcast([P, NP, VW]), ALU.mult)
                for j in range(NP):
                    if j == 0:
                        dve.drain()
                    ins = dve.scalar_tensor_tensor(st[:, j, :], st[:, j, :], e[:, j, 1:2], dm[:, j, :],
                                                   ALU.mult, ALU.add)
                ins.then_inc(st_ready, 1)
                if number(t) != 0:
                    outputs(t.prev, P)
                dve.drain()

            def sample(t):
                for b in range(DEC_B):
                    dve.tensor_scalar(km[:, b, :], qk[0:SAMPLE, t.p, 1, :], seq1[:, b:b + 1], None, ALU.mult)
                dve.wait_ge(qkT_ready, t.now)
                for j in range(NP):
                    ins = dve.tensor_tensor(qTm[:, j, :, :], cols8[:, :, :],
                                            qkT[:, j, 0:SAMPLE].unsqueeze(1).to_broadcast([P, DEC_B, SAMPLE]),
                                            ALU.mult)
                ins.then_inc(q_masked, 1)
                mask_att(t, SAMPLE, tri8[:, :])
                dve.wait_ge(state_in, 32)
                for b in range(DEC_B):
                    d = (dm, sc)[b % 2]
                    dve.wait_ge(d8_ready, b + 1)
                    dve.tensor_tensor(d[:, :, :], (d_ps, b_ps)[b % 2][:, :].rearrange("p (j v) -> p j v", j=NP),
                                      halves[:, :, :, :].rearrange("p j e v -> p j (e v)"), ALU.mult)
                    dve.drain()
                    dve.tensor_tensor(d[:, :, :], d[:, :, :], sts[:, b, :, :], ALU.add)
                    dve.drain()
                    dve.tensor_tensor(nst[:, b, :, :], d[:, :, :], ec[:, t.p, :, b:b + 1].to_broadcast([P, NP, VW]),
                                      ALU.mult).then_inc(d8_used, 1)
                outputs(t, SAMPLE)

            scale_qk(at(dve, 0))
            tiles(dve, step)

        @block.tensor
        def _(pe):
            pe.wait_ge(consts, 1)

            def sums(t):
                n, m, cut = (SAMPLE, tri8[:, :], seq1[:, :]) if is_sample(t) else (P, tric[:, :], cuts[:, :])
                la = zf[0:n, t.p, CL:CL + BQK]
                pe.wait_ge(zf_loaded[t.p], t.dma2)
                pe.wait_ge(b_exp, t.back1)
                pe.matmul(b_ps[0:n, 0:BQK], m, la, start=True, stop=True)
                w = cut.shape[1]
                for j in range(NP):
                    ins = pe.matmul(c_ps[:, j * w:(j + 1) * w], la[:, j * P:(j + 1) * P], cut, start=True, stop=True)
                ins.then_inc(b_ready, 1)

            def turn_qk(t):
                n = SAMPLE if is_sample(t) else P
                pe.wait_ge(scaled, t.now)
                pe.wait_ge(qkT_ready, t.back1)
                for j in range(2 * NP):
                    ins = pe.transpose(qkT_ps[:, j * P:j * P + n], qk[0:n, t.p, j // NP, (j % NP) * P:(j % NP + 1) * P],
                                       ident[0:n, 0:n])
                ins.then_inc(qk_turned, 1)

            def scores(t, n):
                pe.wait_ge(qkT_ready, t.now)
                pe.wait_ge(att_masked, t.back1)
                for h in range(BH):
                    lo, j = h % 2 * BK, h // 2
                    ins = pe.matmul(att_ps[h % 2][0:n, j * P:j * P + n], qkT[lo:lo + BK, NP + j, 0:n],
                                    qkT[lo:lo + BK, j, 0:n], start=True, stop=True)
                ins.then_inc(att_ready, 1)

            def step(t):
                if is_sample(t):
                    sample(t)
                    return
                p = t.p
                sums(t.next)
                pe.wait_ge(zb_loaded[p], t.dma)
                pe.wait_ge(st_ready, t.back1)
                for j in range(NP):
                    ins = pe.matmul(d_ps[:, j * VW:(j + 1) * VW], qk[:, p, 1, j * P:(j + 1) * P],
                                    zb[:, p, CV + j * VW:CV + (j + 1) * VW], start=True, stop=True)
                ins.then_inc(d_ready, 1)
                scores(t, P)
                pe.wait_ge(sc_ready, t.now)
                pe.wait_ge(att_masked, t.now)
                pe.wait_ge(ob_ready, t.back2)
                for j in range(NP):
                    pe.matmul(o_ps[p][:, j * VW:(j + 1) * VW], qkT[:, j, :], sc[:, j, :], start=True, stop=False,
                              skip_group_check=True)
                    for e in range(2):
                        h = 2 * j + e
                        ins = pe.matmul(o_ps[p][:, h * BV:(h + 1) * BV], att[:, h, :],
                                        zb[:, p, CV + h * BV:CV + (h + 1) * BV], start=False, stop=True,
                                        skip_group_check=True)
                ins.then_inc(o_ready, 1)
                turn_qk(t.next)

            def sample(t):
                p, n = t.p, SAMPLE
                scores(t, n)
                pe.wait_ge(zb_loaded[p], t.dma)
                pe.wait_ge(q_masked, 1)
                pe.wait_ge(b_exp, t.now)
                pe.wait_ge(st_ready, t.back1)
                for b in range(DEC_B):
                    if b >= 2:
                        pe.wait_ge(d8_used, b - 1)
                    for j in range(NP):
                        ins = pe.matmul((d_ps, b_ps)[b % 2][:, j * VW:(j + 1) * VW], km[:, b, j * P:(j + 1) * P],
                                        zb[0:n, p, CV + j * VW:CV + (j + 1) * VW], start=True, stop=True)
                    ins.then_inc(d8_ready, 1)
                pe.wait_ge(state_in, 32)
                pe.wait_ge(att_masked, t.now)
                pe.wait_ge(ob_ready, t.back2)
                for j in range(NP):
                    for b in range(DEC_B):
                        pe.matmul(o_ps[p][0:n, j * VW:(j + 1) * VW], qTm[:, j, b, :], sts[:, b, j, :],
                                  start=(b == 0), stop=False, skip_group_check=True)
                    for e in range(2):
                        h = 2 * j + e
                        ins = pe.matmul(o_ps[p][0:n, h * BV:(h + 1) * BV], att[0:n, h, 0:n],
                                        zb[0:n, p, CV + h * BV:CV + (h + 1) * BV], start=False, stop=True,
                                        skip_group_check=True)
                ins.then_inc(o_ready, 1)

            sums(at(pe, 0))
            turn_qk(at(pe, 0))
            tiles(pe, step)


def dilated_sample(nc, Z, cache_k, cache_v, OAS):
    SCALE = AD ** -0.5
    NTL = 11
    CT = 10 * P
    NK = CT + DEC_T
    R = AH * DEC_T
    F0 = WBUF - 512
    with ExitStack() as ctx:
        ph = Phase(nc, ctx, "ds")
        ident = ph.sb("ident", [P, P])
        dist_i = ph.sb("dist_i", [R, NK], I32)
        tok_i = ph.sb("tok_i", [R, 1], I32)
        tok_f = ph.sb("tok_f", [R, 1])
        low_i = ph.sb("low_i", [R, NK], I32)
        dist = ph.sb("dist", [R, NK])
        past = ph.sb("past", [R, NK])
        part = ph.sb("part", [R, NK])
        mult = ph.sb("mult", [R, NK])
        bias = ph.sb("bias", [R, NK])
        diag = ph.sb("diag", [R, AH, AD])
        pick = ph.sb("pick", [R, DEC_T])
        tok8 = ph.sb("tok8", [R, DEC_T])
        new = ph.sb("new", [DEC_T, 2, 3 * AW])
        k_sb = ph.sb("k", [P, 2, 10, AW])
        v_sb = ph.sb("v", [P, 2, 10, AW])
        kT = ph.sb("kT", [P, 4, NK])
        qbd = ph.sb("qbd", [P, 4 * 80])
        sm = ph.sb("sm", [R, NK])
        pr = ph.sb("pr", [R, NK])
        stat = ph.sb("stat", [R, 4])
        pT = ph.sb("pT", [P, NTL, R])
        o_sb = ph.sb("o", [R, AW])
        out = ph.sb("out", [DEC_T, 2, AW])
        t_ps = [ph.ps(f"tps{i}") for i in range(2)]
        s_ps = ph.ps("sps", 1536)
        pT_ps = ph.ps("pTps", 1024)
        o_ps = ph.ps("ops")

        consts = ph.load("consts")
        new_loaded, k_loaded, v_loaded = ph.loads("new_loaded"), ph.loads("k_loaded"), ph.loads("v_loaded")
        out_stored = ph.stores("out_stored")
        q_turned, q_taken = ph.event("q_turned"), ph.event("q_taken")
        k_turned = [ph.event(f"k_turned{i}") for i in range(2)]
        k_taken = [ph.event(f"k_taken{i}") for i in range(2)]
        scored, masked, max_ready, exps_done, p_ready = (ph.event(n) for n in (
            "scored", "masked", "max_ready", "exps_done", "p_ready"))
        p_turned, pT_ready, o_ready, o_scaled, out_ready, out_taken = (ph.event(n) for n in (
            "p_turned", "pT_ready", "o_ready", "o_scaled", "out_ready", "out_taken"))
        block = ctx.enter_context(nc.Block())

        @block.sync
        def _(sp):
            ph.grant(sp)
            Zs = Z[NT - 1]

            def step(t):
                p = t.p
                sp.wait_ge(o_ready, t.back2)
                for src, dst, loaded in ((cache_k, k_sb, k_loaded), (cache_v, v_sb, v_loaded)):
                    rows = src[0][bass.ds(t.t, 1)].rearrange("o (p c) h d -> p (o c) (h d)", c=16)
                    sp.dma_start(dst[:, p, 0:8, :], rows[:, 0:8, :]).then_inc(loaded[p], 16)
                    late = rows[F0 // 16:P, 8:16, :].rearrange("p (u i) n -> i p u n", i=4)
                    for i in range(4):
                        sp.dma_start(dst[32 * i:32 * i + 32, p, 8:10, :], late[i]).then_inc(loaded[p], 16)
                    if src is cache_k:
                        sp.dma_start(new[:, p, :], Zs[bass.ds(t.t * DEC_T, DEC_T), 0:3 * AW]
                                     ).then_inc(new_loaded[p], 16)

            all_steps(sp, DEC_B, step)

        @block.gpsimd
        def _(pool):
            make_identity(pool, ident)
            pool.memset(qbd[:, :], 0.0)
            pool.memset(diag[:, :, :], 1.0)
            pool.iota(dist_i[:, 0:8 * P], [[-1, 8], [-16, P]], base=WBUF, channel_multiplier=0)
            pool.iota(dist_i[:, 8 * P:CT], [[-4, 2], [-1, 4], [-16, 32]], base=WBUF - F0 - 8, channel_multiplier=0)
            pool.iota(dist_i[:, CT:NK], [[-1, DEC_T]], base=0, channel_multiplier=0)
            pool.iota(tok_i[:, :], [[0, 1]], base=0, channel_multiplier=1)
            pool.iota(tok8[:, :], [[1, DEC_T]], base=0, channel_multiplier=0, allow_small_or_imprecise_dtypes=True)
            pool.drain()
            for b0, b1, m in ((0, -DEC_T, 1), (DEC_T - 1, DEC_T, -1)):
                pool.affine_select(out=diag[:, :, :], in_=diag[:, :, :], compare_op=ALU.is_ge, fill=0.0, base=b0,
                                   pattern=[[b1, AH], [0, AD]], channel_multiplier=m)
                pool.drain()
            pool.sem_inc(consts, 1)

        @block.scalar
        def _(act):
            def step(t):
                p = t.p
                for k in range(6):
                    w = P if k < 5 else DEC_T
                    act.wait_ge(k_turned[0], t.of(6, k))
                    if k == 0:
                        act.wait_ge(scored, t.back1)
                    act.activation(kT[:, :, 2 * k * P:2 * k * P + w],
                                   t_ps[0][:, :].rearrange("p (j r) -> p j r", j=4)[:, :, 0:w], ACT.Copy
                                   ).then_inc(k_taken[0], 1)
                act.wait_ge(max_ready, t.now)
                act.activation(pr[:, :], sm[:, :], ACT.Exp, bias=stat[:, 1:2], scale=SCALE).then_inc(exps_done, 1)
                act.wait_ge(out_ready, t.now)
                act.wait_ge(out_stored[p], t.dma)
                act.activation(out[:, p, :], t_ps[1][0:DEC_T, :], ACT.Copy).then_inc(out_taken, 1)
                act.wait_ge(out_taken, t.now)
                act.dma_start(OAS[bass.ds(t.t * DEC_T, DEC_T), :], out[:, p, :]).then_inc(out_stored[p], 16)

            all_steps(act, DEC_B, step)
            for p in range(2):
                act.wait_ge(out_stored[p], 16 * (DEC_B // 2) + 16)

        @block.vector
        def _(dve):
            dve.wait_ge(consts, 1)
            dve.tensor_scalar(tok_i[:, :], tok_i[:, :], DEC_T - 1, None, ALU.bitwise_and)
            dve.drain()
            dve.tensor_copy(tok_f[:, :], tok_i[:, :])
            dve.drain()
            dve.tensor_scalar(dist[:, :], dist_i[:, :], tok_f[:, :], None, ALU.add)
            dve.tensor_scalar(pick[:, :], tok8[:, :], tok_f[:, :], None, ALU.is_equal)
            dve.drain()
            dve.tensor_copy(dist_i[:, :], dist[:, :])
            dve.tensor_scalar(past[:, :], dist[:, :], 0.0, None, ALU.is_ge)
            dve.drain()
            for g, (window, dil) in enumerate(GROUPS):
                if dil > 1:
                    dve.tensor_scalar(low_i[:, :], dist_i[:, :], dil - 1, None, ALU.bitwise_and)
                    dve.drain()
                    dve.tensor_copy(part[:, :], low_i[:, :])
                    dve.drain()
                    dve.tensor_scalar(part[:, :], part[:, :], 0.0, None, ALU.is_equal)
                    dve.drain()
                    dve.scalar_tensor_tensor(part[:, :], dist[:, :], float(window), part[:, :], ALU.is_le, ALU.mult)
                    dve.drain()
                    dve.tensor_tensor(mult[:, :], mult[:, :], part[:, :], ALU.add)
                else:
                    dve.tensor_scalar(mult[:, :], dist[:, :], float(window), None, ALU.is_le)
                dve.drain()
            dve.tensor_tensor(mult[:, :], mult[:, :], past[:, :], ALU.mult)
            dve.drain()
            dve.tensor_scalar(bias[:, :], mult[:, :], 0.0, NEG, ALU.is_equal, ALU.mult)
            dve.drain()

            def step(t):
                p = t.p
                dve.wait_ge(q_turned, t.now)
                dve.wait_ge(scored, t.back1)
                for e in range(2):
                    ins = dve.tensor_copy(
                        qbd[e * AD:(e + 1) * AD, :].rearrange("p (j x) -> p j x", x=80)[:, :, e * 8:e * 8 + 8],
                        pT_ps[e * AD:(e + 1) * AD, 0:4 * DEC_T].rearrange("p (j x) -> p j x", x=DEC_T))
                ins.then_inc(q_taken, 1)
                for k in range(5):
                    dve.wait_ge(k_turned[1], t.of(5, k))
                    dve.tensor_copy(kT[:, :, (2 * k + 1) * P:(2 * k + 2) * P],
                                    t_ps[1][:, :].rearrange("p (j r) -> p j r", j=4)).then_inc(k_taken[1], 1)
                dve.wait_ge(scored, t.now)
                dve.wait_ge(exps_done, t.back1)
                dve.tensor_tensor(sm[:, :], s_ps[0:R, 0:NK], bias[:, :], ALU.add).then_inc(masked, 1)
                dve.drain()
                dve.tensor_reduce(stat[:, 0:1], sm[:, :], AX.X, ALU.max)
                dve.drain()
                dve.tensor_scalar(stat[:, 1:2], stat[:, 0:1], -SCALE, None, ALU.mult).then_inc(max_ready, 1)
                dve.wait_ge(exps_done, t.now)
                dve.scalar_tensor_tensor(pr[:, :], pr[:, :], 1.0, mult[:, :], ALU.mult, ALU.mult,
                                         accum_out=stat[:, 2:3]).then_inc(p_ready, 1)
                dve.drain()
                dve.reciprocal(stat[:, 3:4], stat[:, 2:3])
                dve.wait_ge(p_turned, t.now)
                dve.tensor_copy(pT[:, 0:10, :], pT_ps[:, 0:10 * R].rearrange("p (c r) -> p c r", r=R))
                dve.tensor_copy(pT[0:DEC_T, 10, :], pT_ps[0:DEC_T, 10 * R:11 * R]).then_inc(pT_ready, 1)
                dve.drain()
                dve.wait_ge(o_ready, t.now)
                dve.scalar_tensor_tensor(o_sb[:, :], o_ps[0:R, :], stat[:, 3:4],
                                         diag[:, :, :].rearrange("r h d -> r (h d)"), ALU.mult, ALU.mult
                                         ).then_inc(o_scaled, 1)

            all_steps(dve, DEC_B, step)

        @block.tensor
        def _(pe):
            pe.wait_ge(consts, 1)

            def step(t):
                p = t.p
                pe.wait_ge(new_loaded[p], t.dma)
                pe.wait_ge(pT_ready, t.back1)
                pe.wait_ge(k_loaded[p], t.dma5)
                pe.wait_ge(out_taken, t.back1)
                for c in range(NTL):
                    half, k = c % 2, c // 2
                    if c < 10:
                        pe.wait_ge(k_taken[half], t.of(6 - half, k - 1))
                    if c == 9:
                        pe.wait_ge(k_taken[0], t.of(6, 4))
                    for j in range(4):
                        if c < 10:
                            ins = pe.transpose(t_ps[half][:, j * P:(j + 1) * P], k_sb[:, p, c, j * P:(j + 1) * P],
                                               ident[:, :])
                        else:
                            ins = pe.transpose(t_ps[half][:, j * P:j * P + DEC_T],
                                               new[:, p, AW + j * P:AW + (j + 1) * P], ident[0:DEC_T, 0:DEC_T])
                    ins.then_inc(k_turned[half], 1)
                    if c == 0:
                        for j in range(4):
                            ins = pe.transpose(pT_ps[:, j * DEC_T:(j + 1) * DEC_T], new[:, p, j * P:(j + 1) * P],
                                               ident[0:DEC_T, 0:DEC_T])
                        ins.then_inc(q_turned, 1)
                pe.wait_ge(q_taken, t.now)
                pe.wait_ge(masked, t.back1)
                for lo, hi, a, b in ((0, 512, t.of(6, 1), t.of(5, 1)), (512, 1024, t.of(6, 3), t.of(5, 3)),
                                     (1024, NK, t.of(6, 5), t.of(5, 4))):
                    pe.wait_ge(k_taken[0], a)
                    pe.wait_ge(k_taken[1], b)
                    for j in range(4):
                        ins = pe.matmul(s_ps[0:R, lo:hi], qbd[:, j * R:(j + 1) * R], kT[:, j, lo:hi],
                                        start=(j == 0), stop=(j == 3))
                ins.then_inc(scored, 1)
                pe.wait_ge(consts, 1)
                pe.wait_ge(p_ready, t.now)
                for c in range(10):
                    pe.transpose(pT_ps[:, c * R:(c + 1) * R], pr[:, c * P:(c + 1) * P], ident[0:R, 0:R])
                pe.transpose(pT_ps[0:DEC_T, 10 * R:11 * R], pr[:, CT:NK], ident[0:R, 0:R]).then_inc(p_turned, 1)
                pe.wait_ge(pT_ready, t.now)
                pe.wait_ge(v_loaded[p], t.dma5)
                for c in range(10):
                    pe.matmul(o_ps[0:R, :], pT[:, c, :], v_sb[:, p, c, :], start=(c == 0), stop=False)
                pe.matmul(o_ps[0:R, :], pT[0:DEC_T, 10, :], new[:, p, 2 * AW:3 * AW], start=False, stop=True
                          ).then_inc(o_ready, 1)
                pe.wait_ge(consts, 1)
                pe.wait_ge(o_scaled, t.now)
                pe.matmul(t_ps[1][0:DEC_T, :], pick[:, :], o_sb[:, :], start=True, stop=True).then_inc(out_ready, 1)

            all_steps(pe, DEC_B, step)


def memory_kv(nc, mem, mem_g, w_k, w_v, k_g, new_k, new_v):
    NM = NMEM // P
    with ExitStack() as ctx:
        ph = Phase(nc, ctx, "mk")
        ident = ph.sb("ident", [P, P])
        gc = ph.sb("gc", [P, KD])
        kg = ph.sb("kg", [P, MH, MD])
        w = [ph.sb(f"w{i}", [P, KD, MW]) for i in range(2)]
        x = ph.sb("x", [P, NM, D])
        sq = ph.sb("sq", [P, D])
        tmp = ph.sb("tmp", [P, 2, MH])
        ss = ph.sb("ss", [P, NM, 2])
        xs = ph.sb("xs", [P, NM, D])
        xT = ph.sb("xT", [P, NM, KD, P])
        hs = ph.sb("hs", [P, NM, 2, MH])
        y = ph.sb("y", [P, NM, 2, MW])
        xT_ps = [ph.ps(f"xTps{i}", 1024) for i in range(NM)]
        y_ps = [[ph.ps(f"yps{i}{m}") for i in range(2)] for m in range(NM)]
        loaded, w_loaded, consts, stored = (ph.load(n) for n in ("loaded", "w_loaded", "consts", "stored"))
        x_summed, scaled, turned, xT_ready, projected, squared, summed, k_done, v_done = (
            ph.load(n) for n in ("x_summed", "scaled", "turned", "xT_ready", "projected", "squared", "summed",
                                 "k_done", "v_done"))
        block = ctx.enter_context(nc.Block())

        @block.sync
        def _(sp):
            sp.dma_start(x[:, :, :], mem[0].rearrange("(m p) d -> p m d", p=P)).then_inc(loaded, 16)
            sp.dma_start(gc[:, :], mem_g[0].rearrange("(k p) -> p k", p=P), allow_slow_non_contiguous=True
                         ).then_inc(loaded, 16)
            sp.dma_start(kg[:, :, :], k_g[0].unsqueeze(0).unsqueeze(0).to_broadcast([P, MH, MD])).then_inc(loaded, 16)
            for i, src in enumerate((w_k, w_v)):
                sp.dma_start(w[i][:, :, :], src[0].rearrange("(k p) n -> p k n", p=P)).then_inc(w_loaded, 16)
            for m in range(NM):
                for i, (done, out) in enumerate(((k_done, new_k), (v_done, new_v))):
                    sp.wait_ge(done, m + 1)
                    sp.dma_start(out[0, 0].rearrange("(m p) h d -> m p (h d)", p=P)[m], y[:, m, i, :]
                                 ).then_inc(stored, 16)
            sp.wait_ge(stored, 64)

        @block.gpsimd
        def _(pool):
            make_identity(pool, ident)
            pool.drain()
            pool.sem_inc(consts, 1)

        @block.scalar
        def _(act):
            act.wait_ge(consts, 1)
            act.wait_ge(loaded, 48)
            for m in range(NM):
                act.drain()
                act.activation(sq[:, :], x[:, m, :], ACT.Square, accum_out=ss[:, m, 0:1]).then_inc(x_summed, 1)
            for m in range(NM):
                act.wait_ge(projected, m + 1)
                if m:
                    act.wait_ge(summed, m)
                act.activation(sq[:, 0:MW], y_ps[m][0][:, :], ACT.Square).then_inc(squared, 1)
                act.activation(y[:, m, 1, :], y_ps[m][1][:, :], ACT.Copy).then_inc(v_done, 1)

        @block.vector
        def _(dve):
            for m in range(NM):
                dve.wait_ge(x_summed, m + 1)
                inverse_rms(dve, ss[:, m, 1:2], ss[:, m, 0:1], D, (tmp[:, 0, 0:1], tmp[:, 1, 0:1]))
                dve.drain()
                dve.tensor_scalar(xs[:, m, :], x[:, m, :], ss[:, m, 1:2], None, ALU.mult).then_inc(scaled, 1)
            for m in range(NM):
                dve.wait_ge(turned, m + 1)
                dve.tensor_tensor(xT[:, m, :, :], xT_ps[m][:, :].rearrange("p (k r) -> p k r", r=P),
                                  across(gc[:, :], P), ALU.mult).then_inc(xT_ready, 1)
            for m in range(NM):
                dve.wait_ge(squared, m + 1)
                dve.tensor_reduce(hs[:, m, 0, :], sq[:, 0:MW].rearrange("p (h d) -> p h d", d=MD), AX.X, ALU.add
                                  ).then_inc(summed, 1)
                dve.drain()
                inverse_rms(dve, hs[:, m, 1, :], hs[:, m, 0, :], MD, (tmp[:, 0, :], tmp[:, 1, :]))
                dve.drain()
                k = y[:, m, 0, :].rearrange("p (h d) -> p h d", d=MD)
                dve.tensor_tensor(k, y_ps[m][0][:, :].rearrange("p (h d) -> p h d", d=MD),
                                  across(hs[:, m, 1, :], MD), ALU.mult)
                dve.drain()
                dve.tensor_tensor(k, k, kg[:, :, :], ALU.mult).then_inc(k_done, 1)

        @block.tensor
        def _(pe):
            pe.wait_ge(consts, 1)
            for m in range(NM):
                pe.wait_ge(scaled, m + 1)
                for k in range(KD):
                    ins = pe.transpose(xT_ps[m][:, k * P:(k + 1) * P], xs[:, m, k * P:(k + 1) * P], ident[:, :])
                ins.then_inc(turned, 1)
            pe.wait_ge(w_loaded, 32)
            for m in range(NM):
                pe.wait_ge(xT_ready, m + 1)
                for i in range(2):
                    for k in range(KD):
                        ins = pe.matmul(y_ps[m][i][:, :], xT[:, m, k, :], w[i][:, k, :], start=(k == 0),
                                        stop=(k == KD - 1))
                ins.then_inc(projected, 1)


def mix_attend_route(nc, x_prompt, x_sample, U, OB, OAS, w_out, norm2_g, w_q, q_g, w_o, norm3_g, router_w, router_b,
                     mem_k, mem_v, cache_k, cache_v, H, XN, RT):
    SCALE = MD ** -0.5
    NC = NMEM // P
    with ExitStack() as ctx:
        ph = Phase(nc, ctx, "mx")
        ident = ph.sb("ident", [P, P])
        tmp = ph.sb("tmp", [P, 2, MH])
        wo_sb = ph.sb("wout", [P, KD, D])
        wq_sb = ph.sb("wq", [P, KD, MW])
        wm_sb = ph.sb("wm", [P, MH, D])
        wr_sb = ph.sb("wr", [P, KD, NE])
        g2c, g3c = ph.sb("g2c", [P, KD]), ph.sb("g3c", [P, KD])
        qg = ph.sb("qg", [P, MH, MD])
        rb = ph.sb("rb", [P, NE])
        kv = ph.sb("kv", [P, 2, NC, MW])
        vs = ph.sb("vs", [P, 2, NC, MW])
        kT = ph.sb("kT", [P, MH, NMEM])
        seq = ph.sb("seq", [SAMPLE, DEC_B])
        u = ph.sb("u", [P, 2, 3, UW])
        wt = ph.sb("wt", [P, 8, AH])
        t1 = ph.sb("t1", [P, 2, AW])
        cat = ph.sb("cat", [P, 2, D])
        catT = ph.sb("catT", [P, KD, P])
        x_sb = ph.sb("x", [P, 2, D])
        h = ph.sb("h", [P, 2, D])
        h2 = ph.sb("h2", [P, 2, D])
        sq = ph.sb("sq", [P, D])
        qsq = ph.sb("qsq", [P, MW])
        ss = ph.sb("ss", [P, 4])
        hs = ph.sb("hs", [P, D])
        hT = ph.sb("hT", [P, KD, P])
        qss = ph.sb("qss", [P, 2, MH])
        q = ph.sb("q", [P, 2, MW])
        qT = ph.sb("qT", [P, MH, P])
        sst = ph.sb("sst", [P, 4, MH])
        pr = ph.sb("pr", [P, MH, NMEM])
        pT = ph.sb("pT", [P, MH, NC, P])
        oT = ph.sb("oT", [P, MH, P])
        xn = ph.sb("xn", [P, 2, D])
        xT = ph.sb("xT", [P, KD, P])
        lg = ph.sb("lg", [P, NE])
        top = ph.sb("top", [P, 8])
        tix = ph.sb("tix", [P, 8], U32)
        gt = ph.sb("gt", [P, 8])
        rt = ph.sb("rt", [P, 2, 8])
        zeros = ph.sb("zeros", [P, 512])
        t_ps = [ph.ps(f"tps{i}") for i in range(2)]
        y_ps = ph.ps("yps", 1024)
        s_ps = ph.ps("sps", 1024)
        q_ps = ph.ps("qps")
        m_ps = ph.ps("mps")

        mk_turned, mk_ready = ph.load("mk_turned"), ph.load("mk_ready")
        const_in, w_loaded, consts, mem_in = (ph.load(n) for n in ("const_in", "w_loaded", "consts", "mem_in"))
        in_loaded, b_loaded = ph.loads("in_loaded"), ph.loads("b_loaded")
        rt_stored, h_stored, xn_stored = ph.stores("rt_stored"), ph.stores("h_stored"), ph.stores("xn_stored")
        ev = {n: ph.event(n) for n in (
            "weights", "weights_exp", "cat_ready", "cat_turned", "catT0", "catT1", "y_ready", "h_ready",
            "h_summed", "hs_ready", "h_turned", "hT_ready", "h_kept", "q_ready", "q_squared", "q_summed", 
            "q_scaled", "q_done", "q_turned", "qT_ready", "scored", "max_ready", "exps_done", "p_ready", "p_turned",
            "pT0", "pT1", "o_ready", "oT_ready", "yo_ready", "h2_ready", "h2_summed", "xn_ready", "x_turned",
            "xT_ready", "lg_ready", "lg_taken", "top_ready", "gates_exp", "rt_ready")}
        sq_ev = {n: ph.event("s_" + n) for n in ("k_turned", "kT_ready", "scored", "max_ready", "exps_done",
                                                 "p_ready", "p_turned", "pT_ready", "o_ready")}
        block = ctx.enter_context(nc.Block())

        def steps(eng, step):
            step(at(eng, 0), True, False, False, False)
            step(at(eng, 1), True, True, False, False)
            step(at(eng, 2), True, True, True, False)
            step(at(eng, 3), True, True, True, True)
            with eng.Fori(2, (NT - 1) // 2 - 1) as it:
                pair = Pair(eng, it)
                for k in range(2):
                    step(Turn(pair, k), True, True, True, True)
            for s in range(NT - 3, NT):
                step(at(eng, s), True, True, True, True)
            step(at(eng, NT), False, True, True, True)
            step(at(eng, NT + 1), False, False, True, True)
            step(at(eng, NT + 2), False, False, False, True)

        def is_sample(t):
            return isinstance(t.pair.it, int) and t.t == NT - 1

        @block.sync
        def _(sp):
            ph.grant(sp)
            sp.dma_start(qg[:, :, :], q_g[0].unsqueeze(0).unsqueeze(0).to_broadcast([P, MH, MD])).then_inc(const_in, 16)
            sp.dma_start(rb[:, :], router_b[0].unsqueeze(0).to_broadcast([P, NE])).then_inc(const_in, 16)
            for g, col in ((norm2_g, g2c), (norm3_g, g3c)):
                sp.dma_start(col[:, :], g[0].rearrange("(k p) -> p k", p=P), allow_slow_non_contiguous=True
                             ).then_inc(const_in, 16)

            xr = x_prompt[0].rearrange("(t r) d -> t r d", r=P)
            Ur = [m.rearrange("(t r) w -> t r w", r=P) for m in U]

            def load(t):
                sp.wait_ge(ev["cat_turned"], t.back2)
                for g in range(3):
                    sp.dma_start(u[:, t.p, g, :], Ur[g][t.t]).then_inc(in_loaded[t.p], 16)
                sp.dma_start(cat[:, t.p, AW:D], OB[t.t]).then_inc(in_loaded[t.p], 16)
                sp.wait_ge(ev["h_ready"], t.back2)
                sp.dma_start(x_sb[:, t.p, :], xr[t.t]).then_inc(in_loaded[t.p], 16)

            with sp.Fori(0, (NT - 1) // 2) as it:
                pair = Pair(sp, it)
                for k in range(2):
                    load(Turn(pair, k))
            t = at(sp, NT - 1)
            sp.wait_ge(ev["cat_turned"], t.back2)
            sp.wait_ge(ev["h_ready"], t.back2)
            sp.dma_start(cat[0:SAMPLE, 0, 0:AW], OAS).then_inc(in_loaded[0], 16)
            sp.dma_start(cat[0:SAMPLE, 0, AW:D], OB[NT - 1][0:SAMPLE]).then_inc(in_loaded[0], 16)
            sp.dma_start(x_sb[0:SAMPLE, 0, :], x_sample.rearrange("b t d -> (b t) d")).then_inc(in_loaded[0], 16)
            sp.wait_ge(ev["o_ready"], at(sp, NT - 2).now)
            with sp.Fori(0, DEC_B // 2) as it:
                pair = Pair(sp, it)
                for k in range(2):
                    b = Turn(pair, k)
                    sp.wait_ge(sq_ev["o_ready"], b.back2)
                    for src, dst in ((cache_k, kv), (cache_v, vs)):
                        sp.dma_start(dst[:, b.p, :, :], src[0][b.t].rearrange("(c p) h d -> p c (h d)", p=P)
                                     ).then_inc(b_loaded[b.p], 16)

        @block.gpsimd
        def _(pool):
            make_identity(pool, ident)
            pool.memset(seq[:, :], 1.0)
            pool.memset(zeros[:, :], 0.0)
            pool.drain()
            for b0, b1, m in ((0, -DEC_T, 1), (DEC_T - 1, DEC_T, -1)):
                pool.affine_select(out=seq[:, :], in_=seq[:, :], compare_op=ALU.is_ge, fill=0.0, base=b0,
                                   pattern=[[b1, DEC_B]], channel_multiplier=m)
                pool.drain()
            pool.sem_inc(consts, 1)
            pool.wait_ge(const_in, 4 * 16)

            def step(s, a, b, c, d):
                if b:
                    t = s.prev
                    pool.wait_ge(h_stored[t.p], t.dma)
                    pool.wait_ge(ev["xn_ready"], t.back2)
                    pool.wait_ge(ev["h_ready"], t.now)
                    pool.wait_ge(ev["q_scaled"], t.now)
                    pool.tensor_tensor(q[:, t.p, :], q[:, t.p, :], qg[:, :, :].rearrange("p h d -> p (h d)"),
                                       ALU.mult).then_inc(ev["q_done"], 1)
                    pool.tensor_copy(h2[:, t.p, :], h[:, t.p, :]).then_inc(ev["h_kept"], 1)

            steps(pool, step)

        @block.scalar
        def _(act):
            for src, dst in ((w_out, wo_sb), (w_q, wq_sb), (w_o, wm_sb), (router_w, wr_sb)):
                act.dma_start(dst[:, :, :], src[0].rearrange("(k p) n -> p k n", p=P)).then_inc(w_loaded, 16)
            for i, src in enumerate((mem_k, mem_v)):
                act.dma_start(kv[:, i, :, :], src[0, 0].rearrange("(c p) h d -> p c (h d)", p=P)).then_inc(mem_in, 16)
            act.wait_ge(consts, 1)

            act.wait_ge(mk_turned, 1)
            for j in range(2):
                ins = act.activation(kT[:, 2 * j:2 * j + 2, :], t_ps[j][:, :].rearrange("p (h k) -> p h k", h=2),
                                     ACT.Copy)
            ins.then_inc(mk_ready, 1)

            def exps(rows, ready, value):
                act.wait_ge(ready, value)
                for j in range(MH):
                    ins = act.activation(pr[0:rows, j, :], s_ps[0:rows, j * NMEM:(j + 1) * NMEM], ACT.Exp,
                                         bias=sst[0:rows, 1, j:j + 1], scale=SCALE, accum_out=sst[0:rows, 2, j:j + 1])
                return ins

            def step(s, a, b, c, d):
                if a:
                    act.wait_ge(ev["cat_turned"], s.now)
                    act.wait_ge(ev["y_ready"], s.back1)
                    act.activation(catT[:, 0:4, :], t_ps[0][:, :].rearrange("p (k r) -> p k r", r=P), ACT.Copy
                                   ).then_inc(ev["catT0"], 1)
                if d:
                    r = s.prev.prev.prev
                    act.drain()
                    act.wait_ge(ev["h2_ready"], r.now)
                    act.wait_ge(ev["xn_ready"], r.back1)
                    act.activation(sq[:, :], h2[:, r.p, :], ACT.Square, accum_out=ss[:, 2:3]
                                   ).then_inc(ev["h2_summed"], 1)
                    act.dma_start(H[r.t], h2[:, r.p, :]).then_inc(h_stored[r.p], 16)
                if c:
                    t = s.prev.prev
                    act.wait_ge(ev["q_turned"], t.now)
                    act.wait_ge(ev["scored"], t.back1)
                    act.activation(qT[:, :, :], m_ps[:, :].rearrange("p (k r) -> p k r", r=P), ACT.Copy
                                   ).then_inc(ev["qT_ready"], 1)
                if a and not is_sample(s) and not is_sample(s.next):
                    weigh(s.next)
                if d:
                    act.wait_ge(ev["xn_ready"], r.now)
                    act.dma_start(XN[r.t], xn[:, r.p, :]).then_inc(xn_stored[r.p], 16)
                if a:
                    act.drain()
                    act.wait_ge(ev["h_ready"], s.now)
                    act.wait_ge(ev["hs_ready"], s.back1)
                    act.activation(sq[:, :], h[:, s.p, :], ACT.Square, accum_out=ss[:, 0:1]
                                   ).then_inc(ev["h_summed"], 1)
                if c:
                    if is_sample(t):

                        def sequence(b):
                            act.wait_ge(sq_ev["k_turned"], b.now)
                            act.wait_ge(sq_ev["scored"], b.back1)
                            act.activation(kT[:, 0:2, :], t_ps[0][:, :].rearrange("p (h k) -> p h k", h=2), ACT.Copy)
                            act.activation(kT[:, 2:4, :], t_ps[1][:, :].rearrange("p (h k) -> p h k", h=2), ACT.Copy
                                           ).then_inc(sq_ev["kT_ready"], 1)
                            act.wait_ge(sq_ev["p_turned"], b.back1)
                            exps(SAMPLE, sq_ev["max_ready"], b.now).then_inc(sq_ev["exps_done"], 1)

                        all_steps(act, DEC_B, sequence)
                    else:
                        act.wait_ge(ev["p_turned"], t.back1)
                        exps(P, ev["max_ready"], t.now).then_inc(ev["exps_done"], 1)
                if b:
                    act.wait_ge(ev["q_ready"], s.prev.now)
                    act.wait_ge(ev["q_summed"], s.prev.back1)
                    act.activation(qsq[:, :], q_ps[:, :], ACT.Square).then_inc(ev["q_squared"], 1)
                if c:
                    if not is_sample(t):
                        act.wait_ge(ev["p_turned"], t.now)
                        act.wait_ge(ev["o_ready"], t.back1)
                        act.activation(pT[:, 0:2, :, :], t_ps[0][:, :].rearrange("p (h c r) -> p h c r", h=2, c=NC),
                                       ACT.Copy).then_inc(ev["pT0"], 1)
                    act.wait_ge(ev["o_ready"], t.now)
                    act.wait_ge(ev["yo_ready"], t.back1)
                    act.activation(oT[:, :, :], m_ps[:, :].rearrange("p (k r) -> p k r", r=P), ACT.Copy
                                   ).then_inc(ev["oT_ready"], 1)
                if d:
                    act.wait_ge(ev["top_ready"], r.now)
                    act.activation(gt[:, 0:4], top[:, 0:4], ACT.Exp, bias=gt[:, 4:5], accum_out=gt[:, 5:6]
                                   ).then_inc(ev["gates_exp"], 1)
                    act.wait_ge(ev["rt_ready"], r.now)
                    act.dma_start(RT[r.t], rt[:, r.p, :]).then_inc(rt_stored[r.p], 16)

            def weigh(t):
                act.wait_ge(ev["weights"], t.now)
                act.activation(wt[:, 1:4, :], wt[:, 1:4, :], ACT.Exp).then_inc(ev["weights_exp"], 1)

            weigh(at(act, 0))
            steps(act, step)
            for p, n in enumerate(((NT + 1) // 2, NT // 2)):
                for s in (rt_stored[p], h_stored[p], xn_stored[p]):
                    act.wait_ge(s, 16 * n + 16)

        @block.vector
        def _(dve):
            dve.wait_ge(consts, 1)
            dve.wait_ge(const_in, 4 * 16)

            def combine(t):
                if is_sample(t):
                    dve.wait_ge(in_loaded[0], 80 * (NT // 2) + 48)
                    dve.sem_inc(ev["cat_ready"], 1)
                    return
                p = t.p
                dve.wait_ge(in_loaded[p], t.dma5)
                dve.wait_ge(ev["weights_exp"], t.back1)
                nm = [u[:, p, g, AW:AW + AH] for g in range(3)]
                sums = [u[:, p, g, AW + AH:UW] for g in range(3)]
                dve.tensor_tensor(wt[:, 0, :], nm[0], nm[1], ALU.min)
                dve.drain()
                dve.tensor_tensor(wt[:, 0, :], wt[:, 0, :], nm[2], ALU.min)
                dve.drain()
                for g in range(3):
                    ins = dve.tensor_tensor(wt[:, 1 + g, :], wt[:, 0, :], nm[g], ALU.subtract)
                ins.then_inc(ev["weights"], 1)
                dve.wait_ge(ev["weights_exp"], t.now)
                for g in range(3):
                    dve.tensor_tensor(wt[:, 4 + g, :], wt[:, 1 + g, :], sums[g], ALU.mult)
                dve.drain()
                dve.tensor_tensor(wt[:, 4, :], wt[:, 4, :], wt[:, 5, :], ALU.add)
                dve.drain()
                dve.tensor_tensor(wt[:, 4, :], wt[:, 4, :], wt[:, 6, :], ALU.add)
                dve.drain()
                dve.reciprocal(wt[:, 7, :], wt[:, 4, :])
                dve.drain()
                dve.tensor_tensor(wt[:, 1:4, :], wt[:, 1:4, :],
                                  wt[:, 7, :].unsqueeze(1).to_broadcast([P, 3, AH]), ALU.mult)
                dve.drain()
                dve.wait_ge(ev["cat_turned"], t.back2)

                def weighted(out, g):
                    return dve.tensor_tensor(out.rearrange("p (h d) -> p h d", d=AD),
                                             u[:, p, g, 0:AW].rearrange("p (h d) -> p h d", d=AD),
                                             across(wt[:, 1 + g, :], AD), ALU.mult)

                weighted(t1[:, 0, :], 0)
                weighted(t1[:, 1, :], 1)
                dve.drain()
                dve.tensor_tensor(cat[:, p, 0:AW], t1[:, 0, :], t1[:, 1, :], ALU.add)
                dve.drain()
                weighted(t1[:, 0, :], 2)
                dve.drain()
                dve.tensor_tensor(cat[:, p, 0:AW], cat[:, p, 0:AW], t1[:, 0, :], ALU.add).then_inc(ev["cat_ready"], 1)

            def maxima(rows, scored, value, free, freed):
                dve.wait_ge(scored, value)
                dve.wait_ge(free, freed)
                dve.tensor_reduce(sst[0:rows, 0, :], s_ps[0:rows, :].rearrange("p (h k) -> p h k", h=MH), AX.X, ALU.max)
                dve.drain()
                return dve.tensor_scalar(sst[0:rows, 1, :], sst[0:rows, 0, :], -SCALE, None, ALU.mult)

            def turned_gain(dst, gain, turned, value, free, freed):
                dve.wait_ge(turned, value)
                dve.wait_ge(free, freed)
                for j in range(2):
                    ins = dve.tensor_tensor(dst[:, 4 * j:4 * j + 4, :], t_ps[j][:, :].rearrange("p (k r) -> p k r", r=P),
                                            across(gain[:, 4 * j:4 * j + 4], P), ALU.mult)
                return ins

            def sequence(b):
                n = SAMPLE
                maxima(n, sq_ev["scored"], b.now, sq_ev["p_ready"], b.back1).then_inc(sq_ev["max_ready"], 1)
                dve.wait_ge(sq_ev["exps_done"], b.now)
                dve.reciprocal(sst[0:n, 3, :], sst[0:n, 2, :])
                dve.drain()
                dve.tensor_tensor(sst[0:n, 3, :], sst[0:n, 3, :],
                                  seq[:, bass.ds(b.t, 1)].to_broadcast([n, MH]), ALU.mult)
                dve.drain()
                dve.tensor_tensor(pr[0:n, :, :], pr[0:n, :, :], across(sst[0:n, 3, :], NMEM), ALU.mult
                                  ).then_inc(sq_ev["p_ready"], 1)
                dve.wait_ge(sq_ev["p_turned"], b.now)
                dve.wait_ge(sq_ev["o_ready"], b.back1)
                for j in range(2):
                    ins = dve.tensor_copy(pT[:, 2 * j:2 * j + 2, :, 0:n],
                                          t_ps[j][:, :].rearrange("p (h c r) -> p h c r", h=2, c=NC)[:, :, :, 0:n])
                ins.then_inc(sq_ev["pT_ready"], 1)

            def step(s, a, b, c, d):
                if d:
                    r = s.prev.prev.prev
                    dve.wait_ge(ev["yo_ready"], r.now)
                    dve.wait_ge(ev["h_kept"], r.now)
                    dve.tensor_tensor(h2[:, r.p, :], y_ps[:, :], h2[:, r.p, :], ALU.add).then_inc(ev["h2_ready"], 1)
                if a:
                    dve.wait_ge(ev["cat_turned"], s.now)
                    dve.wait_ge(ev["y_ready"], s.back1)
                    dve.tensor_copy(catT[:, 4:8, :], t_ps[1][:, :].rearrange("p (k r) -> p k r", r=P)
                                    ).then_inc(ev["catT1"], 1)
                if d:
                    dve.wait_ge(ev["h2_summed"], r.now)
                    inverse_rms(dve, ss[:, 3:4], ss[:, 2:3], D, (tmp[:, 0, 0:1], tmp[:, 1, 0:1]))
                    dve.drain()
                    dve.wait_ge(ev["x_turned"], r.back2)
                    dve.wait_ge(xn_stored[r.p], r.dma)
                    dve.tensor_scalar(xn[:, r.p, :], h2[:, r.p, :], ss[:, 3:4], None, ALU.mult
                                      ).then_inc(ev["xn_ready"], 1)
                if b:
                    t = s.prev
                    dve.wait_ge(ev["h_summed"], t.now)
                    inverse_rms(dve, ss[:, 1:2], ss[:, 0:1], D, (tmp[:, 0, 1:2], tmp[:, 1, 1:2]))
                    dve.drain()
                    dve.wait_ge(ev["h_turned"], t.back1)
                    dve.tensor_scalar(hs[:, :], h[:, t.p, :], ss[:, 1:2], None, ALU.mult).then_inc(ev["hs_ready"], 1)
                if a and not is_sample(s):
                    combine(s.next)
                if d:
                    turned_gain(xT, g3c, ev["x_turned"], r.now, ev["lg_ready"], r.back1).then_inc(ev["xT_ready"], 1)
                if a:
                    dve.wait_ge(ev["y_ready"], s.now)
                    dve.wait_ge(ev["hs_ready"], s.back2)
                    dve.wait_ge(ev["h_kept"], s.back2)
                    dve.tensor_tensor(h[:, s.p, :], y_ps[:, :], x_sb[:, s.p, :], ALU.add).then_inc(ev["h_ready"], 1)
                if c and not is_sample(s.prev.prev):
                    t = s.prev.prev
                    maxima(P, ev["scored"], t.now, ev["p_ready"], t.back1).then_inc(ev["max_ready"], 1)
                if b:
                    t = s.prev
                    turned_gain(hT, g2c, ev["h_turned"], t.now, ev["q_ready"], t.back1).then_inc(ev["hT_ready"], 1)
                if d:
                    dve.wait_ge(ev["gates_exp"], r.back1)
                    dve.wait_ge(ev["lg_ready"], r.now)
                    dve.tensor_tensor(lg[:, :], m_ps[:, 0:NE], rb[:, :], ALU.add).then_inc(ev["lg_taken"], 1)
                    dve.drain()
                    dve.max(top[:, :], lg[:, :])
                    dve.drain()
                    dve.max_index(tix[:, :], top[:, :], lg[:, :])
                    dve.tensor_scalar(gt[:, 4:5], top[:, 0:1], -1.0, None, ALU.mult).then_inc(ev["top_ready"], 1)
                if c:
                    t = s.prev.prev
                    if is_sample(t):
                        all_steps(dve, DEC_B, sequence)
                    else:
                        dve.wait_ge(ev["exps_done"], t.now)
                        dve.reciprocal(sst[:, 3, :], sst[:, 2, :])
                        dve.drain()
                        dve.tensor_tensor(pr[:, :, :], pr[:, :, :], across(sst[:, 3, :], NMEM), ALU.mult
                                          ).then_inc(ev["p_ready"], 1)
                        dve.wait_ge(ev["p_turned"], t.now)
                        dve.wait_ge(ev["o_ready"], t.back1)
                        dve.tensor_copy(pT[:, 2:4, :, :], t_ps[1][:, :].rearrange("p (h c r) -> p h c r", h=2, c=NC)
                                        ).then_inc(ev["pT1"], 1)
                if b:
                    t = s.prev
                    dve.wait_ge(ev["q_squared"], t.now)
                    dve.tensor_reduce(qss[:, 0, :], qsq[:, :].rearrange("p (h d) -> p h d", d=MD), AX.X, ALU.add
                                      ).then_inc(ev["q_summed"], 1)
                    dve.drain()
                    inverse_rms(dve, qss[:, 1, :], qss[:, 0, :], MD, (tmp[:, 0, :], tmp[:, 1, :]))
                    dve.drain()
                    dve.wait_ge(ev["q_turned"], t.back2)
                    dve.tensor_tensor(q[:, t.p, :].rearrange("p (h d) -> p h d", d=MD),
                                      q_ps[:, :].rearrange("p (h d) -> p h d", d=MD), across(qss[:, 1, :], MD),
                                      ALU.mult).then_inc(ev["q_scaled"], 1)
                if d:
                    dve.drain()
                    dve.wait_ge(rt_stored[r.p], r.dma)
                    dve.tensor_copy(rt[:, r.p, 4:8], tix[:, 0:4])
                    dve.wait_ge(ev["gates_exp"], r.now)
                    dve.reciprocal(gt[:, 6:7], gt[:, 5:6])
                    dve.drain()
                    dve.tensor_scalar(rt[:, r.p, 0:4], gt[:, 0:4], gt[:, 6:7], None, ALU.mult
                                      ).then_inc(ev["rt_ready"], 1)

            combine(at(dve, 0))
            steps(dve, step)

        @block.tensor
        def _(pe):
            pe.wait_ge(consts, 1)
            pe.wait_ge(mem_in, 32)
            pe.wait_ge(w_loaded, 64)

            def turn8(src):
                for k in range(KD):
                    ins = pe.transpose(t_ps[k // 4][:, k % 4 * P:(k % 4 + 1) * P], src[:, k * P:(k + 1) * P],
                                       ident[:, :])
                return ins

            def turn_k(half):
                for j in range(MH):
                    for c in range(NC):
                        ins = pe.transpose(t_ps[j // 2][:, (j % 2) * NMEM + c * P:(j % 2) * NMEM + (c + 1) * P],
                                           kv[:, half, c, j * MD:(j + 1) * MD], ident[:, :])
                return ins

            def scores(rows):
                for j in range(MH):
                    ins = pe.matmul(s_ps[0:rows, j * NMEM:(j + 1) * NMEM], qT[:, j, 0:rows], kT[:, j, :],
                                    start=True, stop=True)
                return ins

            def turn_p(rows):
                for j in range(MH):
                    for c in range(NC):
                        a = (j % 2) * NMEM + c * P
                        ins = pe.transpose(t_ps[j // 2][:, a:a + rows], pr[0:rows, j, c * P:(c + 1) * P],
                                           ident[0:rows, 0:rows])
                return ins

            def project(out, lhs, w, n):
                for c in range(2):
                    for k in range(n):
                        ins = pe.matmul(out[:, c * 512:(c + 1) * 512], lhs[:, k, :], w[:, k, c * 512:(c + 1) * 512],
                                        start=(k == 0), stop=(k == n - 1))
                return ins

            def sequence(b):
                pe.wait_ge(b_loaded[b.p], b.dma2)
                pe.wait_ge(sq_ev["pT_ready"], b.back1)
                turn_k(b.p).then_inc(sq_ev["k_turned"], 1)
                pe.wait_ge(sq_ev["kT_ready"], b.now)
                pe.wait_ge(sq_ev["exps_done"], b.back1)
                scores(SAMPLE).then_inc(sq_ev["scored"], 1)
                pe.wait_ge(consts, 1)
                pe.wait_ge(sq_ev["p_ready"], b.now)
                turn_p(SAMPLE).then_inc(sq_ev["p_turned"], 1)
                pe.wait_ge(sq_ev["pT_ready"], b.now)
                for j in range(MH):
                    for c in range(NC):
                        ins = pe.matmul(m_ps[:, j * P:j * P + SAMPLE], vs[:, b.p, c, j * MD:(j + 1) * MD],
                                        pT[:, j, c, 0:SAMPLE], start=False, stop=True, skip_group_check=True)
                ins.then_inc(sq_ev["o_ready"], 1)

            turn_k(0).then_inc(mk_turned, 1)
            pe.wait_ge(mk_ready, 1)

            def step(s, a, b, c, d):
                t, r = s.prev.prev, s.prev.prev.prev
                if a:
                    pe.wait_ge(ev["cat_ready"], s.now)
                    turn8(cat[:, s.p, :]).then_inc(ev["cat_turned"], 1)
                if c:
                    pe.wait_ge(ev["q_done"], t.now)
                    pe.wait_ge(ev["oT_ready"], t.back1)
                    for j in range(MH):
                        ins = pe.transpose(m_ps[:, j * P:(j + 1) * P], q[:, t.p, j * MD:(j + 1) * MD], ident[:, :])
                    ins.then_inc(ev["q_turned"], 1)
                if a:
                    pe.wait_ge(ev["catT0"], s.now)
                    pe.wait_ge(ev["catT1"], s.now)
                    pe.wait_ge(ev["h_ready"], s.back1)
                    if d:
                        pe.wait_ge(ev["h2_ready"], r.now)
                    project(y_ps, catT, wo_sb, KD).then_inc(ev["y_ready"], 1)
                if d:
                    pe.wait_ge(ev["xn_ready"], r.now)
                    turn8(xn[:, r.p, :]).then_inc(ev["x_turned"], 1)
                if c:
                    pe.wait_ge(ev["qT_ready"], t.now)
                    if not is_sample(t):
                        pe.wait_ge(ev["exps_done"], t.back1)
                        scores(P).then_inc(ev["scored"], 1)
                if b:
                    if d:
                        pe.wait_ge(ev["xT_ready"], r.now)
                    pe.wait_ge(ev["hs_ready"], s.prev.now)
                    turn8(hs).then_inc(ev["h_turned"], 1)
                if d:
                    pe.wait_ge(ev["xT_ready"], r.now)
                    pe.wait_ge(ev["oT_ready"], r.now)
                    for k in range(KD):
                        ins = pe.matmul(m_ps[:, 0:NE], xT[:, k, :], wr_sb[:, k, :], start=(k == 0), stop=(k == KD - 1))
                    ins.then_inc(ev["lg_ready"], 1)
                if b:
                    pe.wait_ge(ev["hT_ready"], s.prev.now)
                    pe.wait_ge(ev["q_scaled"], s.prev.back1)
                    for k in range(KD):
                        ins = pe.matmul(q_ps[:, :], hT[:, k, :], wq_sb[:, k, :], start=(k == 0), stop=(k == KD - 1))
                    ins.then_inc(ev["q_ready"], 1)
                if c:
                    if not is_sample(t):
                        pe.wait_ge(ev["p_ready"], t.now)
                        turn_p(P).then_inc(ev["p_turned"], 1)
                        pe.wait_ge(ev["pT0"], t.now)
                        pe.wait_ge(ev["pT1"], t.now)
                        pe.wait_ge(ev["lg_taken"], t.back1)
                        for j in range(MH):
                            for c_ in range(NC):
                                ins = pe.matmul(m_ps[:, j * P:(j + 1) * P], kv[:, 1, c_, j * MD:(j + 1) * MD],
                                                pT[:, j, c_, :], start=(c_ == 0), stop=(c_ == NC - 1))
                        ins.then_inc(ev["o_ready"], 1)
                    else:
                        pe.wait_ge(ev["lg_taken"], t.back1)
                        pe.matmul(m_ps[:, :], zeros[:, 0:P], zeros[:, :], start=True, stop=True, skip_group_check=True)
                        all_steps(pe, DEC_B, sequence)
                        pe.wait_ge(sq_ev["o_ready"], at(pe, DEC_B - 1).now)
                        pe.sem_inc(ev["o_ready"], 1)
                    pe.wait_ge(ev["oT_ready"], t.now)
                    pe.wait_ge(ev["h2_ready"], t.back1)
                    if a:
                        pe.wait_ge(ev["h_ready"], s.now)
                    project(y_ps, oT, wm_sb, MH).then_inc(ev["yo_ready"], 1)

            steps(pe, step)


def slots(nc, RT, TBL, SL, TE):
    NK = NT * TOPK
    N3 = NT * NE // 3
    with ExitStack() as ctx:
        ph = Phase(nc, ctx, "sl")
        rt = ph.sb("rt", [P, NT, 8])
        before = ph.sb("before", [P, P])
        ones = ph.sb("ones", [P, P])
        ie = ph.sb("ie", [P, NE])
        it_ = ph.sb("it", [1, NTL])
        hot = ph.sb("hot", [P, NK, NE])
        hit = ph.sb("hit", [P, NT, NE])
        pos = ph.sb("pos", [P, NT, NE])
        cnt = ph.sb("cnt", [P, NT, NE])
        base = ph.sb("base", [P, NT + 1, NE])
        n_f, n_i, end, first = (ph.sb("n_f", [P, NE]), ph.sb("n_i", [P, NE], I32), ph.sb("end", [P, NE]),
                                ph.sb("first", [P, NE]))
        sl_f = ph.sb("sl_f", [P, NK])
        sl_i = ph.sb("sl_i", [P, NK], I32)
        low, high, low_f, high_f = (ph.sb("low", [P, NK], I32), ph.sb("high", [P, NK], I32),
                                    ph.sb("low_f", [P, NK]), ph.sb("high_f", [P, NK]))
        i_low, i_high = ph.sb("i_low", [P, P]), ph.sb("i_high", [P, NTL])
        zeros = ph.sb("zeros", [P, NTL])
        hot_low = ph.sb("hot_low", [P, 2, TOPK, P])
        hot_high = ph.sb("hot_high", [P, 2, TOPK, NTL])
        tbl = ph.sb("tbl", [P, NTL], I32)
        ends = ph.sb("ends", [1, NTL, NE])
        te_f = ph.sb("te_f", [1, 3, NTL])
        te_i = ph.sb("te_i", [1, 3, NTL], I32)
        tok = ph.sb("tok", [P, NT])
        r_ps = [ph.ps(f"rps{i}") for i in range(3)]
        c_ps = [ph.ps(f"cps{i}") for i in range(3)]
        tbl_ps = ph.ps("tblps")
        loaded, consts, hits, ranked, stored, ready, tiles_ready, tbl_ready = (ph.load(n) for n in (
            "loaded", "consts", "hits", "ranked", "stored", "ready", "tiles_ready", "tbl_ready"))
        hot_ready, hot_used = ph.event("hot_ready"), ph.event("hot_used")
        block = ctx.enter_context(nc.Block())

        @block.sync
        def _(sp):
            ph.grant(sp)
            sp.dma_start(rt[:, :, :], RT.rearrange("t p c -> p t c")).then_inc(loaded, 16)
            sp.wait_ge(ready, 1)
            sp.dma_start(SL, sl_i[:, :]).then_inc(stored, 16)
            sp.wait_ge(tiles_ready, 1)
            sp.dma_start(TE.unsqueeze(0), te_i[:, :, :]).then_inc(stored, 16)
            sp.wait_ge(tbl_ready, 1)
            sp.dma_start(TBL, tbl[:, :]).then_inc(stored, 16)
            sp.wait_ge(stored, 48)

        @block.gpsimd
        def _(pool):
            pool.memset(ones[:, :], 1.0)
            pool.memset(before[:, :], 1.0)
            pool.memset(zeros[:, :], 0.0)
            pool.iota(ie[:, :], [[1, NE]], base=0, channel_multiplier=0, allow_small_or_imprecise_dtypes=True)
            pool.iota(it_[:, :], [[1, NTL]], base=0, channel_multiplier=0, allow_small_or_imprecise_dtypes=True)
            for ap, pattern, own in ((tok, [[P, NT]], 1), (i_low, [[1, P]], 0), (i_high, [[1, NTL]], 0)):
                pool.iota(ap[:, :], pattern, base=0, channel_multiplier=own, allow_small_or_imprecise_dtypes=True)
            pool.drain()
            pool.affine_select(out=before[:, :], in_=before[:, :], compare_op=ALU.is_gt, fill=0.0, base=0,
                               pattern=[[1, P]], channel_multiplier=-1)
            pool.drain()
            pool.sem_inc(consts, 1)

        @block.vector
        def _(dve):
            dve.wait_ge(consts, 1)
            dve.wait_ge(loaded, 16)
            for k in range(TOPK):
                dve.tensor_tensor(hot[:, k:NK:TOPK, :], rt[:, :, 4 + k:5 + k].to_broadcast([P, NT, NE]),
                                  ie[:, :].unsqueeze(1).to_broadcast([P, NT, NE]), ALU.is_equal)
            dve.drain()
            dve.memset(hot[SAMPLE:P, NK - TOPK:NK, :], 0.0)
            dve.drain()
            dve.tensor_reduce(hit[:, :, :], hot[:, :, :].rearrange("p (t k) e -> p t e k", k=TOPK), AX.X, ALU.add
                              ).then_inc(hits, 1)
            dve.memset(base[:, 0, :], 0.0)
            dve.wait_ge(ranked, 1)
            cf = cnt[:, :, :].rearrange("p t e -> p (t e)")
            pf = pos[:, :, :].rearrange("p t e -> p (t e)")
            for i in range(3):
                dve.tensor_copy(cf[:, i * N3:(i + 1) * N3], c_ps[i][:, 0:N3])
                dve.tensor_copy(pf[:, i * N3:(i + 1) * N3], r_ps[i][:, 0:N3])
            dve.drain()
            with dve.Fori(0, NT) as t:
                dve.tensor_tensor(base[:, bass.ds(t + 1, 1), :], base[:, bass.ds(t, 1), :],
                                  cnt[:, bass.ds(t, 1), :], ALU.add)
                dve.drain()
            dve.tensor_scalar(n_f[:, :], base[:, NT, :], float(P - 1), None, ALU.add)
            dve.drain()
            dve.tensor_copy(n_i[:, :], n_f[:, :])
            dve.drain()
            dve.tensor_scalar(n_i[:, :], n_i[:, :], 7, None, ALU.logical_shift_right)
            dve.drain()
            dve.tensor_copy(n_f[:, :], n_i[:, :])
            dve.drain()
            dve.tensor_tensor_scan(end[:, :], ones[:, 0:NE], n_f[:, :], 0.0, ALU.mult, ALU.add)
            dve.drain()
            dve.tensor_tensor(first[:, :], end[:, :], n_f[:, :], ALU.subtract)
            dve.drain()
            dve.tensor_scalar(first[:, :], first[:, :], float(P), None, ALU.mult)
            dve.tensor_tensor(pos[:, :, :], pos[:, :, :], base[:, 0:NT, :], ALU.add)
            dve.drain()
            dve.tensor_tensor(pos[:, :, :], pos[:, :, :], first[:, :].unsqueeze(1).to_broadcast([P, NT, NE]), ALU.add)
            dve.drain()
            for k in range(TOPK):
                dve.tensor_tensor(hot[:, k:NK:TOPK, :], hot[:, k:NK:TOPK, :], pos[:, :, :], ALU.mult)
            dve.drain()
            dve.tensor_reduce(sl_f[:, :], hot[:, :, :], AX.X, ALU.add)
            dve.drain()
            dve.tensor_copy(sl_i[:, :], sl_f[:, :]).then_inc(ready, 1)
            dve.drain()
            dve.tensor_scalar(low[:, :], sl_i[:, :], P - 1, None, ALU.bitwise_and)
            dve.tensor_scalar(high[:, :], sl_i[:, :], 7, None, ALU.logical_shift_right)
            dve.drain()
            dve.tensor_copy(low_f[:, :], low[:, :])
            dve.tensor_copy(high_f[:, :], high[:, :])
            dve.drain()
            dve.memset(low_f[SAMPLE:P, NK - TOPK:NK], -1.0)
            dve.drain()
            dve.tensor_tensor(ends[:, :, :], it_[:, :].unsqueeze(2).to_broadcast([1, NTL, NE]),
                              end[0:1, :].unsqueeze(1).to_broadcast([1, NTL, NE]), ALU.is_ge)
            dve.drain()
            dve.tensor_reduce(te_f[:, 0, :], ends[:, :, :], AX.X, ALU.add)
            dve.drain()
            dve.tensor_scalar(te_f[:, 2, :], te_f[:, 0, :], float(NE), None, ALU.is_lt)
            dve.drain()
            dve.tensor_scalar(te_f[:, 0, :], te_f[:, 0, :], float(NE - 1), None, ALU.min)
            dve.memset(te_f[:, 1, :], 1.0)
            dve.drain()
            dve.tensor_tensor(te_f[:, 1, 1:NTL], te_f[:, 0, 1:NTL], te_f[:, 0, 0:NTL - 1], ALU.not_equal)
            dve.drain()
            dve.tensor_copy(te_i[:, :, :], te_f[:, :, :]).then_inc(tiles_ready, 1)

            def one_hots(t):
                dve.wait_ge(hot_used, t.back2)
                dve.tensor_tensor(hot_low[:, t.p, :, :], i_low[:, :].unsqueeze(1).to_broadcast([P, TOPK, P]),
                                  low_f[:, bass.ds(t.t * TOPK, TOPK)].unsqueeze(2).to_broadcast([P, TOPK, P]),
                                  ALU.is_equal)
                for k in range(TOPK):
                    ins = dve.scalar_tensor_tensor(hot_high[:, t.p, k, :], i_high[:, :],
                                                   high_f[:, bass.ds(t.t * TOPK + k, 1)],
                                                   tok[:, bass.ds(t.t, 1)].to_broadcast([P, NTL]),
                                                   ALU.is_equal, ALU.mult)
                ins.then_inc(hot_ready, 1)

            all_steps(dve, NT, one_hots)
            dve.wait_ge(hot_used, at(dve, NT - 1).now)
            dve.tensor_copy(tbl[:, :], tbl_ps[:, 0:NTL]).then_inc(tbl_ready, 1)

        @block.tensor
        def _(pe):
            pe.wait_ge(hits, 1)
            hf = hit[:, :, :].rearrange("p t e -> p (t e)")
            for i in range(3):
                pe.matmul(r_ps[i][:, 0:N3], before[:, :], hf[:, i * N3:(i + 1) * N3], start=True, stop=True)
                ins = pe.matmul(c_ps[i][:, 0:N3], ones[:, :], hf[:, i * N3:(i + 1) * N3], start=True, stop=True)
            ins.then_inc(ranked, 1)

            pe.matmul(tbl_ps[:, 0:NTL], zeros[:, 0:P], zeros[:, :], start=True, stop=True, skip_group_check=True)

            def place(t):
                pe.wait_ge(hot_ready, t.now)
                for k in range(TOPK):
                    ins = pe.matmul(tbl_ps[:, 0:NTL], hot_low[:, t.p, k, :], hot_high[:, t.p, k, :],
                                    start=False, stop=True, skip_group_check=True)
                ins.then_inc(hot_used, 1)

            all_steps(pe, NT, place)


def experts(nc, XN, norm3_g, TBL, TE, w1, b1, w2, b2, YS):
    RING = 3
    F32R = mybir.dt.float32r
    with ExitStack() as ctx:
        ph = Phase(nc, ctx, "ex")
        ident = ph.sb("ident", [P, P])
        gc = ph.sb("gc", [P, KD])
        tbl = ph.sb("tbl", [P, NTL], I32)
        te = ph.sb("te", [1, 3, NTL], I32)
        idx = ph.sb("idx", [P, 2], I32)
        w1_sb = ph.sb("w1", [P, KD, 2 * FF])
        w2_sb = ph.sb("w2", [P, KD, D])
        b1_sb = ph.sb("b1", [P, 2 * FF])
        b2_sb = ph.sb("b2", [P, D])
        xg = ph.sb("xg", [P, 2, D])
        xT = ph.sb("xT", [P, 2, KD, P])
        hb = ph.sb("hb", [P, 2 * FF])
        glu, sig, lin = ph.sb("glu", [P, FF]), ph.sb("sig", [P, FF]), ph.sb("lin", [P, FF])
        aT_hi, aT_lo = ph.sb("aT_hi", [P, KD, P], F32R), ph.sb("aT_lo", [P, KD, P], F32R)
        w2_hi, w2_lo = ph.sb("w2_hi", [P, RING, D], F32R), ph.sb("w2_lo", [P, RING, D], F32R)
        y = ph.sb("y", [P, 2, D])
        h_ps = [ph.ps(f"hps{i}") for i in range(4)]
        t_ps = [ph.ps(f"tps{i}") for i in range(2)]
        y_ps = ph.ps("yps", 1024)
        const_in, tbl_in, te_in, consts = (ph.load(n) for n in ("const_in", "tbl_in", "te_in", "consts"))
        w1_in, w2_in = ph.loads("w1_in", KD), ph.loads("w2_in", KD)
        b1_in, b2_in = ph.load("b1_in"), ph.load("b2_in")
        x_in = ph.loads("x_in")
        y_stored = ph.stores("y_stored")
        w1_used, w2_used = ph.event("w1_used"), ph.event("w2_used")
        hi_split, lo_split, aT_hi_ready = ph.event("hi_split"), ph.event("lo_split"), ph.event("aT_hi_ready")
        x_turned, xT_ready, h_ready, h_taken, glu_ready, sig_ready, a_ready, a_turned, aT_ready, y_ready, y_taken = (
            ph.event(n) for n in ("x_turned", "xT_ready", "h_ready", "h_taken", "glu_ready", "sig_ready", "a_ready",
                                  "a_turned", "aT_ready", "y_ready", "y_taken"))
        block = ctx.enter_context(nc.Block())

        def lagged(eng, step, idle):
            eng.wait_ge(te_in, 16)
            step(at(eng, 0), True, False)
            step(at(eng, 1), True, True)
            with eng.Fori(1, NTL // 2) as it:
                live = eng.value_load(te[0:1, 2, bass.ds(Pair(eng, it).value(2, -1), 1)], min_val=0, max_val=1)
                with eng.If(live):
                    pair = Pair(eng, it)
                    for k in range(2):
                        step(Turn(pair, k), True, True)
                with eng.Else():
                    pair = Pair(eng, it)
                    for k in range(2):
                        idle(Turn(pair, k))
            if NTL % 2:
                step(at(eng, NTL - 1), True, True)
            step(at(eng, NTL), False, True)

        @block.sync
        def _(sp):
            ph.grant(sp)
            sp.dma_start(gc[:, :], norm3_g[0].rearrange("(k p) -> p k", p=P), allow_slow_non_contiguous=True
                         ).then_inc(const_in, 16)
            sp.dma_start(te[:, :, :], TE.unsqueeze(0)).then_inc(te_in, 16)
            sp.wait_ge(te_in, 16)

            def is_first(t):
                return isinstance(t.pair.it, int) and t.t == 0

            def row(which, i):
                return te[0:1, which, bass.ds(i, 1)]

            def expert(i):
                e = sp.value_load(row(0, i), min_val=0, max_val=NE - 1)
                new = sp.value_load(row(1, i), min_val=0, max_val=1)
                return e, new

            def first_weights(t):
                e, new = expert(t.t)
                for k in range(KD):
                    if not is_first(t):
                        sp.wait_ge(w1_used, t.of(8, k - 8))
                    sp.dma_start(w1_sb[:, k, :], w1[0][bass.ds(e, 1), k * P:(k + 1) * P, :].rearrange("o p n -> p (o n)"),
                                 cond=new).then_inc(w1_in[k], 16)
                sp.wait_ge(h_taken, t.back1)
                sp.dma_start(b1_sb[:, :], b1[0][bass.ds(e, 1), :].to_broadcast([P, 2 * FF]), cond=new
                             ).then_inc(b1_in, 16)

            def second_weights(t):
                e, new = expert(t.t)
                for k in range(KD):
                    if not is_first(t):
                        sp.wait_ge(lo_split, t.of(8, k - 8))
                    sp.dma_start(w2_sb[:, k, :], w2[0][bass.ds(e, 1), k * P:(k + 1) * P, :].rearrange("o p n -> p (o n)"),
                                 cond=new).then_inc(w2_in[k], 16)
                sp.wait_ge(y_taken, t.back1)
                sp.dma_start(b2_sb[:, :], b2[0][bass.ds(e, 1), :].to_broadcast([P, D]), cond=new).then_inc(b2_in, 16)

            def step(t):
                first_weights(t)
                if not (isinstance(t.pair.it, int) and t.t == 0):
                    second_weights(t.prev)

            step(at(sp, 0))
            step(at(sp, 1))
            with sp.Fori(1, NTL // 2) as it:
                pair = Pair(sp, it)
                for k in range(2):
                    step(Turn(pair, k))
            if NTL % 2:
                step(at(sp, NTL - 1))
            second_weights(at(sp, NTL - 1))

        @block.gpsimd
        def _(pool):
            make_identity(pool, ident)
            pool.dma_start(tbl[:, :], TBL).then_inc(tbl_in, 16)
            pool.wait_ge(tbl_in, 16)
            pool.drain()
            pool.sem_inc(consts, 1)

            def step(t):
                pool.wait_ge(x_turned, t.back2)
                pool.tensor_copy(idx[:, t.p:t.p + 1], tbl[:, bass.ds(t.t, 1)])
                pool.drain()
                pool.indirect_dma_start(out=xg[:, t.p, :], out_offset=None, in_=XN.rearrange("t p d -> (t p) d"),
                                        in_offset=bass.IndirectOffsetOnAxis(ap=idx[:, t.p:t.p + 1], axis=0)
                                        ).then_inc(x_in[t.p], 16)

            all_steps(pool, NTL, step)

        @block.scalar
        def _(act):
            def step(t, this, before):
                if before:
                    b = t.prev
                    act.wait_ge(a_turned, b.now)
                    act.wait_ge(y_ready, b.back1)
                    for j in range(2):
                        ins = act.activation(aT_hi[:, 4 * j:4 * j + 4, :], t_ps[j][:, :].rearrange("p (k r) -> p k r", r=P),
                                             ACT.Copy)
                    ins.then_inc(aT_hi_ready, 1)
                    for k in range(KD):
                        act.wait_ge(w2_in[k], b.dma1)
                        act.wait_ge(w2_used, b.of(8, k - RING) if k >= RING else b.of(8, min(k - 2, -1)))
                        act.activation(w2_hi[:, k % RING, :], w2_sb[:, k, :], ACT.Copy).then_inc(hi_split, 1)
                if this:
                    act.wait_ge(glu_ready, t.now)
                    act.wait_ge(a_ready, t.back1)
                    act.activation(sig[:, :], glu[:, :], ACT.Sigmoid, scale=ALPHA).then_inc(sig_ready, 1)
                if before:
                    act.wait_ge(y_taken, b.now)
                    act.dma_start(YS[b.t], y[:, b.p, :]).then_inc(y_stored[b.p], 16)

            def idle(t):
                b = t.prev
                act.wait_ge(a_turned, b.now)
                act.wait_ge(y_ready, b.back1)
                act.sem_inc(aT_hi_ready, 1)
                for k in range(KD):
                    act.wait_ge(w2_in[k], b.dma1)
                    act.wait_ge(w2_used, b.of(8, k - RING) if k >= RING else b.of(8, min(k - 2, -1)))
                    act.sem_inc(hi_split, 1)
                act.wait_ge(glu_ready, t.now)
                act.wait_ge(a_ready, t.back1)
                act.sem_inc(sig_ready, 1)
                act.wait_ge(y_taken, b.now)
                act.dma_start(YS[b.t], y[:, b.p, :]).then_inc(y_stored[b.p], 16)

            lagged(act, step, idle)
            for p, n in enumerate(((NTL + 1) // 2, NTL // 2)):
                act.wait_ge(y_stored[p], 16 * n + 16)

        @block.vector
        def _(dve):
            dve.wait_ge(const_in, 16)

            def turn_x(t):
                dve.wait_ge(x_turned, t.now)
                dve.wait_ge(h_ready, t.back2)
                for j in range(2):
                    ins = dve.tensor_tensor(xT[:, t.p, 4 * j:4 * j + 4, :], t_ps[j][:, :].rearrange("p (k r) -> p k r", r=P),
                                            across(gc[:, 4 * j:4 * j + 4], P), ALU.mult)
                ins.then_inc(xT_ready, 1)

            def split(b, pieces):
                for k in pieces:
                    dve.wait_ge(hi_split, b.of(8, k))
                    dve.tensor_tensor(w2_lo[:, k % RING, :], w2_sb[:, k, :], w2_hi[:, k % RING, :], ALU.subtract
                                      ).then_inc(lo_split, 1)

            def step(t, this, before):
                b = t.prev
                if before:
                    dve.wait_ge(aT_hi_ready, b.now)
                    for j in range(2):
                        ins = dve.tensor_tensor(aT_lo[:, 4 * j:4 * j + 4, :],
                                                t_ps[j][:, :].rearrange("p (k r) -> p k r", r=P),
                                                aT_hi[:, 4 * j:4 * j + 4, :], ALU.subtract)
                    ins.then_inc(aT_ready, 1)
                    split(b, range(RING))
                if this:
                    dve.wait_ge(h_ready, t.now)
                    dve.wait_ge(b1_in, t.dma1)
                    for c in range(4):
                        cols = slice(c * 512, (c + 1) * 512)
                        ins = dve.tensor_tensor(hb[:, cols], h_ps[c][:, :], b1_sb[:, cols], ALU.add)
                    ins.then_inc(h_taken, 1)
                if before:
                    split(b, range(RING, RING + 1))
                if this and not (isinstance(t.pair.it, int) and t.t == NTL - 1):
                    turn_x(t.next)
                if before:
                    split(b, range(RING + 1, KD))
                    dve.wait_ge(y_ready, b.now)
                    dve.wait_ge(b2_in, b.dma1)
                    dve.wait_ge(y_stored[b.p], b.dma)
                    dve.tensor_tensor(y[:, b.p, :], y_ps[:, :], b2_sb[:, :], ALU.add).then_inc(y_taken, 1)
                if this:
                    dve.drain()
                    dve.wait_ge(sig_ready, t.back1)
                    dve.wait_ge(a_turned, t.back1)
                    dve.tensor_scalar(glu[:, :], hb[:, 0:2 * FF:2], LIMIT, None, ALU.min).then_inc(glu_ready, 1)
                    dve.tensor_scalar(lin[:, :], hb[:, 1:2 * FF:2], LIMIT, -LIMIT, ALU.min, ALU.max)
                    dve.drain()
                    dve.scalar_tensor_tensor(lin[:, :], lin[:, :], 1.0, glu[:, :], ALU.add, ALU.mult)
                    dve.drain()
                    dve.wait_ge(sig_ready, t.now)
                    dve.tensor_tensor(lin[:, :], lin[:, :], sig[:, :], ALU.mult).then_inc(a_ready, 1)

            def idle(t):
                b = t.prev
                dve.wait_ge(aT_hi_ready, b.now)
                dve.sem_inc(aT_ready, 1)
                for k in range(KD):
                    dve.wait_ge(hi_split, b.of(8, k))
                    dve.sem_inc(lo_split, 1)
                dve.wait_ge(h_ready, t.now)
                dve.wait_ge(b1_in, t.dma1)
                dve.sem_inc(h_taken, 1)
                dve.wait_ge(x_turned, t.next.now)
                dve.sem_inc(xT_ready, 1)
                dve.wait_ge(y_ready, b.now)
                dve.wait_ge(b2_in, b.dma1)
                dve.wait_ge(y_stored[b.p], b.dma)
                dve.sem_inc(y_taken, 1)
                dve.sem_inc(glu_ready, 1)
                dve.wait_ge(sig_ready, t.now)
                dve.sem_inc(a_ready, 1)

            turn_x(at(dve, 0))
            lagged(dve, step, idle)

        @block.tensor
        def _(pe):
            pe.wait_ge(consts, 1)

            def turn8(src):
                for k in range(KD):
                    ins = pe.transpose(t_ps[k // 4][:, k % 4 * P:(k % 4 + 1) * P], src[:, k * P:(k + 1) * P], ident[:, :])
                return ins

            def turn_x(t):
                pe.wait_ge(x_in[t.p], t.dma)
                turn8(xg[:, t.p, :]).then_inc(x_turned, 1)

            def step(t, this, before):
                b = t.prev
                if this:
                    pe.wait_ge(xT_ready, t.now)
                    pe.wait_ge(h_taken, t.back1)
                    for k in range(KD):
                        pe.wait_ge(w1_in[k], t.dma1)
                        for c in range(4):
                            ins = pe.matmul(h_ps[c][:, :], xT[:, t.p, k, :], w1_sb[:, k, c * 512:(c + 1) * 512],
                                            start=(k == 0), stop=(k == KD - 1))
                        ins.then_inc(w1_used, 1)
                        if k == 3 and before:
                            pe.wait_ge(a_ready, b.now)
                            turn8(lin).then_inc(a_turned, 1)
                    pe.wait_ge(w1_used, t.of(8, 7))
                    pe.sem_inc(h_ready, 1)
                elif before:
                    pe.wait_ge(a_ready, b.now)
                    turn8(lin).then_inc(a_turned, 1)
                if before:
                    pe.wait_ge(aT_ready, b.now)
                    pe.wait_ge(y_taken, b.back1)
                if this and not (isinstance(t.pair.it, int) and t.t == NTL - 1):
                    turn_x(t.next)
                if before:
                    for k in range(KD):
                        pe.wait_ge(lo_split, b.of(8, k))
                        for i, (a, w) in enumerate(((aT_hi, w2_hi), (aT_hi, w2_lo), (aT_lo, w2_hi))):
                            for c in range(2):
                                ins = pe.matmul(y_ps[:, c * 512:(c + 1) * 512], a[:, k, :],
                                                w[:, k % RING, c * 512:(c + 1) * 512], start=(k == 0 and i == 0),
                                                stop=(k == KD - 1 and i == 2), skip_group_check=True)
                        ins.then_inc(w2_used, 1)
                    pe.wait_ge(w2_used, b.of(8, 7))
                    pe.sem_inc(y_ready, 1)

            def idle(t):
                b = t.prev
                pe.wait_ge(xT_ready, t.now)
                pe.wait_ge(h_taken, t.back1)
                for k in range(KD):
                    pe.wait_ge(w1_in[k], t.dma1)
                pe.sem_inc(w1_used, KD)
                pe.sem_inc(h_ready, 1)
                pe.wait_ge(a_ready, b.now)
                pe.sem_inc(a_turned, 1)
                pe.wait_ge(aT_ready, b.now)
                pe.wait_ge(y_taken, b.back1)
                pe.wait_ge(x_in[t.next.p], t.next.dma)
                pe.sem_inc(x_turned, 1)
                for k in range(KD):
                    pe.wait_ge(lo_split, b.of(8, k))
                    pe.sem_inc(w2_used, 1)
                pe.sem_inc(y_ready, 1)

            turn_x(at(pe, 0))
            lagged(pe, step, idle)


def combine_experts(nc, H, RT, SL, YS, y_prompt, y_sample):
    with ExitStack() as ctx:
        ph = Phase(nc, ctx, "cb")
        sl = ph.sb("sl", [P, NT * TOPK], I32)
        idx = ph.sb("idx", [P, 2, TOPK], I32)
        gt = ph.sb("gt", [P, NT, 8])
        h = ph.sb("h", [P, 2, D])
        r = ph.sb("r", [P, 2, TOPK, D])
        y = ph.sb("y", [P, 2, D])
        sl_in, gt_in = ph.load("sl_in"), ph.load("gt_in")
        h_in, r_in = ph.loads("h_in"), ph.loads("r_in")
        y_stored = ph.stores("y_stored")
        y_ready = ph.event("y_ready")
        block = ctx.enter_context(nc.Block())

        @block.sync
        def _(sp):
            ph.grant(sp)
            sp.dma_start(sl[:, :], SL).then_inc(sl_in, 16)
            sp.dma_start(gt[:, :, :], RT.rearrange("t p c -> p t c")).then_inc(gt_in, 16)

            def step(t):
                sp.wait_ge(y_ready, t.back2)
                sp.dma_start(h[:, t.p, :], H[t.t]).then_inc(h_in[t.p], 16)

            all_steps(sp, NT, step)

        @block.gpsimd
        def _(pool):
            pool.wait_ge(sl_in, 16)

            def step(t, n=P):
                pool.wait_ge(y_ready, t.back2)
                pool.tensor_copy(idx[:, t.p, :], sl[:, bass.ds(t.t * TOPK, TOPK)])
                pool.drain()
                for k in range(TOPK):
                    pool.indirect_dma_start(out=r[0:n, t.p, k, :], out_offset=None, in_=YS.rearrange("t p d -> (t p) d"),
                                            in_offset=bass.IndirectOffsetOnAxis(ap=idx[0:n, t.p, k:k + 1], axis=0)
                                            ).then_inc(r_in[t.p], 16)

            all_steps(pool, NT, step, lambda t: step(t, SAMPLE))

        @block.scalar
        def _(act):
            yr = y_prompt[0].rearrange("(t r) d -> t r d", r=P)

            def step(t, last=False):
                act.wait_ge(y_ready, t.now)
                if last:
                    act.dma_start(y_sample.rearrange("b t d -> (b t) d"), y[0:SAMPLE, t.p, :]).then_inc(y_stored[t.p], 16)
                else:
                    act.dma_start(yr[t.t], y[:, t.p, :]).then_inc(y_stored[t.p], 16)

            all_steps(act, NT, step, lambda t: step(t, True))
            for p, n in enumerate(((NT + 1) // 2, NT // 2)):
                act.wait_ge(y_stored[p], 16 * n + 16)

        @block.vector
        def _(dve):
            dve.wait_ge(gt_in, 16)

            def step(t, n=P):
                dve.wait_ge(h_in[t.p], t.dma)
                dve.wait_ge(r_in[t.p], t.dma4)
                dve.wait_ge(y_stored[t.p], t.dma)
                for k in range(TOPK):
                    src = h[0:n, t.p, :] if k == 0 else y[0:n, t.p, :]
                    ins = dve.scalar_tensor_tensor(y[0:n, t.p, :], r[0:n, t.p, k, :], gt[0:n, bass.ds(t.t, 1), k],
                                                   src, ALU.mult, ALU.add)
                    if k < TOPK - 1:
                        dve.drain()
                ins.then_inc(y_ready, 1)

            all_steps(dve, NT, step, lambda t: step(t, SAMPLE))


def decoder_step(nc, i, o):
    y_prompt, y_sample, k_prompt, v_prompt, gla_prompt, mk, mv, k_sample, v_sample, gla_sample = o

    def scratch(name, shape, dt=F32):
        return nc.dram_tensor(name, shape, dt, kind="Internal").ap()

    Z = scratch("z_rows", (NT, P, ZW))
    U = [scratch(f"u_rows{g}", (SEQ, UW)) for g in range(len(GROUPS))]
    OB, OAS = scratch("b_rows", (NT, P, BVW)), scratch("a_rows_sample", (SAMPLE, AW))
    H, XN, RT = scratch("h_rows", (NT, P, D)), scratch("x_rows", (NT, P, D)), scratch("routes", (NT, P, 8))
    TBL, SL = scratch("slot_tokens", (P, NTL), I32), scratch("token_slots", (P, NT * TOPK), I32)
    TE, YS = scratch("tile_experts", (3, NTL), I32), scratch("slot_rows", (NTL, P, D))

    for part, shifts in ((0, ((i["cache_swa_k"], k_sample), (i["cache_swa_v"], v_sample))), (1, ())):
        project(nc, part, i["x_prompt"], i["x_sample"], i["norm1_g"], i["w_in"], i["a_q_norm_g"], i["a_k_norm_g"],
                i["gla_w_alpha"], i["gla_b_alpha"], Z, shifts)
    dilated(nc, Z, U, (k_prompt, v_prompt), (k_sample, v_sample))
    gla(nc, Z, i["gla_out_norm_g"], i["state_gla"], OB, gla_prompt, gla_sample)
    dilated_sample(nc, Z, i["cache_swa_k"], i["cache_swa_v"], OAS)
    memory_kv(nc, i["mem_prompt"], i["mem_norm_g"], i["mem_w_k"], i["mem_w_v"], i["mem_k_norm_g"], mk, mv)
    mix_attend_route(nc, i["x_prompt"], i["x_sample"], U, OB, OAS, i["w_out"], i["norm2_g"], i["mem_w_q"],
                     i["mem_q_norm_g"], i["mem_w_o"], i["norm3_g"], i["router_w"], i["router_b"], mk, mv,
                     i["cache_mem_k"], i["cache_mem_v"], H, XN, RT)
    slots(nc, RT, TBL, SL, TE)
    experts(nc, XN, i["norm3_g"], TBL, TE, i["exp_w1"], i["exp_b1"], i["exp_w2"], i["exp_b2"], YS)
    combine_experts(nc, H, RT, SL, YS, y_prompt, y_sample)


_OUTS = [(1, SEQ, D), (DEC_B, DEC_T, D), (1, 1, WBUF, AH, AD), (1, 1, WBUF, AH, AD), (1, 1, BH, BK, BV),
         (1, 1, NMEM, MH, MD), (1, 1, NMEM, MH, MD), (1, DEC_B, WBUF, AH, AD), (1, DEC_B, WBUF, AH, AD),
         (1, DEC_B, BH, BK, BV)]


def kernel(**inputs):
    import numpy as np
    import concourse.bacc as bacc
    from concourse.bass_utils import run_bass_kernel_spmd as run

    nc = bacc.Bacc("TRN2", target_bir_lowering=False, num_devices=1)
    arrays, ins = {}, {}
    for name, a in inputs.items():
        arrays[f"in_{name}"] = np.ascontiguousarray(a)
        ins[name] = nc.dram_tensor(f"in_{name}", a.shape, F32, kind="ExternalInput").ap()
    outs = [nc.dram_tensor(f"out_{k}", s, F32, kind="ExternalOutput").ap() for k, s in enumerate(_OUTS)]
    decoder_step(nc, ins, outs)
    r = run(nc, [arrays], core_ids=[0])
    return tuple(r.results[0][f"out_{k}"] for k in range(len(_OUTS)))
```
